# Optimizing a Trainium2 kernel written in Bass

```python
import jax, jax.numpy as jnp
from jax import lax
import numpy as np
import math

D_MODEL = 2048
BATCH = 1
SEQ = 256
DEPTH = 1

CTX_LEN = 256
GRID_W = 64
HEAD_DIM = 128
ATT_W = (3 * D_MODEL) // 4
N_Q_HEADS = ATT_W // HEAD_DIM
N_KV_HEADS = 4
Q_PER_KV = N_Q_HEADS // N_KV_HEADS
KV_W = N_KV_HEADS * HEAD_DIM
FNET_W = D_MODEL // 4
N_FNET_GROUPS = 4
FNET_GROUP = FNET_W // N_FNET_GROUPS
ROPE_THETA = 10000.0
ROPE_AXIS_DIM = HEAD_DIM // 2
ROPE_NFREQ = ROPE_AXIS_DIM // 2
Q_BLOCK = 128
EPS = 1e-6

OFF_Q = 0
OFF_K = OFF_Q + ATT_W
OFF_V = OFF_K + KV_W
OFF_ZA = OFF_V + KV_W
OFF_UB = OFF_ZA + ATT_W
OFF_ZB = OFF_UB + FNET_W
OFF_GA = OFF_ZB + FNET_W
OFF_GB = OFF_GA + D_MODEL
IN_W = OFF_GB + D_MODEL
R_ZA = 0
R_UB = OFF_UB - OFF_ZA
R_ZB = OFF_ZB - OFF_ZA
R_GA = OFF_GA - OFF_ZA
R_GB = OFF_GB - OFF_ZA


def _rmsnorm(x, g):
    xf = x.astype(jnp.float32)
    y = xf * lax.rsqrt(jnp.mean(xf * xf, axis=-1, keepdims=True) + EPS)
    return (y * g.astype(jnp.float32)).astype(x.dtype)

def _modulate(h, shift, scale):
    return h * (1 + scale) + shift

def _heads(p, lo, n_heads):
    b, n, _ = p.shape
    return p[..., lo:lo + n_heads * HEAD_DIM].reshape(b, n, n_heads, HEAD_DIM)

def _axial_rope_tables(n_tokens):
    rows = n_tokens // GRID_W
    row_pos = jnp.repeat(jnp.arange(rows, dtype=jnp.float32), GRID_W)
    col_pos = jnp.tile(jnp.arange(GRID_W, dtype=jnp.float32), rows)
    inv = ROPE_THETA ** (-jnp.arange(ROPE_NFREQ, dtype=jnp.float32) / ROPE_NFREQ)
    ang = jnp.stack([row_pos[:, None] * inv, col_pos[:, None] * inv], axis=1)
    return jnp.cos(ang), jnp.sin(ang)

def _rope(x, cos, sin):
    b, n, h, _ = x.shape
    xf = x.astype(jnp.float32).reshape(b, n, h, 2, 2, ROPE_NFREQ)
    x1, x2 = xf[..., 0, :], xf[..., 1, :]
    cc, ss = cos[None, :, None], sin[None, :, None]
    out = jnp.stack([x1 * cc - x2 * ss, x2 * cc + x1 * ss], axis=-2)
    return out.reshape(b, n, h, HEAD_DIM).astype(x.dtype)

def _attention(q, k, v):
    b, n = q.shape[:2]
    nblk = n // Q_BLOCK
    qb = q.reshape(b, nblk, Q_BLOCK, N_KV_HEADS, Q_PER_KV, HEAD_DIM).transpose(1, 0, 2, 3, 4, 5)

    def block(qi):
        s = jnp.einsum('bqhgd,bkhd->bhgqk', qi, k, preferred_element_type=jnp.float32)
        w = jax.nn.softmax(s, axis=-1).astype(v.dtype)
        return jnp.einsum('bhgqk,bkhd->bqhgd', w, v)

    o = lax.map(block, qb)
    return o.transpose(1, 0, 2, 3, 4, 5).reshape(b, n, ATT_W)

def _fourier_mix(u):
    b, n, _ = u.shape
    ug = u.astype(jnp.float32).reshape(b, n, N_FNET_GROUPS, FNET_GROUP)
    y = jnp.fft.fftn(ug, axes=(1, 3), norm="ortho").real
    return y.reshape(b, n, FNET_W).astype(u.dtype)

def _merge(p_rest, attn, w_pa, w_pb, w_o):
    z_a = p_rest[..., R_ZA:R_UB]
    u_b = p_rest[..., R_UB:R_ZB]
    z_b = p_rest[..., R_ZB:R_GA]
    g_a = jax.nn.sigmoid(p_rest[..., R_GA:R_GB])
    g_b = jax.nn.sigmoid(p_rest[..., R_GB:])
    y_a = (attn * jax.nn.silu(z_a)) @ w_pa
    y_b = (_fourier_mix(u_b) * jax.nn.silu(z_b)) @ w_pb
    return (g_a * y_a + g_b * y_b) @ w_o

def first_inputs(seed: int = 0) -> dict:
    key = jax.random.key(seed)
    ks = jax.random.split(key, 16)
    f32 = jnp.float32
    nrm = lambda k, shape, s: jax.random.normal(k, shape, f32) * s
    return {
        "x": nrm(ks[0], (BATCH, SEQ, D_MODEL), 1.0),
        "c": nrm(ks[1], (BATCH, D_MODEL), 1.0),
        "ctx": nrm(ks[2], (BATCH, CTX_LEN, D_MODEL), 1.0),
        "c_ctx": nrm(ks[3], (D_MODEL,), 1.0),
        "w_ada": nrm(ks[4], (DEPTH, D_MODEL, 3 * D_MODEL), D_MODEL ** -0.5),
        "b_ada": nrm(ks[5], (DEPTH, 3 * D_MODEL), 0.01),
        "norm_g": 1.0 + nrm(ks[6], (DEPTH, D_MODEL), 0.01),
        "w_in": nrm(ks[7], (DEPTH, D_MODEL, IN_W), D_MODEL ** -0.5),
        "q_norm_g": 1.0 + nrm(ks[8], (DEPTH, HEAD_DIM), 0.01),
        "k_norm_g": 1.0 + nrm(ks[9], (DEPTH, HEAD_DIM), 0.01),
        "w_proj_a": nrm(ks[10], (DEPTH, ATT_W, D_MODEL), ATT_W ** -0.5),
        "w_proj_b": nrm(ks[11], (DEPTH, FNET_W, D_MODEL), FNET_W ** -0.5),
        "w_out": nrm(ks[12], (DEPTH, D_MODEL, D_MODEL), D_MODEL ** -0.5),
        "final_g": 1.0 + nrm(ks[13], (D_MODEL,), 0.01),
    }

def first_block(x, c, ctx, c_ctx, w_ada, b_ada, norm_g, w_in, q_norm_g, k_norm_g,
              w_proj_a, w_proj_b, w_out, final_g):
    n_lat = x.shape[1]
    cos, sin = _axial_rope_tables(n_lat)
    q_scale = HEAD_DIM ** -0.5
    silu_c = jax.nn.silu(c)
    silu_cc = jax.nn.silu(c_ctx)
    xs, cs = x, ctx
    for l in range(DEPTH):
        last = l == DEPTH - 1
        w_l = w_in[l]
        shift, scale, gate = jnp.split(silu_c @ w_ada[l] + b_ada[l], 3, axis=-1)
        shift_c, scale_c, gate_c = jnp.split(silu_cc @ w_ada[l] + b_ada[l], 3, axis=-1)
        h = _modulate(_rmsnorm(xs, norm_g[l]), shift[:, None], scale[:, None])
        hc = _modulate(_rmsnorm(cs, norm_g[l]), shift_c, scale_c)

        pc_kv = hc @ w_l[:, OFF_K:OFF_ZA]
        kc = _rmsnorm(_heads(pc_kv, 0, N_KV_HEADS), k_norm_g[l])
        vc = _heads(pc_kv, KV_W, N_KV_HEADS)

        p = h @ w_l
        q = _rope(_rmsnorm(_heads(p, OFF_Q, N_Q_HEADS), q_norm_g[l]), cos, sin) * q_scale
        k = _rope(_rmsnorm(_heads(p, OFF_K, N_KV_HEADS), k_norm_g[l]), cos, sin)
        v = _heads(p, OFF_V, N_KV_HEADS)
        attn = _attention(q, jnp.concatenate([k, kc], axis=1), jnp.concatenate([v, vc], axis=1))
        y = _merge(p[..., OFF_ZA:], attn, w_proj_a[l], w_proj_b[l], w_out[l])
        new_xs = xs + gate[:, None] * y

        if not last:
            qc = _rmsnorm(_heads(hc @ w_l[:, OFF_Q:OFF_K], 0, N_Q_HEADS), q_norm_g[l]) * q_scale
            attn_c = _attention(qc, kc, vc)
            yc = _merge(hc @ w_l[:, OFF_ZA:], attn_c, w_proj_a[l], w_proj_b[l], w_out[l])
            cs = cs + gate_c * yc
        xs = new_xs
    return _rmsnorm(xs, final_g)


DEPTH_2 = 2

N_MIXERS = 2
N_SSD_LAYERS = (DEPTH_2 + 1) // 2
N_DSA_LAYERS = DEPTH_2 // 2
DN_ALPHA = (2.0 * DEPTH_2) ** 0.25
DN_BETA = (8.0 * DEPTH_2) ** -0.25
LN_EPS = 1e-5
RMS_EPS = 1e-6

SSD_EXPAND = 2
SSD_D_INNER = SSD_EXPAND * D_MODEL
SSD_HEAD_DIM = 64
SSD_N_HEADS = SSD_D_INNER // SSD_HEAD_DIM
SSD_N_GROUPS = 8
SSD_HEADS_PER_GROUP = SSD_N_HEADS // SSD_N_GROUPS
SSD_D_STATE = 128
SSD_D_CONV = 4
SSD_CHUNK = 256
SSD_CONV_DIM = SSD_D_INNER + 2 * SSD_N_GROUPS * SSD_D_STATE
SSD_IN_DIM = SSD_D_INNER + SSD_CONV_DIM + SSD_N_HEADS
SSD_NORM_GROUP = SSD_D_INNER // SSD_N_GROUPS

DSA_N_HEADS = 32
DSA_HEAD_DIM = 128
DSA_WIDTH = DSA_N_HEADS * DSA_HEAD_DIM
DSA_Q_RANK = 512
DSA_KV_RANK = 256
IDX_N_HEADS = 16
IDX_HEAD_DIM = 64
IDX_TOPK = 256
DSA_IN_DIM = DSA_Q_RANK + DSA_KV_RANK + IDX_HEAD_DIM + IDX_N_HEADS + DSA_WIDTH


def layer_norm(x, g, b):
    xf = x.astype(jnp.float32)
    mu = jnp.mean(xf, -1, keepdims=True)
    var = jnp.mean(jnp.square(xf - mu), -1, keepdims=True)
    return ((xf - mu) * lax.rsqrt(var + LN_EPS) * g + b).astype(x.dtype)

def rms_norm(x, g):
    xf = x.astype(jnp.float32)
    y = xf * lax.rsqrt(jnp.mean(xf * xf, -1, keepdims=True) + RMS_EPS) * g
    return y.astype(x.dtype)

def causal_depthwise_conv(u, w, b):
    k, c = w.shape
    out = lax.conv_general_dilated(u, w[:, None, :], window_strides=(1,), padding=[(k - 1, 0)],
                                   dimension_numbers=('NWC', 'WIO', 'NWC'), feature_group_count=c)
    return out + b

def segsum(a):
    cs = jnp.cumsum(a, -1)
    t = a.shape[-1]
    diff = cs[..., :, None] - cs[..., None, :]
    mask = jnp.tril(jnp.ones((t, t), dtype=bool))
    return jnp.where(mask, diff, -jnp.inf)

def ssd_chunked(xs, dt, a, bm, cm, chunk):
    b, L, g, r, p = xs.shape
    n = bm.shape[-1]
    c = L // chunk
    xdt = (xs * dt[..., None]).reshape(b, c, chunk, g, r, p)
    bc = bm.reshape(b, c, chunk, g, n)
    cc = cm.reshape(b, c, chunk, g, n)
    adt = (dt * a).reshape(b, c, chunk, g, r).transpose(0, 3, 4, 1, 2)
    a_cs = jnp.cumsum(adt, -1)
    decay = jnp.exp(segsum(adt))
    cb = jnp.einsum('bclgn,bcsgn->bgcls', cc, bc)
    y_diag = jnp.einsum('bgcls,bgrcls,bcsgrp->bclgrp', cb, decay, xdt)
    decay_states = jnp.exp(a_cs[..., -1:] - a_cs)
    states = jnp.einsum('bclgn,bgrcl,bclgrp->bcgrpn', bc, decay_states, xdt)
    states = jnp.concatenate([jnp.zeros_like(states[:, :1]), states], 1)
    chunk_a = jnp.pad(a_cs[..., -1], ((0, 0), (0, 0), (0, 0), (1, 0)))
    chunk_decay = jnp.exp(segsum(chunk_a))
    new_states = jnp.einsum('bgrzc,bcgrpn->bzgrpn', chunk_decay, states)
    prev_states = new_states[:, :-1]
    y_off = jnp.einsum('bclgn,bcgrpn,bgrcl->bclgrp', cc, prev_states, jnp.exp(a_cs))
    return (y_diag + y_off).reshape(b, L, g, r, p)

def ssd_mixer(x, w_in, conv_w, conv_b, dt_bias, a_log, d_skip, norm_g, w_out):
    b, L, _ = x.shape
    proj = x @ w_in
    z, xbc, dt = jnp.split(proj, [SSD_D_INNER, SSD_D_INNER + SSD_CONV_DIM], -1)
    xbc = jax.nn.silu(causal_depthwise_conv(xbc, conv_w, conv_b))
    xs, bm, cm = jnp.split(xbc, [SSD_D_INNER, SSD_D_INNER + SSD_N_GROUPS * SSD_D_STATE], -1)
    g, r, p = SSD_N_GROUPS, SSD_HEADS_PER_GROUP, SSD_HEAD_DIM
    xs = xs.reshape(b, L, g, r, p)
    bm = bm.reshape(b, L, g, SSD_D_STATE)
    cm = cm.reshape(b, L, g, SSD_D_STATE)
    dt = jax.nn.softplus(dt.astype(jnp.float32) + dt_bias).reshape(b, L, g, r)
    a = -jnp.exp(a_log.astype(jnp.float32)).reshape(g, r)
    chunk = math.gcd(SSD_CHUNK, L)
    y = ssd_chunked(xs, dt, a, bm, cm, chunk)
    y = y + d_skip.reshape(g, r)[..., None] * xs
    y = y.reshape(b, L, SSD_D_INNER).astype(jnp.float32)
    yg = (y * jax.nn.silu(z.astype(jnp.float32))).reshape(b, L, g, SSD_NORM_GROUP)
    yg = yg * lax.rsqrt(jnp.mean(yg * yg, -1, keepdims=True) + RMS_EPS)
    yg = yg.reshape(b, L, SSD_D_INNER) * norm_g
    return yg.astype(x.dtype) @ w_out

def dsa_mixer(x, w_in, q_norm_g, kv_norm_g, w_uq, w_uk, w_uv, w_idx_q, w_out):
    b, L, _ = x.shape
    proj = x @ w_in
    s1 = DSA_Q_RANK
    s2 = s1 + DSA_KV_RANK
    s3 = s2 + IDX_HEAD_DIM
    s4 = s3 + IDX_N_HEADS
    c_q, c_kv, k_idx, w_idx, gate = jnp.split(proj, [s1, s2, s3, s4], -1)
    c_q = rms_norm(c_q, q_norm_g)
    c_kv = rms_norm(c_kv, kv_norm_g)
    q = (c_q @ w_uq).reshape(b, L, DSA_N_HEADS, DSA_HEAD_DIM)
    q_lat = jnp.einsum('bthd,hcd->bthc', q, w_uk)
    q_idx = (c_q @ w_idx_q).reshape(b, L, IDX_N_HEADS, IDX_HEAD_DIM)
    w_idx = w_idx.astype(jnp.float32) * (IDX_N_HEADS ** -0.5)
    k_idx_f = k_idx.astype(jnp.float32)
    k_top = min(IDX_TOPK, L // 4)
    nblk = L // Q_BLOCK
    key_pos = jnp.arange(L)
    idx_scale = IDX_HEAD_DIM ** -0.5
    attn_scale = DSA_HEAD_DIM ** -0.5

    def to_blocks(t):
        return t.reshape((b, nblk, Q_BLOCK) + t.shape[2:]).swapaxes(0, 1)

    def block(args):
        qi, wi, ql, tpos = args
        s = jnp.einsum('bthd,bsd->bths', qi.astype(jnp.float32), k_idx_f)
        score = jnp.einsum('bths,bth->bts', jax.nn.relu(s), wi) * idx_scale
        causal = key_pos[None, :] <= tpos[:, None]
        score = jnp.where(causal[None], score, -jnp.inf)
        _, sel = lax.top_k(score, k_top)
        kv_sel = jax.vmap(lambda c, i: c[i])(c_kv, sel)
        logits = jnp.einsum('bthc,btkc->bthk', ql, kv_sel).astype(jnp.float32) * attn_scale
        valid = sel <= tpos[None, :, None]
        logits = jnp.where(valid[:, :, None, :], logits, -jnp.inf)
        pr = jax.nn.softmax(logits, -1).astype(kv_sel.dtype)
        return jnp.einsum('bthk,btkc->bthc', pr, kv_sel)

    pos = jnp.arange(L).reshape(nblk, Q_BLOCK)
    o_lat = lax.map(block, (to_blocks(q_idx), to_blocks(w_idx), to_blocks(q_lat), pos))
    o_lat = o_lat.swapaxes(0, 1).reshape(b, L, DSA_N_HEADS, DSA_KV_RANK)
    o = jnp.einsum('bthc,hcv->bthv', o_lat, w_uv).reshape(b, L, DSA_WIDTH)
    return (o * jax.nn.silu(gate)) @ w_out

def second_inputs(seed: int = 0) -> dict:
    key = jax.random.key(seed)
    ks = jax.random.split(key, 24)
    f32 = jnp.float32

    def nrm(k, shape, fan_in, scale=1.0):
        return jax.random.normal(k, shape, f32) * (scale * fan_in ** -0.5)

    x = jax.random.normal(ks[0], (BATCH, SEQ, D_MODEL), f32)
    ns, nd = N_SSD_LAYERS, N_DSA_LAYERS
    ssd_w_in = nrm(ks[1], (ns, D_MODEL, SSD_IN_DIM), D_MODEL)
    ssd_conv_w = nrm(ks[2], (ns, SSD_D_CONV, SSD_CONV_DIM), SSD_D_CONV)
    ssd_conv_b = 0.02 * jax.random.normal(ks[3], (ns, SSD_CONV_DIM), f32)
    u = jax.random.uniform(ks[4], (ns, SSD_N_HEADS), f32)
    dt0 = jnp.exp(u * (math.log(0.1) - math.log(0.001)) + math.log(0.001))
    ssd_dt_bias = dt0 + jnp.log(-jnp.expm1(-dt0))
    ssd_a_log = jnp.log(jax.random.uniform(ks[5], (ns, SSD_N_HEADS), f32, 1.0, 16.0))
    ssd_d_skip = 1.0 + 0.02 * jax.random.normal(ks[6], (ns, SSD_N_HEADS), f32)
    ssd_norm_g = 1.0 + 0.02 * jax.random.normal(ks[7], (ns, SSD_D_INNER), f32)
    ssd_w_out = nrm(ks[8], (ns, SSD_D_INNER, D_MODEL), SSD_D_INNER, DN_BETA)
    dsa_w_in = nrm(ks[9], (nd, D_MODEL, DSA_IN_DIM), D_MODEL)
    dsa_q_norm_g = 1.0 + 0.02 * jax.random.normal(ks[10], (nd, DSA_Q_RANK), f32)
    dsa_kv_norm_g = 1.0 + 0.02 * jax.random.normal(ks[11], (nd, DSA_KV_RANK), f32)
    dsa_w_uq = nrm(ks[12], (nd, DSA_Q_RANK, DSA_WIDTH), DSA_Q_RANK)
    dsa_w_uk = nrm(ks[13], (nd, DSA_N_HEADS, DSA_KV_RANK, DSA_HEAD_DIM), DSA_KV_RANK)
    dsa_w_uv = nrm(ks[14], (nd, DSA_N_HEADS, DSA_KV_RANK, DSA_HEAD_DIM), DSA_KV_RANK)
    dsa_w_idx_q = nrm(ks[15], (nd, DSA_Q_RANK, IDX_N_HEADS * IDX_HEAD_DIM), DSA_Q_RANK)
    dsa_w_out = nrm(ks[16], (nd, DSA_WIDTH, D_MODEL), DSA_WIDTH, DN_BETA)
    ln_g = 1.0 + 0.02 * jax.random.normal(ks[17], (DEPTH_2, D_MODEL), f32)
    ln_b = 0.02 * jax.random.normal(ks[18], (DEPTH_2, D_MODEL), f32)
    return {'x': x, 'ssd_w_in': ssd_w_in, 'ssd_conv_w': ssd_conv_w, 'ssd_conv_b': ssd_conv_b,
            'ssd_dt_bias': ssd_dt_bias, 'ssd_a_log': ssd_a_log, 'ssd_d_skip': ssd_d_skip,
            'ssd_norm_g': ssd_norm_g, 'ssd_w_out': ssd_w_out, 'dsa_w_in': dsa_w_in,
            'dsa_q_norm_g': dsa_q_norm_g, 'dsa_kv_norm_g': dsa_kv_norm_g, 'dsa_w_uq': dsa_w_uq,
            'dsa_w_uk': dsa_w_uk, 'dsa_w_uv': dsa_w_uv, 'dsa_w_idx_q': dsa_w_idx_q,
            'dsa_w_out': dsa_w_out, 'ln_g': ln_g, 'ln_b': ln_b}

def second_block(x, ssd_w_in, ssd_conv_w, ssd_conv_b, ssd_dt_bias, ssd_a_log, ssd_d_skip,
              ssd_norm_g, ssd_w_out, dsa_w_in, dsa_q_norm_g, dsa_kv_norm_g, dsa_w_uq,
              dsa_w_uk, dsa_w_uv, dsa_w_idx_q, dsa_w_out, ln_g, ln_b):
    for i in range(DEPTH_2):
        j = i // N_MIXERS
        if i % N_MIXERS == 0:
            h = ssd_mixer(x, ssd_w_in[j], ssd_conv_w[j], ssd_conv_b[j], ssd_dt_bias[j],
                          ssd_a_log[j], ssd_d_skip[j], ssd_norm_g[j], ssd_w_out[j])
        else:
            h = dsa_mixer(x, dsa_w_in[j], dsa_q_norm_g[j], dsa_kv_norm_g[j], dsa_w_uq[j],
                          dsa_w_uk[j], dsa_w_uv[j], dsa_w_idx_q[j], dsa_w_out[j])
        x = layer_norm(DN_ALPHA * x + h, ln_g[i], ln_b[i])
    return x


def setup_inputs(seed=0):
    out = dict(first_inputs(seed))
    for name, value in second_inputs(seed + 1).items():
        if name != "x":
            out[name + "_2"] = value
    return out


def reference(
    x, c, ctx, c_ctx, w_ada, b_ada, norm_g, w_in, q_norm_g, k_norm_g, w_proj_a, w_proj_b, w_out,
    final_g, ssd_w_in_2, ssd_conv_w_2, ssd_conv_b_2, ssd_dt_bias_2, ssd_a_log_2, ssd_d_skip_2,
    ssd_norm_g_2, ssd_w_out_2, dsa_w_in_2, dsa_q_norm_g_2, dsa_kv_norm_g_2, dsa_w_uq_2,
    dsa_w_uk_2, dsa_w_uv_2, dsa_w_idx_q_2, dsa_w_out_2, ln_g_2, ln_b_2,
):
    x = first_block(
        x, c, ctx, c_ctx, w_ada, b_ada, norm_g, w_in, q_norm_g, k_norm_g, w_proj_a, w_proj_b,
        w_out, final_g,
    )
    return second_block(
        x, ssd_w_in_2, ssd_conv_w_2, ssd_conv_b_2, ssd_dt_bias_2, ssd_a_log_2, ssd_d_skip_2,
        ssd_norm_g_2, ssd_w_out_2, dsa_w_in_2, dsa_q_norm_g_2, dsa_kv_norm_g_2, dsa_w_uq_2,
        dsa_w_uk_2, dsa_w_uv_2, dsa_w_idx_q_2, dsa_w_out_2, ln_g_2, ln_b_2,
    )


_drawn_inputs = setup_inputs


def setup_inputs(seed=0):
    import zlib

    import numpy as np

    out = dict(_drawn_inputs(seed))
    spreads = {}
    factors = {'ctx': 3.193,
     'b_ada': 7.295,
     'norm_g': 8.0,
     'q_norm_g': 8.0,
     'k_norm_g': 8.0,
     'final_g': 4.876,
     'ssd_conv_b_2': 5.303,
     'ssd_d_skip_2': 25.742,
     'ssd_norm_g_2': 7.802,
     'dsa_q_norm_g_2': 8.0,
     'dsa_kv_norm_g_2': 8.0}
    for name, (base, spread) in spreads.items():
        noise = np.random.default_rng([zlib.crc32(name.encode()), seed]).standard_normal(out[name].shape)
        drawn = base * np.exp(spread * noise) if base else spread * noise
        out[name] = __import__('jax').numpy.asarray(drawn.astype(out[name].dtype))
    for name, factor in factors.items():
        out[name] = (out[name] * factor).astype(out[name].dtype)
    return out
```

```python
from contextlib import ExitStack

import numpy as np

import concourse.bass as bass
from concourse import mybir

F32 = mybir.dt.float32
F32R = mybir.dt.float32r
ALU = mybir.AluOpType
ACT = mybir.ActivationFunctionType
AX_X = mybir.AxisListType.X
ds = bass.ds

P = 128
L = 256
TT = L // P
D = 2048
KD = D // P
CB = 512
EPS = 1e-6
LN_EPS = 1e-5
ROPE_STEPS = 68

HQ, HKV, DH = 12, 4, 128
ATT_SCALE = DH ** -0.5
COL_Q, COL_K, COL_V, COL_ZA, COL_UB, COL_ZB, COL_GA, COL_GB = 0, 1536, 2048, 2560, 4096, 4608, 5120, 7168

G, R, HD, NS = 8, 8, 64, 128
SSD_IN = 10304
ALPHA = 4.0 ** 0.25

HL = 32
TOPK = 64
NEG = -1.0e30
UNSEEN = -3.0e38
TAKEN = -3.4e38

T_ID = 0
T_TRI = T_ID + 128
T_NEG = T_TRI + 384
T_UNSEEN = T_NEG + 128
T_SEL = T_UNSEEN + 128
T_SELX = T_SEL + 2
T_ROPE = T_SELX + 128
T_DFT = T_ROPE + 512
T_DFTC = T_DFT + 1024
T_W = T_DFTC + 256
T_TX = T_ROPE

V_BADA = 0
V_NORM = 48
V_SSDG = 64
V_QN = 96
V_KVN = 100
V_CB = 102
V_CW = 150
V_C = 342
V_W = 374

RAW = 4
SPLIT = 4

HI2 = 4096
LO = 8192
LO2 = 12288
SPARE = 14336


def make_tables():
    t = np.zeros((P, T_W), np.float32)
    i = np.arange(P)
    t[:, T_ID:T_ID + 128] = np.eye(P)
    tri = (i[:, None] <= i[None, :]).astype(np.float32)
    t[:, T_TRI:T_TRI + 384] = np.concatenate([tri, np.ones((P, P)), tri], 1)
    t[:, T_NEG:T_NEG + 128] = np.where(i[None, :] > i[:, None], NEG, 0.0)
    t[:, T_UNSEEN:T_UNSEEN + 128] = np.where(i[None, :] > i[:, None], UNSEEN, 0.0)
    for r in range(4):
        t[r, T_SEL + r % 2] = 1.0
    t[0, T_SELX:T_SELX + 128] = 1.0
    t[2, T_SELX:T_SELX + 128] = 1.0
    n = np.arange(L)
    inv = 10000.0 ** (-np.arange(32, dtype=np.float64) / 32)
    for a, pos in enumerate((n // 64, n % 64)):
        ang = pos[:, None] * inv[None, :]
        for tt in range(TT):
            c, s = np.cos(ang[tt * P:(tt + 1) * P]), np.sin(ang[tt * P:(tt + 1) * P])
            o = T_ROPE + tt * 128 + a * 64
            t[:, o:o + 32] = c
            t[:, o + 32:o + 64] = c
            o += 256
            t[:, o:o + 32] = -s
            t[:, o + 32:o + 64] = s
    th = 2 * np.pi * ((n[:, None] * n[None, :]) % L) / L
    for k in range(TT):
        o = T_DFT + k * 512
        t[:, o:o + 256] = np.cos(th[k * P:(k + 1) * P])
        t[:, o + 256:o + 512] = np.sin(th[k * P:(k + 1) * P])
    th = 2 * np.pi * ((i[:, None] * i[None, :]) % P) / P
    ortho = (L * P) ** -0.5
    t[:, T_DFTC:T_DFTC + 128] = np.cos(th) * ortho
    t[:, T_DFTC + 128:T_DFTC + 256] = -np.sin(th) * ortho
    return t


def tile_list():
    tiles = []

    def blocks(seg, n, per, dmas=1, width=CB):
        for b in range(n):
            for j in range(per):
                tiles.append((seg, b, j, dmas, width))

    blocks("ada", 8, 4)
    blocks("in", 10, 4)
    blocks("gate_a", 4, 4)
    blocks("gate_b", 4, 4)
    blocks("proj", 4, 4)
    blocks("ada_gate", 4, 4)
    blocks("out", 4, 4)
    blocks("ssd_x", 8, 4)
    blocks("ssd_bc", 4, 4)
    blocks("ssd_z", 8, 4)
    blocks("ssd_out", 4, 8)
    blocks("lat_q", 1, 4)
    blocks("lat_kv", 1, 4, 1, 336)
    blocks("idx_q", 2, 1)
    blocks("lat_gate", 8, 4)
    for b in range(8):
        tiles.append(("head_q", b, 0, 1, CB))
        tiles.append(("head_kv", b, 0, 4, CB))
    blocks("lat_out", 4, 8)
    return tiles


def build(nc, a, out, acs_dram):
    TILES = tile_list()
    NU = 2 * len(TILES)
    FIRST = {}
    for n, t in enumerate(TILES):
        FIRST.setdefault(t[0], n)

    def landed(tile):
        return 16 * sum(TILES[t][3] for t in range(tile % RAW, tile + 1, RAW))

    def linear(f, n, step, i):
        if isinstance(i, int):
            return f(n + step * i)
        return f(n) + i * (f(n + step) - f(n))

    def width(unit):
        return TILES[unit // 2][4]

    BLOCKS = []
    for seg, _, _, _, _ in TILES:
        if seg not in ("head_q", "head_kv") and all(seg != s for s, _ in BLOCKS):
            nb = 1 + max(t[1] for t in TILES if t[0] == seg)
            for b in range(nb):
                scalar = seg in ("gate_a", "gate_b", "ssd_z", "lat_q", "lat_kv", "idx_q", "lat_gate") or (
                    seg == "in" and b in (1, 5, 6, 7, 8, 9))
                BLOCKS.append((seg, "act" if scalar else "dve"))
    BI = {}
    for n, (seg, _) in enumerate(BLOCKS):
        BI.setdefault(seg, n)

    def freed_count(engine, n):
        return sum(1 for _, who in BLOCKS[:n + 1] if who == engine)

    def freed(seg, b=0):
        n = BI[seg]
        if isinstance(b, int):
            return freed_count(BLOCKS[n + b][1], n + b)
        return freed_count(BLOCKS[n][1], n) + b

    def ready(seg, b=0):
        per = 2 * (1 + max(t[2] for t in TILES if t[0] == seg))
        return 2 * FIRST[seg] + per + per * b

    with ExitStack() as ctx:
        def sb(name, shape, dt=F32):
            return ctx.enter_context(nc.sbuf_tensor(name, shape, dt))

        def sem(name):
            return ctx.enter_context(nc.semaphore(name))

        base = (nc.sbuf_base + 31) // 32 * 32
        at = base
        raw = nc.alloc_sbuf_tensor_at("raw", [P, RAW, 4, CB], F32, offset=at)
        at += RAW * 4 * CB * 4
        w_hi = nc.alloc_sbuf_tensor_at("w_hi", [P, SPLIT, 2, CB], F32R, offset=at)
        at += SPLIT * 2 * CB * 4
        w_lo = nc.alloc_sbuf_tensor_at("w_lo", [P, SPLIT, 2, CB], F32R, offset=at)
        at += SPLIT * 2 * CB * 4
        act = nc.alloc_sbuf_tensor_at("act", [P, 2, KD, L], F32R, offset=at)
        actf = nc.alloc_sbuf_tensor_at("actf", [P, 2 * KD * L], F32, offset=at)
        at += 2 * KD * L * 4
        gated = nc.alloc_sbuf_tensor_at("gated", [P, 2, 32, L], F32R, offset=at)
        gatedf = nc.alloc_sbuf_tensor_at("gatedf", [P, 2 * 32 * L], F32, offset=at)
        at += 2 * 32 * L * 4
        x = nc.alloc_sbuf_tensor_at("x", [P, TT, D], F32, offset=at)
        at += TT * D * 4
        lat = nc.alloc_sbuf_tensor_at("lat", [P, 2, 6, L], F32R, offset=at)
        side = nc.alloc_sbuf_tensor_at("side", [P, 4096], F32, offset=at)
        at += 4096 * 4
        tables = nc.alloc_sbuf_tensor_at("tables", [P, T_W], F32, offset=at)
        at += (T_W * 4 + 31) // 32 * 32
        vec = nc.alloc_sbuf_tensor_at("vec", [P, V_W], F32, offset=at)
        at += (V_W * 4 + 31) // 32 * 32
        t0 = nc.alloc_sbuf_tensor_at("t0", [P, 512], F32, offset=at)
        at += 512 * 4
        t1 = nc.alloc_sbuf_tensor_at("t1", [P, 256], F32, offset=at)
        at += 256 * 4
        mod = nc.alloc_sbuf_tensor_at("mod", [P, 4, KD], F32, offset=at)
        at += 64 * 4
        sm = nc.alloc_sbuf_tensor_at("sm", [P, 96], F32, offset=at)
        at += 96 * 4
        arena = ctx.enter_context(nc.sbuf_tensor("arena", [P, (at - nc.sbuf_base) // 4], F32))
        ident = tables[:, T_ID:T_ID + 128]
        tx = tables[:, T_TX:T_TX + 1792]

        ps = ctx.enter_context(nc.psum_tensor("ps", [P, 8, 512], F32))

        raw_landed = [sem(f"raw_landed{s}") for s in range(RAW)]
        hi_done = sem("hi_done")
        lo_done = sem("lo_done")
        units_used = sem("units_used")
        act_freed = sem("act_freed")
        dve_freed = sem("dve_freed")

        def tile_source(seg, b, j):
            def rows(w, k0, c0, n=CB, chunks=4):
                return w[k0:k0 + chunks * P, :].rearrange("(c p) n -> p c n", p=P)[:, :, ds(c0, n)]

            k0 = j * 512
            if seg == "ada":
                return [(0, 4, rows(a["w_ada"], k0, b * CB))]
            if seg == "ada_gate":
                return [(0, 4, rows(a["w_ada"], k0, b * CB + 4096))]
            if seg == "in":
                cols = [COL_K, COL_V, COL_Q, COL_Q + 512, COL_Q + 1024, COL_UB,
                        COL_ZA, COL_ZA + 512, COL_ZA + 1024, COL_ZB]
                return [(0, 4, rows(a["w_in"], k0, cols[b]))]
            if seg == "gate_a":
                return [(0, 4, rows(a["w_in"], k0, b * CB + COL_GA))]
            if seg == "gate_b":
                return [(0, 4, rows(a["w_in"], k0, b * CB + COL_GB))]
            if seg == "proj":
                if j < 3:
                    return [(0, 4, rows(a["w_proj_a"], k0, b * CB))]
                return [(0, 4, rows(a["w_proj_b"], 0, b * CB))]
            if seg == "out":
                return [(0, 4, rows(a["w_out"], k0, b * CB))]
            if seg == "ssd_x":
                return [(0, 4, rows(a["ssd_w_in_2"], k0, b * CB + 4096))]
            if seg == "ssd_bc":
                return [(0, 4, rows(a["ssd_w_in_2"], k0, b * CB + 8192))]
            if seg == "ssd_z":
                return [(0, 4, rows(a["ssd_w_in_2"], k0, b * CB))]
            if seg == "ssd_out":
                return [(0, 4, rows(a["ssd_w_out_2"], k0, b * CB))]
            if seg == "lat_q":
                return [(0, 4, rows(a["dsa_w_in_2"], k0, 0))]
            if seg == "lat_kv":
                return [(0, 4, rows(a["dsa_w_in_2"], k0, 512, 336))]
            if seg == "idx_q":
                return [(0, 4, rows(a["dsa_w_idx_q_2"], 0, b * CB))]
            if seg == "lat_gate":
                return [(0, 4, rows(a["dsa_w_in_2"], k0, b * CB + 848))]
            if seg == "head_q":
                return [(0, 4, rows(a["dsa_w_uq_2"], 0, b * CB))]
            if seg == "head_kv":
                got = []
                for n, w in enumerate((a["dsa_w_uk_2"], a["dsa_w_uv_2"])):
                    for c in range(2):
                        got.append((2 * n + c, 1, w[ds(b * 4, 4), c * P:(c + 1) * P, :].rearrange("h p d -> p h d")))
                return got
            return [(0, 4, rows(a["dsa_w_out_2"], k0, b * CB))]

        def each(engine, turns, body):
            body(0)
            if turns > 1:
                with engine.Fori(1, turns) as i:
                    body(i)

        def last_apart(engine, seg, turns, body):
            after = max(n for n, t in enumerate(TILES) if t[0] == seg) + 1
            if any(t[3] != 1 for t in TILES[after:after + 2]):
                each(engine, turns - 1, body)
                body(turns - 1)
            else:
                each(engine, turns, body)

        names = """small_loaded vec_turned vec_ready silu_c c_hi c_ready c_zero squares1 mean1 root1 rstd1 xn_ready
            mod_turned mod_ready mod_step h_turned h_affine h_hi h_lo sq_ready ss_ready root_ready
            rope_step q_staged v_staged k_turned kt_ready dft1 dft1_out dft2 mix_ready mix_hi mix_lo
            qt_turned qt_ready scores_ready max_step max_ready exp_ready sum_inv probs_ready
            probs_turned pt_ready o_ready o_gated o_hi o_lo proj_read proj_sum proj_hi proj_lo
            c2_silu c2_hi c2_ready c2_zero gate_turned gate_ready bias_loaded rows_loaded out_read
            out_step sq2 mean2 root2 rstd2 scaled2 normed2 x2_turned x2_hi x2_lo dt_mm dt_step
            dt_act acs_stored dt_turned dt_ready conv_step conv_done conv_silu r_loaded b_staged
            cb_ready xs_turned xs_ready cb_masked xdt_step diff_ready decay_ready m_ready y_mm
            y_step y_act y_ready y_turned y_hi y_lo ln_rows ln_stats ln_act ln_rstd ln_dve x3_turned
            x3_hi x3_lo lat_sq lat_mean lat_root lat_rstd lat_act lat_normed lat_turned lat_scaled
            lat_hi lat_lo idxk_ready idx_scores idx_relu idx_step idx_done hq_read hk_read hv_read
            hs_mm hs_masked hs_step hs_max hs_exp hs_inv hs_probs hs_turned hs_pt ho_mm ho_gated
            ho_hi ho_lo fin_rows fin_stats fin_act fin_rstd fin_dve stored half_read""".split()
        S = {n: sem(n) for n in names}

        block = ctx.enter_context(nc.Block())

        @block.sync
        def _(sp):
            def load(n, b, i=0, step=0):
                seg, _, j, _, w = TILES[n]
                if n >= RAW or not isinstance(i, int):
                    sp.wait_ge(lo_done, 2 * (n - RAW) + 2 + 2 * step * i)
                for c0, c, src in tile_source(seg, b, j):
                    sp.dma_start(raw[:, n % RAW, c0:c0 + c, :w], src).then_inc(raw_landed[n % RAW], 16)

            def segment(seg, per, nblocks):
                n0 = FIRST[seg]

                def two(i):
                    for k in range(2):
                        for j in range(per):
                            load(n0 + k * per + j, 2 * i + k, i, 2 * per)
                each(sp, nblocks // 2, two)

            segment("ada", 4, 8)
            for n in range(FIRST["in"], FIRST["gate_a"]):
                load(n, TILES[n][1])
            segment("gate_a", 4, 4)
            segment("gate_b", 4, 4)
            segment("proj", 4, 4)
            segment("ada_gate", 4, 4)
            segment("out", 4, 4)
            segment("ssd_x", 4, 8)
            segment("ssd_bc", 4, 4)
            segment("ssd_z", 4, 8)
            segment("ssd_out", 8, 4)
            for n in range(FIRST["lat_q"], FIRST["lat_gate"]):
                load(n, TILES[n][1])
            segment("lat_gate", 4, 8)

            def heads(i):
                for k in range(2):
                    for j in range(2):
                        load(FIRST["head_q"] + 2 * k + j, 2 * i + k, i, 4)
            each(sp, 4, heads)
            segment("lat_out", 8, 4)

        @block.scalar
        def _(e):
            def split(u, i=0, step=0):
                t, h = u // 2, u % 2
                w = width(u)
                if h == 0:
                    e.wait_ge(raw_landed[t % RAW], linear(landed, t, step // 2, i))
                if u >= SPLIT:
                    e.wait_ge(units_used, linear(lambda v: v - SPLIT + 1, u, step, i))
                e.activation(w_hi[:, u % SPLIT, :, :w], raw[:, t % RAW, 2 * h:2 * h + 2, :w],
                             ACT.Copy).then_inc(hi_done, 1)

            def splits(u0, n, i=0, step=0):
                for u in range(u0, u0 + n):
                    if u < NU:
                        split(u, i, step)

            def fixed():
                e.wait_ge(S["small_loaded"], 16 * 17)

            def segment(seg, per, nblocks, epilogue):
                u0 = 2 * FIRST[seg]

                def two(i):
                    for k in range(2):
                        splits(u0 + (k * per * 2) + 4, 2 * per, i, 4 * per)
                        epilogue(2 * i + k, k)
                last_apart(e, seg, nblocks // 2, two)

            def root(out_, in_, ready, value, done):
                e.wait_ge(ready, value)
                e.activation(out_, in_, ACT.Sqrt).then_inc(done, 1)

            vr = side
            n = 0
            def small(dst, src):
                e.dma_start(dst, src).then_inc(S["small_loaded"], 16)
            small(tables[:, :], a["tables"])
            row = lambda v: v.rearrange("(c p) -> c p", p=P)
            small(t0[0:48, 0:128], row(a["b_ada"]))
            small(t0[48:64, 0:128], row(a["norm_g"]))
            small(t0[64:96, 0:128], row(a["ssd_norm_g_2"]))
            small(t0[96:100, 0:128], row(a["dsa_q_norm_g_2"]))
            small(t0[100:102, 0:128], row(a["dsa_kv_norm_g_2"]))
            small(t0[0:48, 128:256], row(a["ssd_conv_b_2"]))
            small(t0[48:96, 128:256], row(a["ssd_conv_w_2"][0, :]))
            small(t0[0:48, 256:384], row(a["ssd_conv_w_2"][1, :]))
            small(t0[48:96, 256:384], row(a["ssd_conv_w_2"][2, :]))
            small(t0[0:48, 384:512], row(a["ssd_conv_w_2"][3, :]))
            small(t0[48:64, 384:512], row(a["c"]))
            small(t0[64:80, 384:512], row(a["c_ctx"]))
            small(t1[:, 0:128], a["q_norm_g"].partition_broadcast(P))
            small(t1[:, 128:256], a["k_norm_g"].partition_broadcast(P))
            small(x[:, :, :], a["x"].rearrange("(t p) d -> p t d", p=P))
            small(side[:, :].rearrange("p (t d) -> p t d", t=TT), a["ctx"].rearrange("(t p) d -> p t d", p=P))

            cols = gated[:, 1, 16:24, :].rearrange("p a b -> p (a b)").rearrange("p (k m) -> p k m", m=P)

            def c_columns(silu_sem, hi_sem):
                e.activation(sm[:, 0:32], vec[:, V_C:V_C + 32], ACT.Silu).then_inc(silu_sem, 1)
                e.wait_ge(silu_sem, 1)
                e.activation(cols[:, :, 0:2], sm[:, 0:32].rearrange("p (j k) -> p k j", j=2),
                             ACT.Copy).then_inc(hi_sem, 1)

            e.wait_ge(S["vec_ready"], 1)
            e.wait_ge(S["c_zero"], 1)
            c_columns(S["silu_c"], S["c_hi"])
            splits(0, 4)
            e.wait_ge(S["small_loaded"], 16 * 17)
            for n in range(4):
                src = x[:, n, :] if n < 2 else side[:, (n - 2) * D:(n - 1) * D]
                e.activation(gatedf[:, n * D:(n + 1) * D], src, ACT.Square,
                             accum_out=sm[:, 32 + n:33 + n]).then_inc(S["squares1"], 1)
            root(sm[:, 40:44], sm[:, 36:40], S["mean1"], 1, S["root1"])
            e.wait_ge(S["rstd1"], 1)
            e.wait_ge(S["squares1"], 4)
            for n in range(4):
                src = x[:, n, :] if n < 2 else side[:, (n - 2) * D:(n - 1) * D]
                dst = gatedf[:, n * D:(n + 1) * D] if n < 2 else src
                e.activation(dst, src, ACT.Copy, scale=sm[:, 44 + n:45 + n]).then_inc(S["xn_ready"], 1)

            segment("ada", 4, 8, lambda b, k: None)
            for n in range(8):
                r, q = (act, n) if n < 4 else (gated, n - 4)
                o = SPARE + (n % 2) * 1024
                e.wait_ge(S["h_affine"], 4 * n + 4)
                e.activation(r[:, 0, 4 * q:4 * q + 4, :], gatedf[:, o:o + 1024].rearrange("p (c t) -> p c t", c=4),
                             ACT.Copy).then_inc(S["h_hi"], 1)

            u0 = 2 * FIRST["in"]
            nrope = 0
            for b in range(10):
                splits(u0 + 8 * b + 4, 8)
                e.wait_ge(units_used, ready("in", b))
                if b in (0, 2, 3, 4):
                    for tt in range(4 if b == 0 else 2):
                        bank = tt if b == 0 else (0 if b % 2 == 0 else 2) + tt
                        if nrope >= 2:
                            e.wait_ge(S["ss_ready"], nrope - 1)
                        e.activation(side[:, (nrope % 2) * 512:(nrope % 2) * 512 + 512], ps[:, bank, :],
                                     ACT.Square).then_inc(S["sq_ready"], 1)
                        nrope += 1
                        root(sm[:, 52:56], sm[:, 48:52], S["ss_ready"], nrope, S["root_ready"])
                elif b == 1:
                    for tt in range(4):
                        e.activation(gatedf[:, LO2 + 2048 + tt * 512:LO2 + 2560 + tt * 512], ps[:, 4 + tt, :],
                                     ACT.Copy).then_inc(act_freed if tt == 3 else S["half_read"], 1)
                elif b == 5:
                    for tt in range(2):
                        e.activation(gatedf[:, HI2 + 3072 + tt * 512:HI2 + 3584 + tt * 512], ps[:, 2 + tt, :],
                                     ACT.Copy).then_inc(act_freed if tt == 1 else S["half_read"], 1)
                else:
                    for n in range(2):
                        bank = (0 if b % 2 == 0 else 2) + n
                        o = LO + (b - 6) * 1024 + n * 512
                        e.activation(gatedf[:, o:o + 512], ps[:, bank, :], ACT.Silu).then_inc(
                            act_freed if n == 1 else S["half_read"], 1)

            for kv in range(HKV):
                e.wait_ge(S["k_turned"], kv + 1)
                e.activation(side[:, kv * 512:(kv + 1) * 512], ps[:, 4 + kv, :], ACT.Copy).then_inc(S["kt_ready"], 1)
            for g in range(4):
                e.wait_ge(S["dft1"], g + 1)
                e.activation(side[:, 2048 + g * 512:2560 + g * 512], ps[:, 4 + g, :], ACT.Copy).then_inc(S["dft1_out"], 1)
            e.wait_ge(S["mix_ready"], 1)
            e.activation(gated[:, 0, 12:16, :], side[:, 2048:3072].rearrange("p (c t) -> p c t", c=4),
                         ACT.Copy).then_inc(S["mix_hi"], 1)

            probs = gatedf[:, LO2:LO2 + 1024]
            pt = gatedf[:, LO2 + 1024:LO2 + 2048]
            qt = side[:, 3328:4096]

            def kv_turn(kv):
                def exps(j):
                    e.wait_ge(S["max_ready"], 3 * kv + j + 1)
                    if j > 0:
                        e.wait_ge(S["probs_turned"], 3 * kv + j)
                    else:
                        e.wait_ge(S["probs_turned"], 3 * kv)
                    for tt in range(2):
                        e.activation(probs[:, tt * 512:(tt + 1) * 512], ps[:, 4 + 2 * (j % 2) + tt, :], ACT.Exp,
                                     bias=sm[:, 58 + tt:59 + tt], scale=ATT_SCALE,
                                     accum_out=sm[:, 60 + tt:61 + tt]).then_inc(S["exp_ready"], 1)

                def turn(j):
                    e.wait_ge(S["probs_turned"], 3 * kv + j + 1)
                    e.activation(pt.rearrange("p (b c) -> p b c", b=2), ps[:, 2:4, :], ACT.Copy).then_inc(S["pt_ready"], 1)

                def high(j):
                    e.wait_ge(S["o_gated"], 3 * kv + j + 1)
                    fixed()
                    e.activation(gated[:, 0, ds(3 * kv + j, 1), :],
                                 t0[:, (j % 2) * 256:(j % 2) * 256 + 256].unsqueeze(1), ACT.Copy).then_inc(S["o_hi"], 1)

                for j in range(3):
                    e.wait_ge(S["qt_turned"], 3 * kv + (2, 2, 3)[j])
                    e.activation(qt[:, j * 256:(j + 1) * 256], ps[:, j // 2, (j % 2) * 256:(j % 2) * 256 + 256],
                                 ACT.Copy).then_inc(S["qt_ready"], 1)
                exps(0)
                turn(0)
                exps(1)
                high(0)
                turn(1)
                exps(2)
                high(1)
                turn(2)
                high(2)
            each(e, HKV, kv_turn)

            for seg, o in (("gate_a", HI2), ("gate_b", LO2)):
                def sig(b, k, seg=seg, o=o):
                    e.wait_ge(units_used, ready(seg, b))
                    for n in range(2):
                        fixed()
                        e.activation(gatedf[:, ds(o + n * 512 + 1024 * b, 512)], ps[:, 2 * k + n, :],
                                     ACT.Sigmoid).then_inc(act_freed if n == 1 else S["half_read"], 1)
                segment(seg, 4, 4, sig)

            def proj(b, k):
                e.wait_ge(S["proj_sum"], b + 1)
                fixed()
                e.activation(act[:, 0, ds(4 * b, 4), :],
                             side[:, 1024:2048].rearrange("p (c t) -> p c t", c=4),
                             ACT.Copy).then_inc(S["proj_hi"], 1)
            segment("proj", 4, 4, proj)

            e.wait_ge(S["c2_zero"], 1)
            c_columns(S["c2_silu"], S["c2_hi"])
            segment("ada_gate", 4, 4, lambda b, k: None)
            segment("out", 4, 4, lambda b, k: None)

            e.wait_ge(S["out_step"], 8)
            for n in range(2):
                e.activation(gatedf[:, n * D:(n + 1) * D], x[:, n, :], ACT.Square,
                             accum_out=sm[:, 32 + n:33 + n]).then_inc(S["sq2"], 1)
            root(sm[:, 40:42], sm[:, 36:38], S["mean2"], 1, S["root2"])
            e.wait_ge(S["rstd2"], 1)
            for q in range(4):
                for n in range(2):
                    piece = x[:, n, q * 512:(q + 1) * 512]
                    e.activation(piece, piece, ACT.Copy, scale=sm[:, 44 + n:45 + n]).then_inc(S["scaled2"], 1)

            def high_x(turned, done):
                for q in range(4):
                    e.wait_ge(turned, q + 1)
                    b = 4 + 2 * (q % 2)
                    e.activation(act[:, 0, 4 * q:4 * q + 4, :], ps[:, b:b + 2, :].rearrange("p b (c t) -> p (b c) t", c=2),
                                 ACT.Copy).then_inc(done, 1)
            high_x(S["x2_turned"], S["x2_hi"])

            e.wait_ge(S["rows_loaded"], 16 * 5)
            e.wait_ge(S["dt_mm"], 1)
            e.activation(tx[0:64, 0:256], ps[0:64, 4, 0:256], ACT.Identity, bias=sm[0:64, 65:66]).then_inc(S["dt_act"], 1)
            e.activation(sm[0:64, 66:67], sm[0:64, 64:65], ACT.Exp).then_inc(S["dt_act"], 1)
            e.wait_ge(S["dt_step"], 1)
            e.activation(tx[0:64, 512:768], tx[0:64, 256:512], ACT.Exp, scale=-1.0).then_inc(S["dt_act"], 1)
            e.wait_ge(S["dt_step"], 2)
            e.activation(tx[0:64, 1024:1280], tx[0:64, 768:1024], ACT.Ln).then_inc(S["dt_act"], 1)

            def conv_silu(dst, nb):
                def go(b, k):
                    for n in range(2):
                        if n == 0:
                            e.wait_ge(S["conv_done"], b + nb + 1)
                        else:
                            e.wait_ge(dve_freed, freed("ssd_x") + nb + b)
                        fixed()
                        e.activation(dst[:, ds(b * 1024 + n * 512, 512)], tx[:, n * 512:(n + 1) * 512],
                                     ACT.Silu).then_inc(S["conv_silu"], 1)
                return go
            segment("ssd_x", 4, 8, conv_silu(gatedf, 0))
            segment("ssd_bc", 4, 4, conv_silu(side, 8))

            def z_silu(b, k):
                e.wait_ge(units_used, ready("ssd_z", b))
                for n in range(2):
                    fixed()
                    e.activation(gatedf[:, ds(b * 1024 + LO + n * 512, 512)], ps[:, 2 * k + n, :],
                                 ACT.Silu).then_inc(act_freed if n == 1 else S["half_read"], 1)
            segment("ssd_z", 4, 8, z_silu)

            ex = actf[:, 2048:5120]
            xtok = actf[:, 6400:7424]

            def scan_turn(g):
                e.wait_ge(S["y_mm"], g)
                e.wait_ge(S["xs_turned"], g + 1)
                e.activation(xtok.rearrange("p (b c) -> p b c", b=2), ps[:, 1:3, :], ACT.Copy).then_inc(S["xs_ready"], 1)
                for n in range(2):
                    e.wait_ge(S["diff_ready"], 2 * g + n + 1)
                    part = ex[:, n * 1536:(n + 1) * 1536]
                    e.activation(part, part, ACT.Exp).then_inc(S["decay_ready"], 1)
                e.wait_ge(S["y_step"], 5 * g + 2)
                for n in range(2):
                    if n == 1:
                        e.wait_ge(S["y_act"], 3 * g + 1)
                    e.activation(actf[:, 7424:7936], tx[:, n * 512:(n + 1) * 512], ACT.Square,
                                 accum_out=sm[:, 32 + n:33 + n]).then_inc(S["y_act"], 1)
                e.wait_ge(S["y_step"], 5 * g + 3)
                e.activation(sm[:, 40:42], sm[:, 36:38], ACT.Sqrt).then_inc(S["y_act"], 1)
                e.wait_ge(S["y_step"], 5 * g + 4)
                for n in range(2):
                    part = tx[:, n * 512:(n + 1) * 512]
                    e.activation(part, part, ACT.Copy, scale=sm[:, 44 + n:45 + n]).then_inc(S["y_ready"], 1)
                e.wait_ge(S["y_step"], 5 * g + 5)
                fixed()
                e.activation(gated[:, 0, ds(4 * g, 4), :], tx[:, 0:1024].rearrange("p (c t) -> p c t", c=4),
                             ACT.Copy).then_inc(S["y_hi"], 1)
            each(e, G, scan_turn)

            segment("ssd_out", 8, 4, lambda b, k: None)

            def layer_norm(stats, act_sem, rstd):
                e.wait_ge(stats, 1)
                e.activation(sm[:, 40:42], sm[:, 38:40], ACT.Sqrt).then_inc(act_sem, 1)
                e.wait_ge(rstd, 1)
                for q in range(4):
                    for n in range(2):
                        piece = x[:, n, q * 512:(q + 1) * 512]
                        e.activation(piece, piece, ACT.Identity, scale=sm[:, 44 + n:45 + n],
                                     bias=sm[:, 46 + n:47 + n]).then_inc(act_sem, 1)
            layer_norm(S["ln_stats"], S["ln_act"], S["ln_rstd"])
            high_x(S["x3_turned"], S["x3_hi"])

            u0 = 2 * FIRST["lat_q"]
            splits(u0 + 4, 8)
            e.wait_ge(units_used, ready("lat_q"))
            for n in range(2):
                e.activation(tx[:, n * 512:(n + 1) * 512], ps[:, n, :], ACT.Copy).then_inc(act_freed if n == 1 else S["half_read"], 1)
            splits(u0 + 12, 8)
            e.wait_ge(units_used, ready("lat_kv"))
            for n in range(2):
                e.activation(tx[:, 1024 + n * 336:1360 + n * 336], ps[:, 2 + n, 0:336], ACT.Copy).then_inc(act_freed if n == 1 else S["half_read"], 1)
            e.wait_ge(act_freed, freed("lat_kv"))
            lats = [tx[:, 0:512], tx[:, 512:1024], tx[:, 1024:1280], tx[:, 1360:1616]]
            for n, v in enumerate(lats):
                if n:
                    e.wait_ge(S["lat_sq"], n)
                e.activation(t0[:, 0:512 if n < 2 else 256], v, ACT.Square, accum_out=sm[:, 32 + n:33 + n]).then_inc(S["lat_sq"], 1)
            root(sm[:, 40:44], sm[:, 36:40], S["lat_mean"], 2, S["lat_root"])
            e.wait_ge(S["lat_rstd"], 1)
            for n, v in enumerate(lats):
                e.activation(v, v, ACT.Copy, scale=sm[:, 44 + n:45 + n]).then_inc(S["lat_normed"], 1)
            kidx = gatedf[:, 2048:2304]
            e.wait_ge(S["lat_turned"], 1)
            e.activation(kidx, ps[:, 7, 0:256], ACT.Copy).then_inc(S["idxk_ready"], 1)
            e.wait_ge(S["lat_scaled"], 6)
            for c, n, v in ((0, 4, tx[:, 0:1024]), (4, 2, t0[:, 0:512])):
                e.activation(lat[:, 0, c:c + n, :], v.rearrange("p (c t) -> p c t", c=n), ACT.Copy).then_inc(S["lat_hi"], 1)
            for n in range(2):
                e.wait_ge(units_used, ready("idx_q", n))
                e.activation(gatedf[:, n * 1024:(n + 1) * 1024].rearrange("p (b c) -> p b c", b=2),
                             ps[:, 2 * n:2 * n + 2, :], ACT.Copy).then_inc(act_freed, 1)
            splits(2 * FIRST["lat_gate"], 4)
            for h in range(16):
                e.wait_ge(S["idx_scores"], h + 1)
                if h >= 2:
                    e.wait_ge(S["idx_step"], 2 * (h - 1))
                o = 2304 + (h % 2) * 384
                e.activation(gatedf[:, o:o + 384], ps[:, 4 + h % 4, 0:384], ACT.Relu, scale=1.0 / 32).then_inc(S["idx_relu"], 1)

            def gate_silu(b, k):
                e.wait_ge(units_used, ready("lat_gate", b))
                for n in range(2):
                    fixed()
                    e.activation(gatedf[:, ds(b * 1024 + LO + n * 512, 512)], ps[:, 2 * k + n, :],
                                 ACT.Silu).then_inc(act_freed if n == 1 else S["half_read"], 1)
            segment("lat_gate", 4, 8, gate_silu)

            def heads_turn(i):
                for k in range(2):
                    gi = 2 * i + k
                    ahead = 2 * FIRST["head_q"] + 4 * k + 4
                    splits(ahead, 2, i, 8)
                    w = actf[:, k * 3072:(k + 1) * 3072]
                    e.wait_ge(units_used, 2 * FIRST["head_q"] + 2 + 4 * gi)
                    e.activation(w[:, 0:1024].rearrange("p (b c) -> p b c", b=2), ps[:, 0:2, :], ACT.Copy).then_inc(S["hq_read"], 1)
                    splits(ahead + 2, 1, i, 8)
                    e.wait_ge(units_used, 2 * FIRST["head_q"] + 3 + 4 * gi)
                    e.activation(w[:, 1024:2048].rearrange("p (b c) -> p b c", b=2), ps[:, 2:4, :], ACT.Copy).then_inc(S["hk_read"], 1)
                    splits(ahead + 3, 1, i, 8)
                    e.wait_ge(units_used, 2 * FIRST["head_q"] + 4 + 4 * gi)
                    e.activation(w[:, 2048:3072].rearrange("p (b c) -> p b c", b=2), ps[:, 0:2, :], ACT.Copy).then_inc(S["hv_read"], 1)

                    def soft(h):
                        n = 4 * gi + h
                        p = actf[:, 6144 + (h % 2) * 384:6528 + (h % 2) * 384]
                        e.wait_ge(S["hs_max"], n + 1)
                        for tt, v in enumerate((p[:, 0:128], p[:, 128:384])):
                            e.activation(v, v, ACT.Exp, bias=sm[:, 58 + tt:59 + tt], scale=ATT_SCALE,
                                         accum_out=sm[:, 60 + tt:61 + tt]).then_inc(S["hs_exp"], 1)

                    def turn(h):
                        n = 4 * gi + h
                        e.wait_ge(S["hs_turned"], n + 1)
                        e.activation(actf[:, 6912 + (h % 2) * 384:7296 + (h % 2) * 384], ps[:, 6, 0:384],
                                     ACT.Copy).then_inc(S["hs_pt"], 1)

                    def high(h):
                        n = 4 * gi + h
                        e.wait_ge(S["ho_gated"], n + 1)
                        fixed()
                        o = 7680 + (h % 2) * 256
                        e.activation(gated[:, 0, ds(n, 1), :], actf[:, o:o + 256].unsqueeze(1),
                                     ACT.Copy).then_inc(S["ho_hi"], 1)
                    soft(0)
                    for h in range(4):
                        turn(h)
                        if h < 3:
                            soft(h + 1)
                        high(h)
            each(e, 3, heads_turn)
            heads_turn(3)

            splits(2 * FIRST["lat_out"] + 4, 60)
            layer_norm(S["fin_stats"], S["fin_act"], S["fin_rstd"])

        @block.vector
        def _(e):
            def split(u, i=0, step=0):
                t, h = u // 2, u % 2
                w = width(u)
                e.wait_ge(hi_done, linear(lambda v: v + 1, u, step, i))
                e.tensor_tensor(w_lo[:, u % SPLIT, :, :w], raw[:, t % RAW, 2 * h:2 * h + 2, :w],
                                w_hi[:, u % SPLIT, :, :w].bitcast(F32), ALU.subtract).then_inc(lo_done, 1)

            def splits(u0, n, i=0, step=0):
                for u in range(u0, u0 + n):
                    if u < NU:
                        split(u, i, step)

            def segment(seg, per, nblocks, epilogue):
                u0 = 2 * FIRST[seg]

                def two(i):
                    for k in range(2):
                        splits(u0 + (k * per * 2) + 4, 2 * per, i, 4 * per)
                        epilogue(2 * i + k, k)
                last_apart(e, seg, nblocks // 2, two)

            def mean_root_rstd(n, ss_sem, ss_value, size, mean, root, done, eps=EPS):
                e.wait_ge(ss_sem, ss_value)
                e.tensor_scalar(sm[:, 36:36 + n], sm[:, 32:32 + n], 1.0 / size, eps, ALU.mult, ALU.add).then_inc(mean, 1)
                e.wait_ge(root, 1)
                e.reciprocal(sm[:, 44:44 + n], sm[:, 40:40 + n]).then_inc(done, 1)

            cols = gated[:, 1, 16:24, :].rearrange("p a b -> p (a b)").rearrange("p (k m) -> p k m", m=P)

            def c_rest(hi_sem, ready):
                e.wait_ge(hi_sem, 1)
                e.tensor_tensor(cols[:, :, 2:4], sm[:, 0:32].rearrange("p (j k) -> p k j", j=2),
                                cols[:, :, 0:2].bitcast(F32), ALU.subtract).then_inc(ready, 1)

            def low(v, r, q, n):
                return e.tensor_tensor(r[:, 1, q:q + n, :], v.rearrange("p (c t) -> p c t", c=n),
                                       r[:, 0, q:q + n, :].bitcast(F32), ALU.subtract)

            e.memset(cols.bitcast(F32), 0.0).then_inc(S["c_zero"], 1)
            e.wait_ge(S["vec_turned"], 1)
            e.tensor_copy(vec[:, :], ps[:, 4, 0:V_W]).then_inc(S["vec_ready"], 1)
            e.wait_ge(S["silu_c"], 1)
            c_rest(S["c_hi"], S["c_ready"])
            splits(0, 4)
            mean_root_rstd(4, S["squares1"], 4, D, S["mean1"], S["root1"], S["rstd1"])

            def ada_rows(b, k):
                e.wait_ge(units_used, ready("ada", b))
                e.tensor_scalar(gatedf[0:4, ds(HI2 + 512 * b, 512)], ps[0:4, 2 * k, :], 1.0, None,
                                ALU.mult).then_inc(dve_freed, 1)
            segment("ada", 4, 8, ada_rows)

            e.wait_ge(S["mod_turned"], 1)
            for v in range(2):
                sh = ps[:, 4, v:32:2]
                sc = ps[:, 4, 32 + v:64:2]
                e.tensor_tensor(mod[:, 2 * v + 1, :], sh, vec[:, V_BADA:V_BADA + 16], ALU.add).then_inc(S["mod_step"], 1)
                e.tensor_tensor(mod[:, 2 * v, :], sc, vec[:, V_BADA + 16:V_BADA + 32], ALU.add).then_inc(S["mod_step"], 1)
                e.wait_ge(S["mod_step"], 2 * v + 2)
                e.scalar_tensor_tensor(out=mod[:, 2 * v, :], in0=mod[:, 2 * v, :], scalar=1.0,
                                       in1=vec[:, V_NORM:V_NORM + 16], op0=ALU.add, op1=ALU.mult).then_inc(S["mod_ready"], 1)
            e.wait_ge(S["mod_ready"], 2)
            for n in range(8):
                v, q = n // 4, n % 4
                r = act if v == 0 else gated
                spare = SPARE + (n % 2) * 1024
                e.wait_ge(S["h_turned"], n + 1)
                for c in range(4):
                    bank = 4 + 2 * (n % 2) + c // 2
                    o = spare + c * 256
                    e.tensor_scalar(gatedf[:, o:o + 256], ps[:, bank, (c % 2) * 256:(c % 2) * 256 + 256],
                                    mod[:, 2 * v, 4 * q + c:4 * q + c + 1], mod[:, 2 * v + 1, 4 * q + c:4 * q + c + 1],
                                    ALU.mult, ALU.add).then_inc(S["h_affine"], 1)
                e.wait_ge(S["h_hi"], n + 1)
                low(gatedf[:, spare:spare + 1024], r, 4 * q, 4).then_inc(S["h_lo"], 1)

            u0 = 2 * FIRST["in"]
            steps = 0

            def step(ins):
                nonlocal steps
                steps += 1
                ins.then_inc(S["rope_step"], 1)

            def settle():
                e.wait_ge(S["rope_step"], steps)

            nrope = 0
            for b in range(10):
                splits(u0 + 8 * b + 4, 8)
                if b in (0, 2, 3, 4):
                    for tt in range(4 if b == 0 else 2):
                        bank = tt if b == 0 else (0 if b % 2 == 0 else 2) + tt
                        src = ps[:, bank, :].rearrange("p (h d) -> p h d", d=DH)
                        if b == 0:
                            dst = gatedf[:, LO2 + tt * 512:LO2 + (tt + 1) * 512]
                        else:
                            dst = gatedf[:, HI2 + tt * 1536 + (b - 2) * 512:HI2 + tt * 1536 + (b - 1) * 512]
                        heads = dst.rearrange("p (h d) -> p h d", d=DH)
                        gain = t1[:, 128:256] if b == 0 else t1[:, 0:128]
                        sq = side[:, (nrope % 2) * 512:(nrope % 2) * 512 + 512].rearrange("p (h d) -> p h d", d=DH)
                        nrope += 1
                        e.wait_ge(S["sq_ready"], nrope)
                        step(e.tensor_reduce(sm[:, 32:36], sq, AX_X, ALU.add))
                        settle()
                        e.tensor_scalar(sm[:, 48:52], sm[:, 32:36], 1.0 / DH, EPS, ALU.mult, ALU.add).then_inc(S["ss_ready"], 1)
                        e.wait_ge(S["root_ready"], nrope)
                        step(e.reciprocal(sm[:, 68:72], sm[:, 52:56]))
                        settle()
                        ins = e.tensor_tensor(heads, src, sm[:, 68:72].unsqueeze(2).to_broadcast([P, 4, DH]), ALU.mult)
                        if tt == (3 if b == 0 else 1):
                            ins.then_inc(dve_freed, 1)
                            e.wait_ge(dve_freed, freed("in", b))
                        else:
                            step(ins)
                            settle()
                        step(e.tensor_tensor(heads, heads, gain.unsqueeze(1).to_broadcast([P, 4, DH]), ALU.mult))
                        if tt < 2:
                            o = T_ROPE + tt * 128
                            cc = tables[:, o:o + 128]
                            ss = tables[:, o + 256:o + 384].rearrange("p (a w f) -> p a w f", a=2, w=2)
                            halves = dst.rearrange("p (h a w f) -> p h a w f", h=4, a=2, w=2)
                            tmp = side[:, 1024:1536]
                            tmph = tmp.rearrange("p (h a w f) -> p h a w f", h=4, a=2, w=2)
                            settle()
                            for w in range(2):
                                step(e.tensor_tensor(tmph[:, :, :, w, :], halves[:, :, :, 1 - w, :],
                                                     ss[:, :, w, :].unsqueeze(1).to_broadcast([P, 4, 2, 32]), ALU.mult))
                            settle()
                            step(e.tensor_tensor(heads, heads, cc.unsqueeze(1).to_broadcast([P, 4, DH]), ALU.mult))
                            settle()
                            step(e.tensor_tensor(dst, dst, tmp, ALU.add))
            assert steps == ROPE_STEPS, steps

            e.wait_ge(S["dft2"], 1)
            mixed = side[:, 2048:3072]
            e.tensor_tensor(mixed.rearrange("p (b c) -> p b c", b=2), ps[:, 0:2, :],
                            gatedf[:, LO + 3072:LO + 4096].rearrange("p (b c) -> p b c", b=2),
                            ALU.mult).then_inc(S["mix_ready"], 1)
            e.wait_ge(S["mix_hi"], 1)
            low(mixed, gated, 12, 4).then_inc(S["mix_lo"], 1)

            probs = gatedf[:, LO2:LO2 + 1024]

            def kv_turn(kv):
                def top(j):
                    n = 3 * kv + j
                    e.wait_ge(S["scores_ready"], n + 1)
                    e.tensor_reduce(sm[:, 56:58], ps[:, 4 + 2 * (j % 2):6 + 2 * (j % 2), :], AX_X, ALU.max).then_inc(S["max_step"], 1)
                    e.wait_ge(S["max_step"], n + 1)
                    e.tensor_scalar(sm[:, 58:60], sm[:, 56:58], -ATT_SCALE, None, ALU.mult).then_inc(S["max_ready"], 1)

                def norm(j):
                    n = 3 * kv + j
                    e.wait_ge(S["exp_ready"], 2 * n + 2)
                    e.reciprocal(sm[:, 62:64], sm[:, 60:62]).then_inc(S["sum_inv"], 1)
                    e.wait_ge(S["sum_inv"], n + 1)
                    v = probs.rearrange("p (t s) -> p t s", t=2)
                    e.tensor_tensor(v, v, sm[:, 62:64].unsqueeze(2).to_broadcast([P, 2, 512]), ALU.mult).then_inc(S["probs_ready"], 1)

                def gate(j):
                    n = 3 * kv + j
                    e.wait_ge(S["o_ready"], n + 1)
                    e.tensor_tensor(t0[:, (j % 2) * 256:(j % 2) * 256 + 256], ps[:, 1, 256:512],
                                    gatedf[:, ds(768 * kv + LO + 256 * j, 256)], ALU.mult).then_inc(S["o_gated"], 1)

                def rest(j):
                    n = 3 * kv + j
                    e.wait_ge(S["o_hi"], n + 1)
                    v = t0[:, (j % 2) * 256:(j % 2) * 256 + 256]
                    e.tensor_tensor(gated[:, 1, ds(3 * kv + j, 1), :], v.unsqueeze(1),
                                    gated[:, 0, ds(3 * kv + j, 1), :].bitcast(F32), ALU.subtract).then_inc(S["o_lo"], 1)
                top(0)
                norm(0)
                top(1)
                gate(0)
                norm(1)
                rest(0)
                top(2)
                gate(1)
                norm(2)
                rest(1)
                gate(2)
                rest(2)
            each(e, HKV, kv_turn)

            segment("gate_a", 4, 4, lambda b, k: None)
            segment("gate_b", 4, 4, lambda b, k: None)

            def proj(b, k):
                e.wait_ge(units_used, ready("proj", b))
                m = side[:, 1024:2048].rearrange("p (b c) -> p b c", b=2)
                t = side[:, 0:1024].rearrange("p (b c) -> p b c", b=2)
                e.tensor_tensor(m, ps[:, 4 * k:4 * k + 2, :], gatedf[:, ds(HI2 + 1024 * b, 1024)].rearrange(
                    "p (b c) -> p b c", b=2), ALU.mult).then_inc(S["proj_read"], 1)
                e.tensor_tensor(t, ps[:, 4 * k + 2:4 * k + 4, :], gatedf[:, ds(LO2 + 1024 * b, 1024)].rearrange(
                    "p (b c) -> p b c", b=2), ALU.mult).then_inc(dve_freed, 1)
                e.wait_ge(dve_freed, freed("proj", b))
                e.tensor_tensor(m, m, t, ALU.add).then_inc(S["proj_sum"], 1)
                e.wait_ge(S["proj_hi"], b + 1)
                v = side[:, 1024:2048].rearrange("p (c t) -> p c t", c=4)
                e.tensor_tensor(act[:, 1, ds(4 * b, 4), :], v, act[:, 0, ds(4 * b, 4), :].bitcast(F32),
                                ALU.subtract).then_inc(S["proj_lo"], 1)
            segment("proj", 4, 4, proj)

            e.wait_ge(units_used, ready("proj", 3))
            e.memset(cols.bitcast(F32), 0.0).then_inc(S["c2_zero"], 1)
            c_rest(S["c2_hi"], S["c2_ready"])

            def gate_rows(b, k):
                e.wait_ge(units_used, ready("ada_gate", b))
                e.tensor_scalar(gatedf[0:4, ds(HI2 + 512 * b, 512)], ps[0:4, 2 * k, :], 1.0, None,
                                ALU.mult).then_inc(dve_freed, 1)
            segment("ada_gate", 4, 4, gate_rows)
            e.wait_ge(S["bias_loaded"], 32)
            e.wait_ge(S["gate_turned"], 1)
            gate = side[:, 0:D]
            e.tensor_tensor(gate.rearrange("p (b c) -> p b c", b=4), ps[:, 4:8, :],
                            gate.rearrange("p (b c) -> p b c", b=4), ALU.add).then_inc(S["gate_ready"], 1)
            e.wait_ge(S["gate_ready"], 1)

            def out_add(b, k):
                e.wait_ge(units_used, ready("out", b))
                for tt in range(2):
                    e.wait_ge(S["out_step"], 2 * b + tt)
                    ins = e.tensor_tensor(t0[:, :], ps[:, 2 * k + tt, :], side[:, ds(512 * b, 512)], ALU.mult)
                    if tt == 0:
                        ins.then_inc(S["out_read"], 1)
                        e.wait_ge(S["out_read"], b + 1)
                    else:
                        ins.then_inc(dve_freed, 1)
                        e.wait_ge(dve_freed, freed("out", b))
                    v = x[:, tt, ds(512 * b, 512)]
                    e.tensor_tensor(v, v, t0[:, :], ALU.add).then_inc(S["out_step"], 1)
            segment("out", 4, 4, out_add)

            e.wait_ge(S["out_step"], 8)
            mean_root_rstd(2, S["sq2"], 2, D, S["mean2"], S["root2"], S["rstd2"])
            for q in range(4):
                for n in range(2):
                    e.wait_ge(S["scaled2"], 2 * q + n + 1)
                    v = x[:, n, q * 512:(q + 1) * 512]
                    e.tensor_tensor(v, v, side[:, D + q * 512:D + (q + 1) * 512], ALU.mult).then_inc(S["normed2"], 1)

            def low_x(hi, done):
                for q in range(4):
                    e.wait_ge(hi, q + 1)
                    b = 4 + 2 * (q % 2)
                    e.tensor_tensor(act[:, 1, 4 * q:4 * q + 4, :], ps[:, b:b + 2, :].rearrange("p b (c t) -> p (b c) t", c=2),
                                    act[:, 0, 4 * q:4 * q + 4, :].bitcast(F32), ALU.subtract).then_inc(done, 1)
            low_x(S["x2_hi"], S["x2_lo"])

            y, mag, ee, u, ln, dd, dt = (tx[0:64, n * 256:(n + 1) * 256] for n in range(7))
            adt, acs, rec = u, mag, ee

            def step(n, ins):
                ins.then_inc(S["dt_step"], 1)
            e.wait_ge(S["dt_act"], 1)
            step(1, e.scalar_tensor_tensor(out=mag, in0=y, scalar=-1.0, in1=y, op0=ALU.mult, op1=ALU.max))
            e.wait_ge(S["dt_act"], 3)
            step(2, e.tensor_scalar(u, ee, 1.0, None, ALU.add))
            e.wait_ge(S["dt_step"], 2)
            step(3, e.scalar_tensor_tensor(out=dd, in0=u, scalar=-1.0, in1=ee, op0=ALU.add, op1=ALU.subtract))
            e.wait_ge(S["dt_step"], 3)
            step(4, e.reciprocal(rec, u))
            e.wait_ge(S["dt_step"], 4)
            step(5, e.tensor_tensor(dd, dd, rec, ALU.mult))
            e.wait_ge(S["dt_act"], 4)
            e.wait_ge(S["dt_step"], 5)
            step(6, e.tensor_tensor(ln, ln, dd, ALU.subtract))
            e.wait_ge(S["dt_step"], 6)
            step(7, e.scalar_tensor_tensor(out=dt, in0=y, scalar=0.0, in1=ln, op0=ALU.max, op1=ALU.add))
            step(8, e.memset(dd, 1.0))
            e.wait_ge(S["dt_step"], 8)
            step(9, e.tensor_scalar(adt, dt, sm[0:64, 66:67], -1.0, ALU.mult, ALU.mult))
            e.wait_ge(S["dt_step"], 9)
            step(10, e.tensor_tensor_scan(acs, dd, adt, 0.0, ALU.mult, ALU.add))
            e.wait_ge(S["dt_turned"], 1)
            e.tensor_copy(t1[:, :], ps[:, 5, 0:256]).then_inc(S["dt_ready"], 1)
            e.wait_ge(S["acs_stored"], 16)

            def conv(nb, ch0):
                def go(b, k):
                    e.wait_ge(units_used, ready("ssd_x") + nb + b)
                    for n in range(2):
                        if n == 1:
                            e.wait_ge(S["conv_silu"], 2 * nb + 2 * b)
                        for c in range(2):
                            fc = 2 * n + c
                            ch = 4 * b + ch0 + fc
                            src = ps[:, 2 * k + n, c * 256:(c + 1) * 256]
                            acc = tx[:, fc * 256:(fc + 1) * 256]
                            before = 14 * nb + 7 * n + 4 * c + 14 * b
                            e.tensor_scalar(acc, src, vec[:, ds(ch + V_CW + 144, 1)], vec[:, ds(ch + V_CB, 1)],
                                            ALU.mult, ALU.add).then_inc(S["conv_step"], 1)
                            for s in range(1, 4):
                                e.wait_ge(S["conv_step"], before + s)
                                ins = e.scalar_tensor_tensor(out=acc[:, s:], in0=src[:, :L - s],
                                                             scalar=vec[:, ds(ch + V_CW + 48 * (3 - s), 1)],
                                                             in1=acc[:, s:], op0=ALU.mult, op1=ALU.add)
                                last = s == 3 and c == 1
                                ins.then_inc((S["conv_done"], dve_freed)[n] if last else S["conv_step"], 1)
                    e.wait_ge(S["conv_silu"], 2 * nb + 1 + 2 * b)
                return go
            segment("ssd_x", 4, 8, conv(0, 0))
            segment("ssd_bc", 4, 4, conv(8, 32))
            segment("ssd_z", 4, 8, lambda b, k: None)

            ex = actf[:, 2048:5120]
            rb = actf[:, 0:2048]
            xtok = actf[:, 6400:7424]
            cbm = t0[:, 0:384]

            def by_head(v, g, per_head):
                return per_head[:, ds(8 * g, 8)].unsqueeze(2).to_broadcast([P, R, HD])

            def scan_turn(g):
                e.wait_ge(S["y_lo"], g)
                e.wait_ge(S["xs_ready"], g + 1)
                for tt in range(2):
                    v = xtok[:, tt * 512:(tt + 1) * 512].rearrange("p (h d) -> p h d", d=HD)
                    yb = tx[:, tt * 512:(tt + 1) * 512].rearrange("p (h d) -> p h d", d=HD)
                    e.tensor_tensor(yb, v, by_head(v, g, t0[:, 384:448]), ALU.mult).then_inc(S["xdt_step"], 1)
                for tt in range(2):
                    v = xtok[:, tt * 512:(tt + 1) * 512].rearrange("p (h d) -> p h d", d=HD)
                    e.tensor_tensor(v, v, by_head(v, g, t1[:, 128 + tt * 64:192 + tt * 64]), ALU.mult).then_inc(S["xdt_step"], 1)
                e.wait_ge(S["cb_ready"], g + 1)
                e.tensor_tensor(cbm, ps[:, 0, 0:384], tables[:, T_TRI:T_TRI + 384], ALU.mult).then_inc(S["cb_masked"], 1)
                e.wait_ge(S["r_loaded"], 16 * g + 16)
                for h in range(R):
                    for tt in range(2):
                        o = h * 384 + tt * 256
                        w = 256 - tt * 128
                        ins = e.tensor_scalar(ex[:, o:o + w], rb[:, h * 256 + tt * 128:h * 256 + 256],
                                              t1[:, ds(8 * g + tt * 64 + h, 1)], 0.0, ALU.subtract, ALU.min)
                    if h % 4 == 3:
                        ins.then_inc(S["diff_ready"], 1)
                e.wait_ge(S["cb_masked"], g + 1)
                for n in range(2):
                    e.wait_ge(S["decay_ready"], 2 * g + n + 1)
                    v = ex[:, n * 1536:(n + 1) * 1536].rearrange("p (h l) -> p h l", h=4)
                    e.tensor_tensor(v, v, cbm.unsqueeze(1).to_broadcast([P, 4, 384]), ALU.mult).then_inc(S["m_ready"], 1)
                e.wait_ge(S["y_mm"], g + 1)
                e.wait_ge(S["xdt_step"], 4 * g + 4)
                yb = tx[:, 0:1024]
                e.tensor_tensor(yb.rearrange("p (b c) -> p b c", b=2), ps[:, 3:5, :], yb.rearrange("p (b c) -> p b c", b=2),
                                ALU.add).then_inc(S["y_step"], 1)
                e.wait_ge(S["y_step"], 5 * g + 1)
                e.tensor_tensor(yb, yb, gatedf[:, ds(1024 * g + LO, 1024)], ALU.mult).then_inc(S["y_step"], 1)
                e.wait_ge(S["y_act"], 3 * g + 2)
                e.tensor_scalar(sm[:, 36:38], sm[:, 32:34], 1.0 / 512, EPS, ALU.mult, ALU.add).then_inc(S["y_step"], 1)
                e.wait_ge(S["y_act"], 3 * g + 3)
                e.reciprocal(sm[:, 44:46], sm[:, 40:42]).then_inc(S["y_step"], 1)
                e.wait_ge(S["y_turned"], g + 1)
                for c in range(4):
                    ins = e.tensor_scalar(tx[:, c * 256:(c + 1) * 256],
                                          ps[:, 5 + c // 2, (c % 2) * 256:(c % 2) * 256 + 256],
                                          vec[:, ds(4 * g + V_SSDG + c, 1)], None, ALU.mult)
                ins.then_inc(S["y_step"], 1)
                e.wait_ge(S["y_hi"], g + 1)
                e.tensor_tensor(gated[:, 1, ds(4 * g, 4), :], tx[:, 0:1024].rearrange("p (c t) -> p c t", c=4),
                                gated[:, 0, ds(4 * g, 4), :].bitcast(F32), ALU.subtract).then_inc(S["y_lo"], 1)
            each(e, G, scan_turn)

            def residual(seg, name):
                def go(b, k):
                    e.wait_ge(units_used, ready(seg, b))
                    for tt in range(2):
                        v = x[:, tt, ds(512 * b, 512)]
                        e.scalar_tensor_tensor(out=v, in0=v, scalar=ALPHA, in1=ps[:, 2 * k + tt, :], op0=ALU.mult,
                                               op1=ALU.add).then_inc(dve_freed if tt else S[name], 1)
                return go
            segment("ssd_out", 8, 4, residual("ssd_out", "half_read"))

            def layer_norm(seg, dve, stats, act_sem, rstd, rows):
                e.wait_ge(dve_freed, freed(seg, 3))
                for n in range(2):
                    for q in range(4):
                        e.bn_stats(t0[:, n * 24 + q * 6:n * 24 + q * 6 + 6], x[:, n, q * 512:(q + 1) * 512]).then_inc(dve, 1)
                e.wait_ge(dve, 8)
                for n in range(2):
                    e.bn_aggr(sm[:, 32 + 2 * n:34 + 2 * n], t0[:, n * 24:n * 24 + 24]).then_inc(dve, 1)
                e.wait_ge(dve, 10)
                e.tensor_scalar(sm[:, 38:40], sm[:, 33:37:2], LN_EPS, None, ALU.add).then_inc(stats, 1)
                e.wait_ge(act_sem, 1)
                e.reciprocal(sm[:, 44:46], sm[:, 40:42]).then_inc(dve, 1)
                e.wait_ge(dve, 11)
                e.scalar_tensor_tensor(out=sm[:, 46:48], in0=sm[:, 32:36:2], scalar=-1.0, in1=sm[:, 44:46],
                                       op0=ALU.mult, op1=ALU.mult).then_inc(rstd, 1)
                e.wait_ge(rows, 32)
                for q in range(4):
                    for n in range(2):
                        e.wait_ge(act_sem, 2 + 2 * q + n)
                        v = x[:, n, q * 512:(q + 1) * 512]
                        e.tensor_tensor(v, v, side[:, q * 512:(q + 1) * 512], ALU.mult).then_inc(dve, 1)
                    for n in range(2):
                        e.wait_ge(dve, 11 + 4 * q + n + 1)
                        v = x[:, n, q * 512:(q + 1) * 512]
                        e.tensor_tensor(v, v, side[:, D + q * 512:D + (q + 1) * 512], ALU.add).then_inc(dve, 1)
            layer_norm("ssd_out", S["ln_dve"], S["ln_stats"], S["ln_act"], S["ln_rstd"], S["ln_rows"])
            low_x(S["x3_hi"], S["x3_lo"])

            u0 = 2 * FIRST["lat_q"]
            splits(u0 + 4, 16)
            e.wait_ge(S["lat_sq"], 4)
            e.tensor_scalar(sm[:, 36:38], sm[:, 32:34], 1.0 / 512, EPS, ALU.mult, ALU.add).then_inc(S["lat_mean"], 1)
            e.tensor_scalar(sm[:, 38:40], sm[:, 34:36], 1.0 / 256, EPS, ALU.mult, ALU.add).then_inc(S["lat_mean"], 1)
            e.wait_ge(S["lat_root"], 1)
            e.reciprocal(sm[:, 44:48], sm[:, 40:44]).then_inc(S["lat_rstd"], 1)
            for tt in range(2):
                o = 1024 + tt * 336 + 256
                e.tensor_copy(t1[:, tt * 128:(tt + 1) * 128].rearrange("p (r d) -> p r d", r=2),
                              tx[:, o:o + 64].unsqueeze(1).to_broadcast([P, 2, 64])).then_inc(S["lat_act"], 1)
            e.wait_ge(S["lat_turned"], 1)
            for c in range(6):
                bank, o = (4 + c // 2, (c % 2) * 256) if c < 4 else (6, (c - 4) * 256)
                gain = V_QN + c if c < 4 else V_KVN + c - 4
                dst = tx[:, c * 256:(c + 1) * 256] if c < 4 else t0[:, (c - 4) * 256:(c - 3) * 256]
                e.tensor_scalar(dst, ps[:, bank, o:o + 256],
                                vec[:, gain:gain + 1], None, ALU.mult).then_inc(S["lat_scaled"], 1)
            e.wait_ge(S["lat_hi"], 2)
            low(tx[:, 0:1024], lat, 0, 4).then_inc(S["lat_lo"], 1)
            low(t0[:, 0:512], lat, 4, 2).then_inc(S["lat_lo"], 1)
            splits(2 * FIRST["lat_gate"], 4)

            score = side[:, 3072:3456]
            bias = side[:, 3456:3840]
            parts = ((0, 128), (128, 384))
            for h in range(16):
                e.wait_ge(S["idx_relu"], h + 1)
                o = 2304 + (h % 2) * 384
                for tt, (lo, hi) in enumerate(parts):
                    w = tx[:, 1024 + tt * 336 + 320 + h:1025 + tt * 336 + 320 + h]
                    if h == 0:
                        ins = e.tensor_scalar(score[:, lo:hi], gatedf[:, o + lo:o + hi], w, None, ALU.mult)
                    else:
                        e.wait_ge(S["idx_step"], 2 * h - 1 + tt)
                        ins = e.scalar_tensor_tensor(out=score[:, lo:hi], in0=gatedf[:, o + lo:o + hi], scalar=w,
                                                     in1=score[:, lo:hi], op0=ALU.mult, op1=ALU.add)
                    ins.then_inc(S["idx_step"], 1)
            e.wait_ge(S["idx_step"], 32)
            for lo in (0, 256):
                v = score[:, lo:lo + 128]
                e.tensor_tensor(v, v, tables[:, T_UNSEEN:T_UNSEEN + 128], ALU.add).then_inc(S["idx_step"], 1)
            for r in range(TOPK // 8):
                for tt, (lo, hi) in enumerate(parts):
                    e.wait_ge(S["idx_step"], 34 + 4 * r if r == 0 else 33 + 4 * r + tt)
                    e.max(sm[:, 8 * tt:8 * tt + 8], score[:, lo:hi]).then_inc(S["idx_step"], 1)
                for tt, (lo, hi) in enumerate(parts):
                    e.wait_ge(S["idx_step"], 35 + 4 * r + tt)
                    e.match_replace(score[:, lo:hi], sm[:, 8 * tt:8 * tt + 8], score[:, lo:hi],
                                    TAKEN).then_inc(S["idx_step"], 1)
            e.wait_ge(S["idx_step"], 66)
            e.tensor_scalar(bias, score, -3.2e38, NEG, ALU.is_gt, ALU.mult).then_inc(S["idx_step"], 1)
            e.wait_ge(S["idx_step"], 67)
            for lo in (0, 256):
                v = bias[:, lo:lo + 128]
                e.tensor_tensor(v, v, tables[:, T_NEG:T_NEG + 128], ALU.add).then_inc(S["idx_done"], 1)
            segment("lat_gate", 4, 8, lambda b, k: None)

            e.wait_ge(S["idx_done"], 2)

            def heads_turn(i):
                for k in range(2):
                    gi = 2 * i + k
                    splits(2 * FIRST["head_q"] + 4 * k + 4, 4, i, 8)

                    def top(h):
                        n = 4 * gi + h
                        p = actf[:, 6144 + (h % 2) * 384:6528 + (h % 2) * 384]
                        e.wait_ge(S["hs_mm"], n + 1)
                        e.tensor_tensor(p, ps[:, 4 + h % 2, 0:384], bias, ALU.add).then_inc(S["hs_masked"], 1)
                        e.wait_ge(S["hs_masked"], n + 1)
                        for tt, (lo, hi) in enumerate(parts):
                            e.tensor_reduce(sm[:, 56 + tt:57 + tt], p[:, lo:hi], AX_X, ALU.max).then_inc(S["hs_step"], 1)
                        e.wait_ge(S["hs_step"], 2 * n + 2)
                        e.tensor_scalar(sm[:, 58:60], sm[:, 56:58], -ATT_SCALE, None, ALU.mult).then_inc(S["hs_max"], 1)

                    def norm(h):
                        n = 4 * gi + h
                        p = actf[:, 6144 + (h % 2) * 384:6528 + (h % 2) * 384]
                        e.wait_ge(S["hs_exp"], 2 * n + 2)
                        e.reciprocal(sm[:, 62:64], sm[:, 60:62]).then_inc(S["hs_inv"], 1)
                        e.wait_ge(S["hs_inv"], n + 1)
                        for tt, (lo, hi) in enumerate(parts):
                            ins = e.tensor_scalar(p[:, lo:hi], p[:, lo:hi], sm[:, 62 + tt:63 + tt], None, ALU.mult)
                        ins.then_inc(S["hs_probs"], 1)

                    def gate(h):
                        n = 4 * gi + h
                        e.wait_ge(S["ho_mm"], n + 1)
                        o = 7680 + (h % 2) * 256
                        e.tensor_tensor(actf[:, o:o + 256], ps[:, 7, (h % 2) * 256:(h % 2) * 256 + 256],
                                        gatedf[:, ds(LO + 256 * n, 256)], ALU.mult).then_inc(S["ho_gated"], 1)

                    def rest(h):
                        n = 4 * gi + h
                        e.wait_ge(S["ho_hi"], n + 1)
                        v = actf[:, 7680 + (h % 2) * 256:7936 + (h % 2) * 256]
                        e.tensor_tensor(gated[:, 1, ds(n, 1), :], v.unsqueeze(1), gated[:, 0, ds(n, 1), :].bitcast(F32),
                                        ALU.subtract).then_inc(S["ho_lo"], 1)
                    top(0)
                    norm(0)
                    for h in range(4):
                        if h < 3:
                            top(h + 1)
                        gate(h)
                        if h < 3:
                            norm(h + 1)
                        rest(h)
            each(e, 3, heads_turn)
            heads_turn(3)

            u0 = 2 * FIRST["lat_out"]
            add = residual("lat_out", "half_read")
            for b in range(4):
                splits(u0 + 16 * b + 4, 16)
                add(b, b % 2)
            layer_norm("lat_out", S["fin_dve"], S["fin_stats"], S["fin_act"], S["fin_rstd"], S["fin_rows"])

        @block.gpsimd
        def _(e):
            def fixed():
                e.wait_ge(S["small_loaded"], 16 * 17)

            def bc(dst, src, done):
                e.dma_start(dst, src.partition_broadcast(P)).then_inc(done, 16)

            def stage(kv):
                e.wait_ge(S["qt_turned"], 3 * kv)
                fixed()
                e.tensor_copy(side[:, 2048:2816].rearrange("p (t c) -> p t c", t=2),
                              gatedf[:, HI2:HI2 + 3072].rearrange("p (t c) -> p t c", t=2)[:, :, ds(384 * kv, 384)]
                              ).then_inc(S["q_staged"], 1)
                e.wait_ge(S["o_ready"], 3 * kv)
                fixed()
                e.tensor_copy(side[:, 2816:3328].rearrange("p (t c) -> p t c", t=4),
                              gatedf[:, LO2 + 2048:LO2 + 4096].rearrange("p (t c) -> p t c", t=4)[:, :, ds(128 * kv, 128)]
                              ).then_inc(S["v_staged"], 1)
            e.wait_ge(S["mix_lo"], 1)
            each(e, HKV, stage)

            e.wait_ge(S["proj_lo"], 4)
            bc(side[:, 0:D], a["b_ada"][2 * D:3 * D], S["bias_loaded"])
            bc(side[:, D:2 * D], a["final_g"], S["bias_loaded"])
            e.wait_ge(dve_freed, freed("out", 3))

            e.wait_ge(S["out_step"], 8)
            bc(t0[:, 384:448], a["ssd_d_skip_2"], S["rows_loaded"])
            e.dma_start(sm[0:64, 64:65], a["ssd_a_log_2"].rearrange("(h o) -> h o", o=1)).then_inc(S["rows_loaded"], 16)
            e.dma_start(sm[0:64, 65:66], a["ssd_dt_bias_2"].rearrange("(h o) -> h o", o=1)).then_inc(S["rows_loaded"], 16)
            e.wait_ge(S["normed2"], 8)
            for n in range(2):
                e.dma_start(side[:, n * 512:(n + 1) * 512].rearrange("p (c h) -> p c h", c=8),
                            a["ssd_w_in_2"][n * 1024:(n + 1) * 1024, 10240:10304].rearrange("(c p) h -> p c h", p=P)
                            ).then_inc(S["rows_loaded"], 16)
            e.wait_ge(S["dt_step"], 10)
            e.dma_start(acs_dram, tx[0:64, 256:512]).then_inc(S["acs_stored"], 16)
            e.wait_ge(S["acs_stored"], 16)

            e.wait_ge(units_used, ready("ssd_z", 7))
            e.wait_ge(S["conv_silu"], 24)

            def stage_scan(g):
                e.wait_ge(S["diff_ready"], 2 * g)
                e.dma_start(actf[:, 0:2048], acs_dram[ds(8 * g, 8), :].rearrange("h l -> (h l)").partition_broadcast(P)
                            ).then_inc(S["r_loaded"], 16)
                e.wait_ge(S["cb_ready"], g)
                fixed()
                e.tensor_copy(actf[:, 6144:6400], side[:, ds(256 * g, 256)]).then_inc(S["b_staged"], 1)
                e.wait_ge(S["xs_turned"], g)
                fixed()
                e.tensor_copy(actf[:, 5120:6144], gatedf[:, ds(1024 * g, 1024)]).then_inc(S["b_staged"], 1)
            each(e, G, stage_scan)
            e.wait_ge(S["cb_ready"], G)
            bc(side[:, 0:D], a["ln_g_2"][0, :], S["ln_rows"])
            bc(side[:, D:2 * D], a["ln_b_2"][0, :], S["ln_rows"])
            e.wait_ge(S["hs_masked"], 32)
            e.wait_ge(units_used, 2 * FIRST["lat_out"])
            bc(side[:, 0:D], a["ln_g_2"][1, :], S["fin_rows"])
            bc(side[:, D:2 * D], a["ln_b_2"][1, :], S["fin_rows"])
            o_v = out.rearrange("(t p) d -> p t d", p=P)
            for q in range(4):
                e.wait_ge(S["fin_dve"], 15 + 4 * q)
                e.dma_start(o_v[:, :, q * 512:(q + 1) * 512], x[:, :, q * 512:(q + 1) * 512]).then_inc(S["stored"], 16)
            e.wait_ge(S["stored"], 64)

        @block.tensor
        def _(e):
            def unit(u, i, step, body):
                e.wait_ge(lo_done, linear(lambda v: v + 1, u, step, i))
                for c in range(2):
                    last = body(c, u % SPLIT)
                last.then_inc(units_used, 1)

            def tokens_out(banks, left, kc, slot, c, first, last, w=CB):
                for bank, (hi, lo) in zip(banks, left):
                    e.matmul(ps[:, bank, :w], hi, w_hi[:, slot, c, :w], start=first, stop=False)
                    e.matmul(ps[:, bank, :w], hi, w_lo[:, slot, c, :w], start=False, stop=False)
                    ins = e.matmul(ps[:, bank, :w], lo, w_hi[:, slot, c, :w], start=False, stop=last)
                return ins

            def features_out(bank, hi, lo, slot, c, first, last):
                for f in range(4):
                    o = ps[:, bank + f // 2, (f % 2) * 256:(f % 2) * 256 + 256]
                    wh = w_hi[:, slot, c, f * P:(f + 1) * P]
                    wl = w_lo[:, slot, c, f * P:(f + 1) * P]
                    e.matmul(o, wh, hi, start=first and f % 2 == 0, stop=False, skip_group_check=True)
                    e.matmul(o, wh, lo, start=False, stop=False, skip_group_check=True)
                    ins = e.matmul(o, wl, hi, start=False, stop=last and f % 2 == 1, skip_group_check=True)
                return ins

            def tok(src, kc, tt):
                return src[:, 0, kc, tt * P:(tt + 1) * P], src[:, 1, kc, tt * P:(tt + 1) * P]

            def gemm(u0, n, src, bank, by_token, i=0, step=0, w=CB, kc0=0):
                for m in range(n):
                    def body(c, slot, m=m):
                        kc = kc0 + 2 * m + c
                        first, last = m == 0 and c == 0, m == n - 1 and c == 1
                        if by_token:
                            return tokens_out((bank, bank + 1), (tok(src, kc, 0), tok(src, kc, 1)), kc, slot, c, first, last, w)
                        return features_out(bank, src[:, 0, kc, :], src[:, 1, kc, :], slot, c, first, last)
                    unit(u0 + m, i, step, body)

            def pair_free(n, i=0):
                for sem_, who in ((act_freed, "act"), (dve_freed, "dve")):
                    if n >= 2 and isinstance(i, int) and freed_count(who, n + 2 * i - 2):
                        e.wait_ge(sem_, freed_count(who, n + 2 * i - 2))

            def segment(seg, per, nblocks, body):
                n0 = BI[seg]
                who = BLOCKS[n0][1]
                mine = act_freed if who == "act" else dve_freed
                other, its = (dve_freed, "dve") if who == "act" else (act_freed, "act")
                pair_free(n0)

                def two(i):
                    for k in range(2):
                        done = freed_count(who, n0 - 1) - 1 + k
                        if done >= 0:
                            e.wait_ge(mine, done + 2 * i)
                        if k == 1 and freed_count(its, n0 - 1):
                            e.wait_ge(other, freed_count(its, n0 - 1))
                        body(2 * i + k, k, i, 2 * FIRST[seg] + 2 * per * k, 4 * per)
                each(e, nblocks // 2, two)

            def turn4(src_at, q, b):
                for c in range(4):
                    for tt in range(2):
                        ins = e.transpose(ps[:, b + c // 2, (c % 2) * 256 + tt * P:(c % 2) * 256 + (tt + 1) * P],
                                          src_at(4 * q + c, tt), ident)
                return ins

            e.wait_ge(S["small_loaded"], 16 * 17)
            o = 0
            for n, rows in enumerate((102, 96, 96, 80)):
                ins = e.transpose(ps[:, 4, o:o + rows], t0[0:rows, n * P:(n + 1) * P], ident[0:rows, 0:rows])
                o += rows
            ins.then_inc(S["vec_turned"], 1)

            cols = gated[:, 1, 16:24, :].rearrange("p a b -> p (a b)").rearrange("p (k m) -> p k m", m=P)

            def modulation(b, k, i, u0, step):
                for m in range(8):
                    def body(c, slot, m=m):
                        kc = 2 * m + c
                        e.matmul(ps[:, 2 * k, :], cols[:, kc, :], w_hi[:, slot, c, :], start=kc == 0, stop=False)
                        return e.matmul(ps[:, 2 * k, :], cols[:, kc, :], w_lo[:, slot, c, :], start=False, stop=kc == 15)
                    unit(u0 + m, i, step, body)
            e.wait_ge(S["c_ready"], 1)
            ADA = BI["ada"]
            assert ADA == 0

            def first_two(i):
                for k in range(2):
                    if k == 1:
                        e.wait_ge(dve_freed, 2 * i)
                    modulation(2 * i + k, k, i, 8 * k, 16)
                    if k == 1:
                        e.wait_ge(dve_freed, 2 * i + 1)
            each(e, 4, first_two)

            e.wait_ge(dve_freed, freed("ada", 7))
            for c in range(32):
                ins = e.matmul(ps[:, 4, 2 * c:2 * c + 2], gatedf[0:4, HI2 + c * P:HI2 + (c + 1) * P],
                               tables[0:4, T_SEL:T_SEL + 2], start=True, stop=True)
            ins.then_inc(S["mod_turned"], 1)
            e.wait_ge(S["xn_ready"], 4)
            e.wait_ge(S["mod_ready"], 2)
            for n in range(8):
                if n >= 2:
                    e.wait_ge(S["h_affine"], 4 * n - 4)
                src = gatedf if n < 4 else side
                turn4(lambda c, tt: src[:, tt * D + c * P:tt * D + (c + 1) * P], n % 4,
                      4 + 2 * (n % 2)).then_inc(S["h_turned"], 1)

            e.wait_ge(S["h_lo"], 8)
            for b in range(10):
                u0 = 2 * FIRST["in"] + 8 * b
                if b < 2:
                    for m in range(8):
                        def body(c, slot, m=m, b=b):
                            kc = 2 * m + c
                            return tokens_out([4 * b + t for t in range(4)],
                                              [tok(act, kc, 0), tok(act, kc, 1), tok(gated, kc, 0), tok(gated, kc, 1)],
                                              kc, slot, c, kc == 0, kc == 15)
                        unit(u0 + m, 0, 0, body)
                    continue
                if b < 4:
                    e.wait_ge(dve_freed, freed("in", 0))
                else:
                    pair_free(BI["in"] + b)
                gemm(u0, 8, act, 2 * (b % 2), b < 6)

            e.wait_ge(S["rope_step"], ROPE_STEPS)
            e.wait_ge(act_freed, freed("in", 1))
            for kv in range(HKV):
                for tt in range(4):
                    o = LO2 + tt * 512 + kv * P
                    ins = e.transpose(ps[:, 4 + kv, tt * P:(tt + 1) * P], gatedf[:, o:o + P], ident)
                ins.then_inc(S["k_turned"], 1)
            e.wait_ge(act_freed, freed("in", 5))
            for g in range(4):
                e.wait_ge(S["kt_ready"], g + 1)
                for kt in range(2):
                    o = HI2 + 3072 + kt * 512 + g * P
                    ins = e.matmul(ps[:, 4 + g, :], gatedf[:, o:o + P], tables[:, T_DFT + kt * 512:T_DFT + (kt + 1) * 512],
                                   start=kt == 0, stop=kt == 1)
                ins.then_inc(S["dft1"], 1)
            e.wait_ge(act_freed, freed("in", 9))
            e.wait_ge(S["dft1_out"], 4)
            for g in range(4):
                for w in range(2):
                    o = 2048 + g * 512 + w * 256
                    ins = e.matmul(ps[:, g // 2, (g % 2) * 256:(g % 2) * 256 + 256],
                                   tables[:, T_DFTC + w * P:T_DFTC + (w + 1) * P], side[:, o:o + 256],
                                   start=w == 0, stop=w == 1)
            ins.then_inc(S["dft2"], 1)

            e.wait_ge(S["mix_ready"], 1)
            probs = gatedf[:, LO2:LO2 + 1024]
            pt = gatedf[:, LO2 + 1024:LO2 + 2048]
            qt = side[:, 3328:4096]

            def kv_turn(kv):
                e.wait_ge(S["q_staged"], kv + 1)
                e.wait_ge(S["qt_ready"], 3 * kv)
                e.wait_ge(S["o_gated"], 3 * kv)
                for j in range(3):
                    for tt in range(2):
                        o = 2048 + tt * 384 + j * P
                        ins = e.transpose(ps[:, j // 2, (j % 2) * 256 + tt * P:(j % 2) * 256 + (tt + 1) * P],
                                          side[:, o:o + P], ident)
                    ins.then_inc(S["qt_turned"], 1)

                def scores(j):
                    e.wait_ge(S["qt_ready"], 3 * kv + j + 1)
                    e.wait_ge(S["exp_ready"], 6 * kv + (2 if j == 2 else 0))
                    for tt in range(2):
                        ins = e.matmul(ps[:, 4 + 2 * (j % 2) + tt, :], qt[:, j * 256 + tt * P:j * 256 + (tt + 1) * P],
                                       side[:, ds(512 * kv, 512)], start=True, stop=True)
                    ins.then_inc(S["scores_ready"], 1)

                def mix(j):
                    n = 3 * kv + j
                    e.wait_ge(S["probs_ready"], n + 1)
                    e.wait_ge(S["pt_ready"], n)
                    for tt in range(2):
                        for c in range(4):
                            o = tt * 512 + c * P
                            ins = e.transpose(ps[:, 2 + c // 2, (c % 2) * 256 + tt * P:(c % 2) * 256 + (tt + 1) * P],
                                              probs[:, o:o + P], ident)
                    ins.then_inc(S["probs_turned"], 1)
                    e.wait_ge(S["pt_ready"], n + 1)
                    e.wait_ge(S["v_staged"], kv + 1)
                    e.wait_ge(S["o_gated"], n)
                    for c in range(4):
                        ins = e.matmul(ps[:, 1, 256:512], side[:, 2816 + c * P:2816 + (c + 1) * P],
                                       pt[:, c * 256:(c + 1) * 256], start=c == 0, stop=c == 3)
                    ins.then_inc(S["o_ready"], 1)
                scores(0)
                scores(1)
                mix(0)
                scores(2)
                mix(1)
                mix(2)
            each(e, HKV, kv_turn)

            e.wait_ge(S["o_gated"], 12)

            def from_act(by_token):
                def go(b, k, i, u0, step):
                    gemm(u0, 8, act, 2 * k, by_token, i, step)
                return go
            segment("gate_a", 4, 4, from_act(False))
            segment("gate_b", 4, 4, from_act(False))

            e.wait_ge(S["o_lo"], 12)
            e.wait_ge(S["mix_lo"], 1)
            e.wait_ge(act_freed, freed("gate_b", 3))

            def project(b, k, i, u0, step):
                gemm(u0, 6, gated, 4 * k, False, i, step)
                gemm(u0 + 6, 2, gated, 4 * k + 2, False, i, step, kc0=12)
            segment("proj", 4, 4, project)

            e.wait_ge(S["c2_ready"], 1)
            segment("ada_gate", 4, 4, modulation)
            e.wait_ge(dve_freed, freed("ada_gate", 3))
            for q in range(4):
                ins = e.matmul(ps[:, 4 + q, :], tables[0:4, T_SELX:T_SELX + P],
                               gatedf[0:4, HI2 + q * 512:HI2 + (q + 1) * 512], start=True, stop=True)
            ins.then_inc(S["gate_turned"], 1)
            e.wait_ge(S["proj_lo"], 4)
            segment("out", 4, 4, from_act(True))

            def turn_x(norm, value, gap, low_done, done):
                for q in range(4):
                    e.wait_ge(norm, value + gap * q)
                    if q >= 2:
                        e.wait_ge(low_done, q - 1)
                    turn4(lambda c, tt: x[:, tt, c * P:(c + 1) * P], q, 4 + 2 * (q % 2)).then_inc(done, 1)
            e.wait_ge(S["gate_ready"], 1)
            turn_x(S["normed2"], 2, 2, S["x2_lo"], S["x2_turned"])

            e.wait_ge(S["x2_lo"], 4)
            e.wait_ge(S["rows_loaded"], 16 * 5)
            for kc in range(KD):
                for v in range(2):
                    ins = e.matmul(ps[0:64, 4, 0:256], side[:, kc * 64:(kc + 1) * 64], act[:, v, kc, :].bitcast(F32),
                                   start=kc == 0 and v == 0, stop=kc == KD - 1 and v == 1)
            ins.then_inc(S["dt_mm"], 1)
            e.wait_ge(S["dt_step"], 10)
            for n in range(4):
                o = (256, 384, 1536, 1664)[n]
                ins = e.transpose(ps[:, 5, n * 64:(n + 1) * 64], tx[0:64, o:o + P], ident[0:64, 0:64])
            ins.then_inc(S["dt_turned"], 1)
            segment("ssd_x", 4, 8, from_act(False))
            segment("ssd_bc", 4, 4, from_act(False))
            segment("ssd_z", 4, 8, from_act(True))

            ex = actf[:, 2048:5120]
            xst = actf[:, 5120:6144]
            bst = actf[:, 6144:6400]
            xtok = actf[:, 6400:7424]
            e.wait_ge(act_freed, freed("ssd_z", 7))

            def scan_turn(g):
                e.wait_ge(S["b_staged"], 2 * g + 1)
                e.wait_ge(S["cb_masked"], g)
                e.matmul(ps[:, 0, 0:256], bst[:, 0:P], side[:, ds(256 * g + 2048, 256)], start=True, stop=True)
                e.matmul(ps[:, 0, 256:384], bst[:, P:2 * P], side[:, ds(256 * g + 2048 + P, P)],
                         start=True, stop=True).then_inc(S["cb_ready"], 1)
                e.wait_ge(S["b_staged"], 2 * g + 2)
                e.wait_ge(S["xs_ready"], g)
                for fc in range(4):
                    for tt in range(2):
                        o = fc * 256 + tt * P
                        ins = e.transpose(ps[:, 1 + tt, fc * P:(fc + 1) * P], xst[:, o:o + P], ident)
                ins.then_inc(S["xs_turned"], 1)
                e.wait_ge(S["xdt_step"], 4 * g + 4)
                e.wait_ge(S["y_step"], 5 * g)
                for n in range(2):
                    e.wait_ge(S["m_ready"], 2 * g + n + 1)
                    for h in range(4 * n, 4 * n + 4):
                        cs = slice(h * HD, (h + 1) * HD)
                        m = ex[:, h * 384:(h + 1) * 384]
                        e.matmul(ps[:, 3, cs], m[:, 0:128], xtok[:, h * HD:(h + 1) * HD], start=True, stop=True)
                        e.matmul(ps[:, 4, cs], m[:, 128:256], xtok[:, h * HD:(h + 1) * HD], start=True, stop=False)
                        ins = e.matmul(ps[:, 4, cs], m[:, 256:384], xtok[:, 512 + h * HD:512 + (h + 1) * HD],
                                       start=False, stop=True)
                ins.then_inc(S["y_mm"], 1)
                e.wait_ge(S["y_ready"], 2 * g + 2)
                turn4(lambda c, tt: tx[:, tt * 512 + c * P:tt * 512 + (c + 1) * P], 0, 5).then_inc(S["y_turned"], 1)
            each(e, G, scan_turn)

            e.wait_ge(S["y_lo"], G)

            def from_gated(b, k, i, u0, step):
                gemm(u0, 16, gated, 2 * k, True, i, step)
            segment("ssd_out", 8, 4, from_gated)
            turn_x(S["ln_dve"], 15, 4, S["x3_lo"], S["x3_turned"])

            e.wait_ge(S["x3_lo"], 4)
            u0 = 2 * FIRST["lat_q"]
            pair_free(BI["lat_q"])
            gemm(u0, 8, act, 0, True)
            pair_free(BI["lat_kv"])
            gemm(u0 + 8, 8, act, 2, True, w=336)
            e.wait_ge(S["lat_normed"], 4)
            turn4(lambda c, tt: tx[:, tt * 512 + c * P:tt * 512 + (c + 1) * P], 0, 4)
            for c in range(2):
                for tt in range(2):
                    o = 1024 + tt * 336 + c * P
                    e.transpose(ps[:, 6, c * 256 + tt * P:c * 256 + (tt + 1) * P], tx[:, o:o + P], ident)
            e.wait_ge(S["lat_act"], 2)
            for tt in range(2):
                ins = e.transpose(ps[:, 7, tt * P:(tt + 1) * P], t1[:, tt * P:(tt + 1) * P], ident)
            ins.then_inc(S["lat_turned"], 1)
            e.wait_ge(S["lat_lo"], 2)
            for b in range(2):
                pair_free(BI["idx_q"] + b)
                gemm(u0 + 16 + 2 * b, 2, lat, 2 * b, False)
            e.wait_ge(S["idxk_ready"], 1)
            e.wait_ge(act_freed, freed("idx_q", 1))
            for h in range(16):
                r = slice(64 * (h % 2), 64 * (h % 2) + 64)
                qa = gatedf[r, (h // 2) * 256:(h // 2) * 256 + 256]
                if h >= 4:
                    e.wait_ge(S["idx_relu"], h - 3)
                bank = 4 + h % 4
                e.matmul(ps[:, bank, 0:128], qa[:, 0:P], gatedf[r, 2048:2176], start=True, stop=True)
                e.matmul(ps[:, bank, 128:384], qa[:, P:2 * P], gatedf[r, 2048:2304],
                         start=True, stop=True).then_inc(S["idx_scores"], 1)
            segment("lat_gate", 4, 8, from_act(False))

            e.wait_ge(act_freed, freed("lat_gate", 7))
            e.wait_ge(S["idx_relu"], 16)

            def heads_turn(i):
                for k in range(2):
                    gi = 2 * i + k
                    u0 = 2 * FIRST["head_q"] + 4 * k
                    w = actf[:, k * 3072:(k + 1) * 3072]
                    e.wait_ge(S["hv_read"], gi)
                    gemm(u0, 2, lat, 0, False, i, 8)
                    e.wait_ge(S["hk_read"], gi)
                    gemm(u0 + 2, 1, lat, 2, False, i, 8, kc0=4)
                    e.wait_ge(S["hq_read"], gi + 1)
                    gemm(u0 + 3, 1, lat, 0, True, i, 8, kc0=4)

                    def scores(h):
                        n = 4 * gi + h
                        if h == 0:
                            e.wait_ge(S["hk_read"], gi + 1)
                        e.wait_ge(S["hs_masked"], 4 * gi if h < 2 else n - 1)
                        e.matmul(ps[:, 4 + h % 2, 0:128], w[:, h * 256:h * 256 + P], w[:, 1024 + h * 256:1152 + h * 256],
                                 start=True, stop=True)
                        e.matmul(ps[:, 4 + h % 2, 128:384], w[:, h * 256 + P:h * 256 + 2 * P],
                                 w[:, 1024 + h * 256:1280 + h * 256], start=True, stop=True).then_inc(S["hs_mm"], 1)

                    def mix(h):
                        n = 4 * gi + h
                        p = actf[:, 6144 + (h % 2) * 384:6528 + (h % 2) * 384]
                        pt = actf[:, 6912 + (h % 2) * 384:7296 + (h % 2) * 384]
                        e.wait_ge(S["hs_probs"], n + 1)
                        e.wait_ge(S["hs_pt"], n)
                        for c in range(3):
                            ins = e.transpose(ps[:, 6, c * P:(c + 1) * P], p[:, c * P:(c + 1) * P], ident)
                        ins.then_inc(S["hs_turned"], 1)
                        e.wait_ge(S["hs_pt"], n + 1)
                        if h == 0:
                            e.wait_ge(S["hv_read"], gi + 1)
                        e.wait_ge(S["ho_gated"], 4 * gi if h < 2 else n - 1)
                        o = (h % 2) * 256
                        e.matmul(ps[:, 7, o:o + 256], w[:, 2048 + h * P:2048 + (h + 1) * P], pt[:, 0:256],
                                 start=True, stop=False, skip_group_check=True)
                        e.matmul(ps[:, 7, o + P:o + 256], w[:, 2560 + h * P:2560 + (h + 1) * P], pt[:, 256:384],
                                 start=False, stop=True, skip_group_check=True).then_inc(S["ho_mm"], 1)
                    scores(0)
                    for h in range(4):
                        if h < 3:
                            scores(h + 1)
                        mix(h)
            each(e, 4, heads_turn)

            e.wait_ge(S["ho_lo"], 32)
            e.wait_ge(S["hv_read"], 8)
            e.wait_ge(S["hk_read"], 8)
            for b in range(4):
                pair_free(BI["lat_out"] + b)
                gemm(2 * FIRST["lat_out"] + 16 * b, 16, gated, 2 * (b % 2), True)


_INS = ["x", "c", "ctx", "c_ctx", "w_ada", "b_ada", "norm_g", "w_in", "q_norm_g", "k_norm_g", "w_proj_a", "w_proj_b",
        "w_out", "final_g", "ssd_w_in_2", "ssd_conv_w_2", "ssd_conv_b_2", "ssd_dt_bias_2", "ssd_a_log_2",
        "ssd_d_skip_2", "ssd_norm_g_2", "ssd_w_out_2", "dsa_w_in_2", "dsa_q_norm_g_2", "dsa_kv_norm_g_2",
        "dsa_w_uq_2", "dsa_w_uk_2", "dsa_w_uv_2", "dsa_w_idx_q_2", "dsa_w_out_2", "ln_g_2", "ln_b_2"]


def kernel(**inputs):
    import concourse.bacc as bacc
    from concourse.bass_utils import run_bass_kernel_spmd

    nc = bacc.Bacc("TRN2", target_bir_lowering=False, num_devices=1)
    arrays, views = {}, {}
    for name in _INS:
        v = np.ascontiguousarray(inputs[name])
        if name not in ("c_ctx", "final_g", "ln_g_2", "ln_b_2"):
            v = v.reshape(v.shape[1:])
        arrays[f"in_{name}"] = v
    arrays["in_tables"] = make_tables()
    for name, v in arrays.items():
        views[name[3:]] = nc.dram_tensor(name, v.shape, F32, kind="ExternalInput").ap()
    out = nc.dram_tensor("out_dram", (L, D), F32, kind="ExternalOutput").ap()
    acs = nc.dram_tensor("acs_dram", (64, L), F32, kind="Internal").ap()
    build(nc, views, out, acs)
    r = run_bass_kernel_spmd(nc, [arrays], core_ids=[0])
    return r.results[0]["out_dram"].reshape(1, L, D)
```

```python
from contextlib import ExitStack

import numpy as np

import concourse.bass as bass
from concourse import mybir

F32 = mybir.dt.float32
F32R = mybir.dt.float32r
ALU = mybir.AluOpType
ACT = mybir.ActivationFunctionType
AX_X = mybir.AxisListType.X
ds = bass.ds

P = 128
L = 256
TT = L // P
D = 2048
KD = D // P
CB = 512
EPS = 1e-6
LN_EPS = 1e-5
ROPE_STEPS = 68

HQ, HKV, DH = 12, 4, 128
ATT_SCALE = DH ** -0.5
COL_Q, COL_K, COL_V, COL_ZA, COL_UB, COL_ZB, COL_GA, COL_GB = 0, 1536, 2048, 2560, 4096, 4608, 5120, 7168

G, R, HD, NS = 8, 8, 64, 128
SSD_IN = 10304
ALPHA = 4.0 ** 0.25

HL = 32
TOPK = 64
NEG = -1.0e30
UNSEEN = -3.0e38
TAKEN = -3.4e38

T_ID = 0
T_TRI = T_ID + 128
T_NEG = T_TRI + 384
T_UNSEEN = T_NEG + 128
T_SEL = T_UNSEEN + 128
T_SELX = T_SEL + 2
T_ROPE = T_SELX + 128
T_DFT = T_ROPE + 512
T_DFTC = T_DFT + 1024
T_W = T_DFTC + 256
T_TX = T_ROPE

V_BADA = 0
V_NORM = 48
V_SSDG = 64
V_QN = 96
V_KVN = 100
V_CB = 102
V_CW = 150
V_C = 342
V_W = 374

RAW = 4
SPLIT = 4

HI2 = 4096
LO = 8192
LO2 = 12288
SPARE = 14336


def make_tables():
    t = np.zeros((P, T_W), np.float32)
    i = np.arange(P)
    t[:, T_ID:T_ID + 128] = np.eye(P)
    tri = (i[:, None] <= i[None, :]).astype(np.float32)
    t[:, T_TRI:T_TRI + 384] = np.concatenate([tri, np.ones((P, P)), tri], 1)
    t[:, T_NEG:T_NEG + 128] = np.where(i[None, :] > i[:, None], NEG, 0.0)
    t[:, T_UNSEEN:T_UNSEEN + 128] = np.where(i[None, :] > i[:, None], UNSEEN, 0.0)
    for r in range(4):
        t[r, T_SEL + r % 2] = 1.0
    t[0, T_SELX:T_SELX + 128] = 1.0
    t[2, T_SELX:T_SELX + 128] = 1.0
    n = np.arange(L)
    inv = 10000.0 ** (-np.arange(32, dtype=np.float64) / 32)
    for a, pos in enumerate((n // 64, n % 64)):
        ang = pos[:, None] * inv[None, :]
        for tt in range(TT):
            c, s = np.cos(ang[tt * P:(tt + 1) * P]), np.sin(ang[tt * P:(tt + 1) * P])
            o = T_ROPE + tt * 128 + a * 64
            t[:, o:o + 32] = c
            t[:, o + 32:o + 64] = c
            o += 256
            t[:, o:o + 32] = -s
            t[:, o + 32:o + 64] = s
    th = 2 * np.pi * ((n[:, None] * n[None, :]) % L) / L
    for k in range(TT):
        o = T_DFT + k * 512
        t[:, o:o + 256] = np.cos(th[k * P:(k + 1) * P])
        t[:, o + 256:o + 512] = np.sin(th[k * P:(k + 1) * P])
    th = 2 * np.pi * ((i[:, None] * i[None, :]) % P) / P
    ortho = (L * P) ** -0.5
    t[:, T_DFTC:T_DFTC + 128] = np.cos(th) * ortho
    t[:, T_DFTC + 128:T_DFTC + 256] = -np.sin(th) * ortho
    return t


def tile_list():
    tiles = []

    def blocks(seg, n, per, dmas=1, width=CB):
        for b in range(n):
            for j in range(per):
                tiles.append((seg, b, j, dmas, width))

    blocks("ada", 8, 4)
    blocks("in", 10, 4)
    blocks("gate_a", 4, 4)
    blocks("gate_b", 4, 8)
    blocks("proj", 4, 4)
    blocks("out", 4, 4)
    blocks("ssd_x", 8, 4)
    blocks("ssd_bc", 4, 4)
    blocks("ssd_z", 8, 4)
    blocks("ssd_out", 32, 1)
    blocks("lat_q", 1, 4)
    blocks("lat_kv", 1, 4, 1, 336)
    blocks("lat_gate0", 2, 4)
    blocks("idx_q", 2, 1)
    blocks("lat_gate", 6, 4)
    for b in range(8):
        tiles.append(("head_q", b, 0, 1, CB))
        tiles.append(("head_kv", b, 0, 4, CB))
    blocks("lat_out", 4, 8)
    return tiles


def build(nc, a, out, acs_dram):
    TILES = tile_list()
    NU = 2 * len(TILES)
    FIRST = {}
    for n, t in enumerate(TILES):
        FIRST.setdefault(t[0], n)

    def landed(tile):
        return 16 * sum(TILES[t][3] for t in range(tile % RAW, tile + 1, RAW))

    def linear(f, n, step, i):
        if isinstance(i, int):
            return f(n + step * i)
        return f(n) + i * (f(n + step) - f(n))

    def width(unit):
        return TILES[unit // 2][4]

    BLOCKS = []
    for seg, _, _, _, _ in TILES:
        if seg not in ("head_q", "head_kv") and all(seg != s for s, _ in BLOCKS):
            nb = 1 + max(t[1] for t in TILES if t[0] == seg)
            for b in range(nb):
                scalar = seg in ("gate_a", "gate_b", "ssd_z", "lat_q", "lat_kv", "lat_gate0", "idx_q", "lat_gate") or (
                    seg == "in" and b in (1, 5, 6, 7, 8, 9))
                BLOCKS.append((seg, "act" if scalar else "dve"))
    BI = {}
    for n, (seg, _) in enumerate(BLOCKS):
        BI.setdefault(seg, n)

    def freed_count(engine, n):
        return sum(1 for _, who in BLOCKS[:n + 1] if who == engine)

    def freed(seg, b=0):
        n = BI[seg]
        if isinstance(b, int):
            return freed_count(BLOCKS[n + b][1], n + b)
        return freed_count(BLOCKS[n][1], n) + b

    def ready(seg, b=0):
        per = 2 * (1 + max(t[2] for t in TILES if t[0] == seg))
        return 2 * FIRST[seg] + per + per * b

    with ExitStack() as ctx:
        def sb(name, shape, dt=F32):
            return ctx.enter_context(nc.sbuf_tensor(name, shape, dt))

        def sem(name):
            return ctx.enter_context(nc.semaphore(name))

        base = (nc.sbuf_base + 31) // 32 * 32
        at = base
        raw = nc.alloc_sbuf_tensor_at("raw", [P, RAW, 4, CB], F32, offset=at)
        at += RAW * 4 * CB * 4
        w_hi = nc.alloc_sbuf_tensor_at("w_hi", [P, SPLIT, 2, CB], F32R, offset=at)
        at += SPLIT * 2 * CB * 4
        w_lo = nc.alloc_sbuf_tensor_at("w_lo", [P, SPLIT, 2, CB], F32R, offset=at)
        at += SPLIT * 2 * CB * 4
        act = nc.alloc_sbuf_tensor_at("act", [P, 2, KD, L], F32R, offset=at)
        actf = nc.alloc_sbuf_tensor_at("actf", [P, 2 * KD * L], F32, offset=at)
        at += 2 * KD * L * 4
        gated = nc.alloc_sbuf_tensor_at("gated", [P, 2, 32, L], F32R, offset=at)
        gatedf = nc.alloc_sbuf_tensor_at("gatedf", [P, 2 * 32 * L], F32, offset=at)
        at += 2 * 32 * L * 4
        x = nc.alloc_sbuf_tensor_at("x", [P, TT, D], F32, offset=at)
        at += TT * D * 4
        lat = nc.alloc_sbuf_tensor_at("lat", [P, 2, 6, L], F32R, offset=at)
        side = nc.alloc_sbuf_tensor_at("side", [P, 4096], F32, offset=at)
        at += 4096 * 4
        tables = nc.alloc_sbuf_tensor_at("tables", [P, T_W], F32, offset=at)
        at += (T_W * 4 + 31) // 32 * 32
        vec = nc.alloc_sbuf_tensor_at("vec", [P, V_W], F32, offset=at)
        at += (V_W * 4 + 31) // 32 * 32
        t0 = nc.alloc_sbuf_tensor_at("t0", [P, 512], F32, offset=at)
        at += 512 * 4
        t1 = nc.alloc_sbuf_tensor_at("t1", [P, 256], F32, offset=at)
        at += 256 * 4
        mod = nc.alloc_sbuf_tensor_at("mod", [P, 4, KD], F32, offset=at)
        at += 64 * 4
        sm = nc.alloc_sbuf_tensor_at("sm", [P, 96], F32, offset=at)
        at += 96 * 4
        arena = ctx.enter_context(nc.sbuf_tensor("arena", [P, (at - nc.sbuf_base) // 4], F32))
        ident = tables[:, T_ID:T_ID + 128]
        tx = tables[:, T_TX:T_TX + 1792]

        ps = ctx.enter_context(nc.psum_tensor("ps", [P, 8, 512], F32))

        raw_landed = [sem(f"raw_landed{s}") for s in range(RAW)]
        hi_done = sem("hi_done")
        lo_done = sem("lo_done")
        units_used = sem("units_used")
        act_freed = sem("act_freed")
        dve_freed = sem("dve_freed")

        def tile_source(seg, b, j):
            def rows(w, k0, c0, n=CB, chunks=4):
                return w[k0:k0 + chunks * P, :].rearrange("(c p) n -> p c n", p=P)[:, :, ds(c0, n)]

            k0 = j * 512
            if seg == "ada":
                return [(0, 4, rows(a["w_ada"], k0, b * CB))]
            if seg == "in":
                cols = [COL_K, COL_V, COL_Q, COL_Q + 512, COL_Q + 1024,
                        COL_ZA, COL_ZA + 512, COL_ZA + 1024, COL_ZB, COL_UB]
                return [(0, 4, rows(a["w_in"], k0, cols[b]))]
            if seg == "gate_a":
                return [(0, 4, rows(a["w_in"], k0, b * CB + COL_GA))]
            if seg == "gate_b" and j % 2:
                return [(0, 4, rows(a["w_ada"], j // 2 * 512, b * CB + 2 * D))]
            if seg == "gate_b":
                return [(0, 4, rows(a["w_in"], j // 2 * 512, b * CB + COL_GB))]
            if seg == "proj":
                if j < 3:
                    return [(0, 4, rows(a["w_proj_a"], k0, b * CB))]
                return [(0, 4, rows(a["w_proj_b"], 0, b * CB))]
            if seg == "out":
                return [(0, 4, rows(a["w_out"], k0, b * CB))]
            if seg == "ssd_x":
                return [(0, 4, rows(a["ssd_w_in_2"], k0, b * CB + 4096))]
            if seg == "ssd_bc":
                return [(0, 4, rows(a["ssd_w_in_2"], k0, b * CB + 8192))]
            if seg == "ssd_z":
                return [(0, 4, rows(a["ssd_w_in_2"], k0, b * CB))]
            if seg == "lat_q":
                return [(0, 4, rows(a["dsa_w_in_2"], k0, 0))]
            if seg == "lat_kv":
                return [(0, 4, rows(a["dsa_w_in_2"], k0, 512, 336))]
            if seg == "idx_q":
                return [(0, 4, rows(a["dsa_w_idx_q_2"], 0, b * CB))]
            if seg == "lat_gate0":
                return [(0, 4, rows(a["dsa_w_in_2"], k0, b * CB + 848))]
            if seg == "lat_gate":
                return [(0, 4, rows(a["dsa_w_in_2"], k0, b * CB + 848 + 2 * CB))]
            if seg == "head_q":
                return [(0, 4, rows(a["dsa_w_uq_2"], 0, b * CB))]
            if seg == "head_kv":
                got = []
                for n, w in enumerate((a["dsa_w_uk_2"], a["dsa_w_uv_2"])):
                    for c in range(2):
                        got.append((2 * n + c, 1, w[ds(b * 4, 4), c * P:(c + 1) * P, :].rearrange("h p d -> p h d")))
                return got
            return [(0, 4, rows(a["dsa_w_out_2"], k0, b * CB))]

        def each(engine, turns, body):
            body(0)
            if turns > 1:
                with engine.Fori(1, turns) as i:
                    body(i)

        def last_apart(engine, seg, turns, body):
            after = max(n for n, t in enumerate(TILES) if t[0] == seg) + 1
            if any(t[3] != 1 for t in TILES[after:after + 2]):
                each(engine, turns - 1, body)
                body(turns - 1)
            else:
                each(engine, turns, body)

        names = """small_loaded rows_in h_copied vec_turned vec_ready silu_c c_hi c_ready c_zero squares1 mean1 root1
            rstd1 xn_ready mod_turned mod_ready mod_step h_turned h_affine h_hi h_lo sq_ready
            ss_ready root_ready rope_step q_staged v_staged k_turned kt_ready dft1 dft1_out dft2
            mix_ready mix_hi mix_lo qt_turned qt_ready scores_ready max_step max_ready exp_ready
            sum_inv probs_ready probs_turned pt_ready o_ready o_gated o_hi o_lo proj_read proj_sum
            proj_hi proj_lo gate_turned gate_ready bias_loaded final_loaded rows_read rows_loaded
            out_read out_step sq2 mean2 root2 rstd2 scaled2 normed2 x2_turned x2_hi x2_lo dt_mm
            dt_step dt_act acs_stored dt_turned dt_ready conv_step conv_done conv_silu r_loaded
            b_staged cb_ready xt_turned xt_copied x_scaled acs_staged g_staged cb_masked xdt_step
            diff_ready decay_ready m_ready y_mm y_step y_act y_ready y_turned y_hi y_lo ln_rows
            ln_stats ln_act ln_rstd ln_dve x3_turned x3_hi x3_lo lat_sq lat_mean lat_root lat_rstd
            lat_act lat_normed lat_turned lat_scaled lat_hi lat_lo idxk_ready idx_scores idx_relu
            idx_step idx_done hq_read hk_read hv_read hs_mm hs_masked hs_step hs_max hs_exp hs_inv
            hs_probs hs_turned hs_pt ho_mm ho_gated ho_hi ho_lo fin_rows fin_stats fin_act fin_rstd
            fin_dve stored half_read""".split()
        S = {n: sem(n) for n in names}

        block = ctx.enter_context(nc.Block())

        @block.sync
        def _(sp):
            def load(n, b, i=0, step=0):
                seg, _, j, _, w = TILES[n]
                if n >= RAW or not isinstance(i, int):
                    sp.wait_ge(lo_done, 2 * (n - RAW) + 2 + 2 * step * i)
                for c0, c, src in tile_source(seg, b, j):
                    sp.dma_start(raw[:, n % RAW, c0:c0 + c, :w], src).then_inc(raw_landed[n % RAW], 16)

            def segment(seg, per, nblocks):
                n0 = FIRST[seg]

                def two(i):
                    for k in range(2):
                        for j in range(per):
                            load(n0 + k * per + j, 2 * i + k, i, 2 * per)
                each(sp, nblocks // 2, two)

            segment("ada", 4, 8)
            for n in range(FIRST["in"], FIRST["gate_a"]):
                load(n, TILES[n][1])
            segment("gate_a", 4, 4)
            segment("gate_b", 8, 4)
            segment("proj", 4, 4)
            segment("out", 4, 4)
            segment("ssd_x", 4, 8)
            segment("ssd_bc", 4, 4)
            segment("ssd_z", 4, 8)

            def out_group(g):
                w = a["ssd_w_out_2"].rearrange("(g c p) n -> p g c n", p=P, c=4)
                for t in range(4):
                    n = FIRST["ssd_out"] + t
                    sp.wait_ge(lo_done, 2 * (n - RAW) + 2 + 8 * g)
                    sp.dma_start(raw[:, n % RAW:n % RAW + 1, :, :],
                                 w[:, ds(g, 1), :, t * CB:(t + 1) * CB]).then_inc(raw_landed[n % RAW], 16)
            each(sp, G, out_group)
            for n in range(FIRST["lat_q"], FIRST["lat_gate"]):
                load(n, TILES[n][1])
            segment("lat_gate", 4, 6)

            def heads(i):
                for k in range(2):
                    for j in range(2):
                        load(FIRST["head_q"] + 2 * k + j, 2 * i + k, i, 4)
            each(sp, 4, heads)
            segment("lat_out", 8, 4)

        @block.scalar
        def _(e):
            def split(u, i=0, step=0):
                t, h = u // 2, u % 2
                w = width(u)
                if h == 0:
                    e.wait_ge(raw_landed[t % RAW], linear(landed, t, step // 2, i))
                if u >= SPLIT:
                    e.wait_ge(units_used, linear(lambda v: v - SPLIT + 1, u, step, i))
                e.activation(w_hi[:, u % SPLIT, :, :w], raw[:, t % RAW, 2 * h:2 * h + 2, :w],
                             ACT.Copy).then_inc(hi_done, 1)

            def splits(u0, n, i=0, step=0):
                for u in range(u0, u0 + n):
                    if u < NU:
                        split(u, i, step)

            def fixed():
                e.wait_ge(S["small_loaded"], 16 * 13)

            def segment(seg, per, nblocks, epilogue):
                u0 = 2 * FIRST[seg]

                def two(i):
                    for k in range(2):
                        splits(u0 + (k * per * 2) + 4, 2 * per, i, 4 * per)
                        epilogue(2 * i + k, k)
                last_apart(e, seg, nblocks // 2, two)

            def root(out_, in_, ready, value, done):
                e.wait_ge(ready, value)
                e.activation(out_, in_, ACT.Sqrt).then_inc(done, 1)

            vr = side
            n = 0
            def small(dst, src):
                e.dma_start(dst, src).then_inc(S["small_loaded"], 16)
            small(tables[:, 0:P], a["tables"][:, 0:P])
            row = lambda v: v.rearrange("(c p) -> c p", p=P)
            small(t0[0:48, 0:128], row(a["b_ada"]))
            small(t0[48:64, 0:128], row(a["norm_g"]))
            small(t0[64:96, 0:128], row(a["ssd_norm_g_2"]))
            small(t0[96:100, 0:128], row(a["dsa_q_norm_g_2"]))
            small(t0[100:102, 0:128], row(a["dsa_kv_norm_g_2"]))
            small(t0[0:48, 128:256], row(a["ssd_conv_b_2"]))
            small(t0[48:96, 128:256], row(a["ssd_conv_w_2"][0, :]))
            small(t0[0:48, 256:384], row(a["ssd_conv_w_2"][1, :]))
            small(t0[48:96, 256:384], row(a["ssd_conv_w_2"][2, :]))
            small(t0[0:48, 384:512], row(a["ssd_conv_w_2"][3, :]))
            small(t0[48:64, 384:512], row(a["c"]))
            small(t0[64:80, 384:512], row(a["c_ctx"]))
            def rows_in(dst, src):
                e.dma_start(dst, src).then_inc(S["rows_in"], 16)
            rows_in(x[:, :, :], a["x"].rearrange("(t p) d -> p t d", p=P))
            rows_in(side[:, :].rearrange("p (t d) -> p t d", t=TT), a["ctx"].rearrange("(t p) d -> p t d", p=P))
            rows_in(t1[:, 0:128], a["q_norm_g"].partition_broadcast(P))
            rows_in(t1[:, 128:256], a["k_norm_g"].partition_broadcast(P))
            rows_in(tables[:, P:T_W], a["tables"][:, P:T_W])

            cols = gated[:, 1, 16:24, :].rearrange("p a b -> p (a b)").rearrange("p (k m) -> p k m", m=P)
            cols2 = lat.rearrange("p a b c -> p (a b c)")[:, 0:D].rearrange("p (k m) -> p k m", m=P)

            def c_columns(cols, time):
                e.activation(sm[:, 0:32], vec[:, V_C:V_C + 32], ACT.Silu).then_inc(S["silu_c"], 1)
                e.wait_ge(S["silu_c"], time)
                e.activation(cols[:, :, 0:2], sm[:, 0:32].rearrange("p (j k) -> p k j", j=2),
                             ACT.Copy).then_inc(S["c_hi"], 1)

            e.wait_ge(S["vec_ready"], 1)
            e.wait_ge(S["c_zero"], 1)
            c_columns(cols, 1)
            splits(0, 4)
            e.wait_ge(S["rows_in"], 16 * 5)
            for n in range(4):
                splits(4 + 4 * n, 4)
                src = x[:, n, :] if n < 2 else side[:, (n - 2) * D:(n - 1) * D]
                e.activation(gatedf[:, n * D:(n + 1) * D], src, ACT.Square,
                             accum_out=sm[:, 32 + n:33 + n]).then_inc(S["squares1"], 1)
            root(sm[:, 40:44], sm[:, 36:40], S["mean1"], 1, S["root1"])
            splits(20, 2)
            e.wait_ge(S["rstd1"], 1)
            e.wait_ge(S["squares1"], 4)
            for n in range(4):
                src = x[:, n, :] if n < 2 else side[:, (n - 2) * D:(n - 1) * D]
                dst = gatedf[:, n * D:(n + 1) * D] if n < 2 else src
                e.activation(dst, src, ACT.Copy, scale=sm[:, 44 + n:45 + n]).then_inc(S["xn_ready"], 1)
                splits(22 + 4 * n, 4 if n < 3 else 2)
            for n in range(8):
                splits(36 + 4 * n, 4)
                o = (LO if n < 4 else HI2) + (n % 4) * 1024
                b = 4 + 2 * (n % 2)
                e.wait_ge(S["h_turned"], n + 1)
                e.activation(gatedf[:, o:o + 1024].rearrange("p (b c) -> p b c", b=2), ps[:, b:b + 2, :],
                             ACT.Copy).then_inc(S["h_copied"], 1)
            for n in range(8):
                r, q = (gated if n % 2 else act), n // 2
                o = SPARE + (n % 2) * 1024
                e.wait_ge(S["h_affine"], 4 * n + 4)
                e.activation(r[:, 0, 4 * q:4 * q + 4, :], gatedf[:, o:o + 1024].rearrange("p (c t) -> p c t", c=4),
                             ACT.Copy).then_inc(S["h_hi"], 1)

            u0 = 2 * FIRST["in"]
            nrope = 0
            for b in range(6):
                early = 2 if b in (3, 4, 5) else 0
                splits(u0 + 8 * b + 4 + early, 8 - early)
                e.wait_ge(units_used, ready("in", b))
                if b in (0, 2, 3, 4):
                    for tt in range(4 if b == 0 else 2):
                        bank = tt if b == 0 else (0 if b % 2 == 0 else 2) + tt
                        if nrope >= 2:
                            e.wait_ge(S["ss_ready"], nrope - 1)
                        e.activation(side[:, (nrope % 2) * 512:(nrope % 2) * 512 + 512], ps[:, bank, :],
                                     ACT.Square).then_inc(S["sq_ready"], 1)
                        nrope += 1
                        root(sm[:, 52:56], sm[:, 48:52], S["ss_ready"], nrope, S["root_ready"])
                        if b > 0 and tt == 0:
                            splits(u0 + 8 * b + 12, 2)
                elif b == 1:
                    for tt in range(4):
                        e.activation(gatedf[:, LO2 + 2048 + tt * 512:LO2 + 2560 + tt * 512], ps[:, 4 + tt, :],
                                     ACT.Copy).then_inc(act_freed if tt == 3 else S["half_read"], 1)
                else:
                    for n in range(2):
                        e.activation(gatedf[:, LO + n * 512:LO + (n + 1) * 512], ps[:, 2 + n, :], ACT.Silu).then_inc(
                            act_freed if n == 1 else S["half_read"], 1)

            for kv in range(HKV):
                e.wait_ge(S["k_turned"], kv + 1)
                e.activation(side[:, kv * 512:(kv + 1) * 512], ps[:, 4 + kv, :], ACT.Copy).then_inc(S["kt_ready"], 1)

            probs = gatedf[:, LO2:LO2 + 1024]
            pt = gatedf[:, LO2 + 1024:LO2 + 2048]
            qt = side[:, 3328:4096]

            def kv_turn(kv):
                def ahead(m):
                    if isinstance(kv, int):
                        split(u0 + 48 + 8 * kv + m)
                    else:
                        split(u0 + 48 + m, kv, 8)

                def exps(j):
                    e.wait_ge(S["max_ready"], 3 * kv + j + 1)
                    e.wait_ge(S["probs_turned"], 3 * kv + j)
                    for tt in range(2):
                        e.activation(probs[:, tt * 512:(tt + 1) * 512], ps[:, 4 + tt, :], ACT.Exp,
                                     bias=sm[:, 58 + tt:59 + tt], scale=ATT_SCALE,
                                     accum_out=sm[:, 60 + tt:61 + tt]).then_inc(S["exp_ready"], 1)

                def turn(j):
                    e.wait_ge(S["probs_turned"], 3 * kv + j + 1)
                    e.activation(pt.rearrange("p (b c) -> p b c", b=2), ps[:, 6:8, :], ACT.Copy).then_inc(S["pt_ready"], 1)

                def high(j):
                    e.wait_ge(S["o_gated"], 3 * kv + j + 1)
                    fixed()
                    e.activation(gated[:, 0, ds(3 * kv + j, 1), :],
                                 t0[:, (j % 2) * 256:(j % 2) * 256 + 256].unsqueeze(1), ACT.Copy).then_inc(S["o_hi"], 1)

                e.wait_ge(S["qt_turned"], kv + 1)
                e.activation(qt[:, 0:512], ps[:, 3, :], ACT.Copy).then_inc(S["qt_ready"], 1)
                e.activation(qt[:, 512:768], ps[:, 2, 0:256], ACT.Copy).then_inc(S["qt_ready"], 1)
                ahead(4)
                exps(0)
                ahead(5)
                turn(0)
                exps(1)
                ahead(6)
                high(0)
                ahead(7)
                turn(1)
                exps(2)
                ahead(8)
                high(1)
                ahead(9)
                turn(2)
                ahead(10)
                ahead(11)
                e.wait_ge(units_used, ready("in", 6) + 8 * kv)
                for n in range(2):
                    done = act_freed if n == 1 else S["half_read"]
                    if isinstance(kv, int) and kv == 3:
                        e.activation(gatedf[:, HI2 + 3072 + n * 512:HI2 + 3584 + n * 512], ps[:, n, :],
                                     ACT.Copy).then_inc(done, 1)
                    else:
                        fixed()
                        e.activation(gatedf[:, ds(1024 * kv + LO + 1024 + n * 512, 512)], ps[:, n, :],
                                     ACT.Silu).then_inc(done, 1)
                high(2)
            each(e, HKV - 1, kv_turn)
            kv_turn(3)
            for g in range(4):
                e.wait_ge(S["dft1"], g + 1)
                e.activation(side[:, 2048 + g * 512:2560 + g * 512], ps[:, 4 + g, :], ACT.Copy).then_inc(S["dft1_out"], 1)
            e.wait_ge(S["mix_ready"], 1)
            e.activation(gated[:, 0, 12:16, :], side[:, 2048:3072].rearrange("p (c t) -> p c t", c=4),
                         ACT.Copy).then_inc(S["mix_hi"], 1)

            e.wait_ge(S["c_zero"], 2)
            c_columns(cols2, 2)
            for seg, o, after in (("gate_a", HI2, 0), ("gate_b", LO2, 2)):
                def sig(b, k, seg=seg, o=o, after=after):
                    e.wait_ge(units_used, ready(seg, b) - after)
                    for n in range(2):
                        fixed()
                        e.activation(gatedf[:, ds(o + n * 512 + 1024 * b, 512)], ps[:, 2 * k + n, :],
                                     ACT.Sigmoid).then_inc(act_freed if n == 1 else S["half_read"], 1)
                segment(seg, 8 if after else 4, 4, sig)

            def proj(b, k):
                e.wait_ge(S["proj_sum"], b + 1)
                fixed()
                e.activation(act[:, 0, ds(4 * b, 4), :],
                             side[:, 1024:2048].rearrange("p (c t) -> p c t", c=4),
                             ACT.Copy).then_inc(S["proj_hi"], 1)
            segment("proj", 4, 4, proj)


            def out_squares(b, k):
                for n in range(2):
                    e.wait_ge(S["out_step"], 2 * b + n + 1)
                    e.activation(gatedf[:, (2 * b + n) * 512:(2 * b + n + 1) * 512], x[:, n, b * 512:(b + 1) * 512],
                                 ACT.Square, accum_out=sm[:, 72 + 4 * n + b:73 + 4 * n + b]).then_inc(S["sq2"], 1)
            segment("out", 4, 4, out_squares)
            root(sm[:, 40:42], sm[:, 36:38], S["mean2"], 1, S["root2"])
            e.wait_ge(S["rstd2"], 1)
            for q in range(4):
                for n in range(2):
                    piece = x[:, n, q * 512:(q + 1) * 512]
                    e.activation(piece, piece, ACT.Copy, scale=sm[:, 44 + n:45 + n]).then_inc(S["scaled2"], 1)

            def high_x(turned, done):
                for q in range(4):
                    e.wait_ge(turned, q + 1)
                    b = 4 + 2 * (q % 2)
                    e.activation(act[:, 0, 4 * q:4 * q + 4, :], ps[:, b:b + 2, :].rearrange("p b (c t) -> p (b c) t", c=2),
                                 ACT.Copy).then_inc(done, 1)
            high_x(S["x2_turned"], S["x2_hi"])

            def conv_silu(dst, nb, b):
                for n in range(2):
                    if n == 0:
                        e.wait_ge(S["conv_done"], b + nb + 1)
                    else:
                        e.wait_ge(dve_freed, freed("ssd_x") + nb + b)
                    fixed()
                    e.activation(dst[:, n * 512:(n + 1) * 512], tx[:, n * 512:(n + 1) * 512],
                                 ACT.Silu).then_inc(S["conv_silu"], 1)

            def x_tokens(b, k):
                e.wait_ge(S["xt_turned"], b + 1)
                fixed()
                e.activation(gatedf[:, ds(1024 * b, 1024)].rearrange("p (b c) -> p b c", b=2),
                             ps[:, 4 + 2 * k:6 + 2 * k, :], ACT.Copy).then_inc(S["xt_copied"], 1)

            def conv_x(i):
                for k in range(2):
                    b = 2 * i + k
                    ahead = 2 * FIRST["ssd_x"] + 8 * k + 4
                    splits(ahead, 4, i, 16)
                    if k or not isinstance(i, int):
                        x_tokens(b - 1, (k + 1) % 2)
                    splits(ahead + 4, 4, i, 16)
                    conv_silu(gatedf[:, LO + k * 1024:LO + (k + 1) * 1024], 0, b)
            each(e, 4, conv_x)

            def conv_bc(i):
                for k in range(2):
                    b = 2 * i + k
                    ahead = 2 * FIRST["ssd_bc"] + 8 * k + 4
                    splits(ahead, 4, i, 16)
                    if k == 0 and isinstance(i, int) and i == 0:
                        x_tokens(7, 1)
                    splits(ahead + 4, 4, i, 16)
                    conv_silu(side[:, ds(b * 1024, 1024)], 8, b)
            each(e, 2, conv_bc)

            def dt_splits(u0):
                e.wait_ge(S["rows_loaded"], 16 * 5)
                e.wait_ge(S["conv_silu"], 24)
                e.wait_ge(S["dt_mm"], 1)
                e.activation(tx[0:64, 0:256], ps[0:64, 4, 0:256], ACT.Identity, bias=sm[0:64, 65:66]).then_inc(S["dt_act"], 1)
                e.activation(sm[0:64, 66:67], sm[0:64, 64:65], ACT.Exp).then_inc(S["dt_act"], 1)
                splits(u0, 1)
                e.wait_ge(S["dt_step"], 1)
                e.activation(tx[0:64, 512:768], tx[0:64, 256:512], ACT.Exp, scale=-1.0).then_inc(S["dt_act"], 1)
                splits(u0 + 1, 1)
                e.wait_ge(S["dt_step"], 2)
                e.activation(tx[0:64, 1024:1280], tx[0:64, 768:1024], ACT.Ln).then_inc(S["dt_act"], 1)
                splits(u0 + 2, 6)

            def z_two(i):
                for k in range(2):
                    ahead = 2 * FIRST["ssd_z"] + 8 * k + 4
                    if k == 0 and isinstance(i, int):
                        dt_splits(ahead)
                    elif isinstance(i, int):
                        splits(ahead, 4)
                        e.activation(x[:, :, :], x[:, :, :], ACT.Copy, scale=ALPHA).then_inc(S["x_scaled"], 1)
                        splits(ahead + 4, 4)
                    else:
                        splits(ahead, 8, i, 16)
                    b = 2 * i + k
                    e.wait_ge(units_used, ready("ssd_z", b))
                    for n in range(2):
                        fixed()
                        e.activation(gatedf[:, ds(b * 1024 + LO + n * 512, 512)], ps[:, 2 * k + n, :],
                                     ACT.Silu).then_inc(act_freed if n == 1 else S["half_read"], 1)
            each(e, 4, z_two)

            ex = actf[:, 1024:4096]
            rb = actf[:, 5120:7168]
            U0 = 2 * FIRST["ssd_out"]
            e.wait_ge(units_used, ready("ssd_z", 7))

            def decay(g, n):
                if n == 0:
                    e.wait_ge(S["r_loaded"], 16 * g + 16)
                    e.wait_ge(S["acs_staged"], g + 1)
                    e.wait_ge(S["y_mm"], g)
                for h in range(4 * n, 4 * n + 4):
                    for tt in range(2):
                        o = h * 384 + tt * 256
                        w = 256 - tt * 128
                        ins = e.activation(ex[:, o:o + w], rb[:, h * 256 + tt * 128:h * 256 + 256], ACT.Relu,
                                           scale=-1.0, bias=sm[:, 76 + tt * 8 + h:77 + tt * 8 + h])
                ins.then_inc(S["diff_ready"], 1)
                e.wait_ge(S["diff_ready"], 2 * g + n + 1)
                part = ex[:, n * 1536:(n + 1) * 1536]
                e.activation(part, part, ACT.Exp, scale=-1.0).then_inc(S["decay_ready"], 1)

            def scan_turn(g):
                def ahead(m):
                    if not isinstance(g, int) or g > 0:
                        split(U0 - 8 + m, g, 8)

                decay(g, 1)
                for m in range(4, 8):
                    ahead(m)
                e.wait_ge(S["y_step"], 4 * g + 2)
                for n in range(2):
                    if n == 1:
                        e.wait_ge(S["y_act"], 3 * g + 1)
                    e.activation(ps[:, 7, :], tx[:, n * 512:(n + 1) * 512], ACT.Square,
                                 accum_out=sm[:, 32 + n:33 + n]).then_inc(S["y_act"], 1)
                ahead(8)
                e.wait_ge(S["y_step"], 4 * g + 3)
                e.activation(sm[:, 40:42], sm[:, 36:38], ACT.Sqrt).then_inc(S["y_act"], 1)
                e.wait_ge(S["y_step"], 4 * g + 4)
                for n in range(2):
                    part = tx[:, n * 512:(n + 1) * 512]
                    e.activation(part, part, ACT.Copy, scale=sm[:, 44 + n:45 + n]).then_inc(S["y_ready"], 1)
                ahead(9)
                e.wait_ge(S["g_staged"], g + 1)
                for c in range(4):
                    if c % 2 == 0:
                        e.wait_ge(S["y_turned"], 2 * g + 1 + c // 2)
                    e.activation(act[:, 0, c, :], ps[:, 5 + c // 2, (c % 2) * 256:(c % 2) * 256 + 256], ACT.Copy,
                                 scale=sm[:, 72 + c:73 + c]).then_inc(S["y_hi"], 1)
                ahead(10)
                ahead(11)
                if not isinstance(g, int) or g < G - 1:
                    decay(g + 1, 0)
            decay(0, 0)
            each(e, G - 1, scan_turn)
            scan_turn(G - 1)
            splits(U0 + 60, 8)

            def layer_norm(stats, act_sem, rstd):
                e.wait_ge(stats, 1)
                e.activation(sm[:, 40:42], sm[:, 38:40], ACT.Sqrt).then_inc(act_sem, 1)
                e.wait_ge(rstd, 1)
                for q in range(4):
                    for n in range(2):
                        piece = x[:, n, q * 512:(q + 1) * 512]
                        e.activation(piece, piece, ACT.Identity, scale=sm[:, 44 + n:45 + n],
                                     bias=sm[:, 46 + n:47 + n]).then_inc(act_sem, 1)
            layer_norm(S["ln_stats"], S["ln_act"], S["ln_rstd"])
            high_x(S["x3_turned"], S["x3_hi"])

            u0 = 2 * FIRST["lat_q"]
            splits(u0 + 4, 8)
            e.wait_ge(units_used, ready("lat_q"))
            for n in range(2):
                e.activation(tx[:, n * 512:(n + 1) * 512], ps[:, n, :], ACT.Copy).then_inc(act_freed if n == 1 else S["half_read"], 1)
            splits(u0 + 12, 8)
            e.wait_ge(units_used, ready("lat_kv"))
            for n in range(2):
                e.activation(tx[:, 1024 + n * 336:1360 + n * 336], ps[:, 2 + n, 0:336], ACT.Copy).then_inc(act_freed if n == 1 else S["half_read"], 1)
            e.wait_ge(act_freed, freed("lat_kv"))
            lats = [tx[:, 0:512], tx[:, 512:1024], tx[:, 1024:1280], tx[:, 1360:1616]]
            for n, v in enumerate(lats):
                if n:
                    e.wait_ge(S["lat_sq"], n)
                e.activation(t0[:, 0:512 if n < 2 else 256], v, ACT.Square, accum_out=sm[:, 32 + n:33 + n]).then_inc(S["lat_sq"], 1)
            def gate_silu(seg, first):
                def go(b, k):
                    e.wait_ge(units_used, ready(seg, b))
                    for n in range(2):
                        fixed()
                        e.activation(gatedf[:, ds(b * 1024 + first * 1024 + LO + n * 512, 512)], ps[:, 2 * k + n, :],
                                     ACT.Silu).then_inc(act_freed if n == 1 else S["half_read"], 1)
                return go
            u0 = 2 * FIRST["lat_gate0"]
            splits(u0 + 4, 2)
            root(sm[:, 40:44], sm[:, 36:40], S["lat_mean"], 2, S["lat_root"])
            e.wait_ge(S["lat_rstd"], 1)
            for n, v in enumerate(lats):
                e.activation(v, v, ACT.Copy, scale=sm[:, 44 + n:45 + n]).then_inc(S["lat_normed"], 1)
            splits(u0 + 6, 2)
            kidx = gatedf[:, 2048:2304]
            e.wait_ge(S["lat_turned"], 1)
            e.activation(kidx, ps[:, 7, 0:256], ACT.Copy).then_inc(S["idxk_ready"], 1)
            splits(u0 + 8, 2)
            e.wait_ge(S["lat_scaled"], 6)
            for c, n, v in ((0, 4, tx[:, 0:1024]), (4, 2, t0[:, 0:512])):
                e.activation(lat[:, 0, c:c + n, :], v.rearrange("p (c t) -> p c t", c=n), ACT.Copy).then_inc(S["lat_hi"], 1)
            splits(u0 + 10, 2)
            gate_silu("lat_gate0", 0)(0, 0)
            splits(u0 + 12, 8)
            gate_silu("lat_gate0", 0)(1, 1)
            for n in range(2):
                e.wait_ge(units_used, ready("idx_q", n))
                e.activation(gatedf[:, n * 1024:(n + 1) * 1024].rearrange("p (b c) -> p b c", b=2),
                             ps[:, 2 * n:2 * n + 2, :], ACT.Copy).then_inc(act_freed, 1)
            splits(2 * FIRST["lat_gate"], 4)
            for h in range(16):
                e.wait_ge(S["idx_scores"], h + 1)
                if h >= 2:
                    e.wait_ge(S["idx_step"], 2 * (h - 1))
                o = 2304 + (h % 2) * 384
                e.activation(gatedf[:, o:o + 384], ps[:, 4 + h % 4, 0:384], ACT.Relu, scale=1.0 / 32).then_inc(S["idx_relu"], 1)

            segment("lat_gate", 4, 6, gate_silu("lat_gate", 2))

            def heads_turn(t, k, ahead, i, softmax=True, project=True):
                def soft(h, here=softmax, of=t - 1):
                    if here:
                        n = 4 * of + h
                        p = actf[:, 6144 + (h % 2) * 384:6528 + (h % 2) * 384]
                        c = 72 + 8 * (h % 2)
                        e.wait_ge(S["hs_max"], n + 1)
                        for tt, v in enumerate((p[:, 0:128], p[:, 128:384])):
                            e.activation(v, v, ACT.Exp, bias=sm[:, c + 2 + tt:c + 3 + tt], scale=ATT_SCALE,
                                         accum_out=sm[:, c + 4 + tt:c + 5 + tt]).then_inc(S["hs_exp"], 1)

                def turn(h):
                    if softmax:
                        e.wait_ge(S["hs_turned"], 4 * (t - 1) + h + 1)
                        e.activation(actf[:, 6912 + (h % 2) * 384:7296 + (h % 2) * 384], ps[:, 6, 0:384],
                                     ACT.Copy).then_inc(S["hs_pt"], 1)

                def high(h):
                    if softmax:
                        n = 4 * (t - 1) + h
                        e.wait_ge(S["ho_gated"], n + 1)
                        fixed()
                        o = 7680 + (h % 2) * 256
                        e.activation(gated[:, 0, ds(n, 1), :], actf[:, o:o + 256].unsqueeze(1),
                                     ACT.Copy).then_inc(S["ho_hi"], 1)

                def read(part, bank, name):
                    if project:
                        w = actf[:, k * 3072 + part * 1024:k * 3072 + (part + 1) * 1024]
                        e.wait_ge(units_used, 2 * FIRST["head_q"] + 2 + part + 4 * t)
                        e.activation(w.rearrange("p (b c) -> p b c", b=2), ps[:, bank:bank + 2, :],
                                     ACT.Copy).then_inc(S[name], 1)
                soft(1)
                turn(0)
                splits(ahead, 1, i, 8)
                soft(2)
                splits(ahead + 1, 1, i, 8)
                turn(1)
                read(0, 0, "hq_read")
                high(0)
                soft(3)
                turn(2)
                splits(ahead + 2, 1, i, 8)
                high(1)
                read(1, 2, "hk_read")
                splits(ahead + 3, 1, i, 8)
                turn(3)
                read(2, 0, "hv_read")
                high(2)
                soft(0, project, t)
                high(3)

            HEAD = 2 * FIRST["head_q"] + 4
            heads_turn(0, 0, HEAD, 0, softmax=False)
            heads_turn(1, 1, HEAD + 4, 0)
            with e.Fori(1, 3) as i:
                for k in range(2):
                    heads_turn(2 * i + k, k, HEAD + 4 * k, i)
            heads_turn(6, 0, HEAD + 24, 0)
            heads_turn(7, 1, HEAD + 28, 0)
            heads_turn(8, 0, HEAD + 32, 0, project=False)

            splits(2 * FIRST["lat_out"] + 8, 56)
            layer_norm(S["fin_stats"], S["fin_act"], S["fin_rstd"])

        @block.vector
        def _(e):
            def split(u, i=0, step=0):
                t, h = u // 2, u % 2
                w = width(u)
                e.wait_ge(hi_done, linear(lambda v: v + 1, u, step, i))
                e.tensor_tensor(w_lo[:, u % SPLIT, :, :w], raw[:, t % RAW, 2 * h:2 * h + 2, :w],
                                w_hi[:, u % SPLIT, :, :w].bitcast(F32), ALU.subtract).then_inc(lo_done, 1)

            def splits(u0, n, i=0, step=0):
                for u in range(u0, u0 + n):
                    if u < NU:
                        split(u, i, step)

            def segment(seg, per, nblocks, epilogue):
                u0 = 2 * FIRST[seg]

                def two(i):
                    for k in range(2):
                        splits(u0 + (k * per * 2) + 4, 2 * per, i, 4 * per)
                        epilogue(2 * i + k, k)
                last_apart(e, seg, nblocks // 2, two)

            def mean_root_rstd(n, ss_sem, ss_value, size, mean, root, done, eps=EPS):
                e.wait_ge(ss_sem, ss_value)
                e.tensor_scalar(sm[:, 36:36 + n], sm[:, 32:32 + n], 1.0 / size, eps, ALU.mult, ALU.add).then_inc(mean, 1)
                e.wait_ge(root, 1)
                e.reciprocal(sm[:, 44:44 + n], sm[:, 40:40 + n]).then_inc(done, 1)

            cols = gated[:, 1, 16:24, :].rearrange("p a b -> p (a b)").rearrange("p (k m) -> p k m", m=P)

            cols2 = lat.rearrange("p a b c -> p (a b c)")[:, 0:D].rearrange("p (k m) -> p k m", m=P)

            def c_rest(cols, time):
                e.wait_ge(S["c_hi"], time)
                e.tensor_tensor(cols[:, :, 2:4], sm[:, 0:32].rearrange("p (j k) -> p k j", j=2),
                                cols[:, :, 0:2].bitcast(F32), ALU.subtract).then_inc(S["c_ready"], 1)

            def low(v, r, q, n):
                return e.tensor_tensor(r[:, 1, q:q + n, :], v.rearrange("p (c t) -> p c t", c=n),
                                       r[:, 0, q:q + n, :].bitcast(F32), ALU.subtract)

            e.memset(cols.bitcast(F32), 0.0).then_inc(S["c_zero"], 1)
            e.wait_ge(S["vec_turned"], 1)
            e.tensor_copy(vec[:, :], ps[:, 4, 0:V_W]).then_inc(S["vec_ready"], 1)
            e.wait_ge(S["silu_c"], 1)
            c_rest(cols, 1)
            splits(0, 4)

            def ada_rows(b):
                e.wait_ge(units_used, ready("ada", b))
                e.tensor_scalar(actf[0:4, 512 * b:512 * b + 512], ps[0:4, 2 * (b % 2), :], 1.0, None,
                                ALU.mult).then_inc(dve_freed, 1)
            for b in range(8):
                splits(8 * b + 4, 8)
                if b == 1:
                    mean_root_rstd(4, S["squares1"], 4, D, S["mean1"], S["root1"], S["rstd1"])
                ada_rows(b)

            e.wait_ge(S["mod_turned"], 1)
            for v in range(2):
                sh = ps[:, 1, v:32:2]
                sc = ps[:, 1, 32 + v:64:2]
                e.tensor_tensor(mod[:, 2 * v + 1, :], sh, vec[:, V_BADA:V_BADA + 16], ALU.add).then_inc(S["mod_step"], 1)
                e.tensor_tensor(mod[:, 2 * v, :], sc, vec[:, V_BADA + 16:V_BADA + 32], ALU.add).then_inc(S["mod_step"], 1)
                e.wait_ge(S["mod_step"], 2 * v + 2)
                e.scalar_tensor_tensor(out=mod[:, 2 * v, :], in0=mod[:, 2 * v, :], scalar=1.0,
                                       in1=vec[:, V_NORM:V_NORM + 16], op0=ALU.add, op1=ALU.mult).then_inc(S["mod_ready"], 1)
            e.wait_ge(S["mod_ready"], 2)
            e.wait_ge(S["h_copied"], 8)

            def affine(n):
                v, q = n % 2, n // 2
                if n >= 2:
                    e.wait_ge(S["h_lo"], n - 1)
                for c in range(4):
                    o = SPARE + v * 1024 + c * 256
                    t = (HI2 if v else LO) + (4 * q + c) * 256
                    e.tensor_scalar(gatedf[:, o:o + 256], gatedf[:, t:t + 256],
                                    mod[:, 2 * v, 4 * q + c:4 * q + c + 1], mod[:, 2 * v + 1, 4 * q + c:4 * q + c + 1],
                                    ALU.mult, ALU.add).then_inc(S["h_affine"], 1)
            affine(0)
            for n in range(8):
                if n < 7:
                    affine(n + 1)
                e.wait_ge(S["h_hi"], n + 1)
                o = SPARE + (n % 2) * 1024
                low(gatedf[:, o:o + 1024], gated if n % 2 else act, 4 * (n // 2), 4).then_inc(S["h_lo"], 1)

            u0 = 2 * FIRST["in"]
            steps = 0

            def step(ins):
                nonlocal steps
                steps += 1
                ins.then_inc(S["rope_step"], 1)

            def settle():
                e.wait_ge(S["rope_step"], steps)

            nrope = 0
            for b in range(6):
                early = 2 if b in (3, 4, 5) else 0
                splits(u0 + 8 * b + 4 + early, 8 - early)
                if b in (0, 2, 3, 4):
                    for tt in range(4 if b == 0 else 2):
                        bank = tt if b == 0 else (0 if b % 2 == 0 else 2) + tt
                        src = ps[:, bank, :].rearrange("p (h d) -> p h d", d=DH)
                        if b == 0:
                            dst = gatedf[:, LO2 + tt * 512:LO2 + (tt + 1) * 512]
                        else:
                            dst = gatedf[:, HI2 + tt * 1536 + (b - 2) * 512:HI2 + tt * 1536 + (b - 1) * 512]
                        heads = dst.rearrange("p (h d) -> p h d", d=DH)
                        gain = t1[:, 128:256] if b == 0 else t1[:, 0:128]
                        sq = side[:, (nrope % 2) * 512:(nrope % 2) * 512 + 512].rearrange("p (h d) -> p h d", d=DH)
                        nrope += 1
                        e.wait_ge(S["sq_ready"], nrope)
                        step(e.tensor_reduce(sm[:, 32:36], sq, AX_X, ALU.add))
                        settle()
                        e.tensor_scalar(sm[:, 48:52], sm[:, 32:36], 1.0 / DH, EPS, ALU.mult, ALU.add).then_inc(S["ss_ready"], 1)
                        e.wait_ge(S["root_ready"], nrope)
                        step(e.reciprocal(sm[:, 68:72], sm[:, 52:56]))
                        settle()
                        ins = e.tensor_tensor(heads, src, sm[:, 68:72].unsqueeze(2).to_broadcast([P, 4, DH]), ALU.mult)
                        if tt == (3 if b == 0 else 1):
                            ins.then_inc(dve_freed, 1)
                            e.wait_ge(dve_freed, freed("in", b))
                        else:
                            step(ins)
                            settle()
                        step(e.tensor_tensor(heads, heads, gain.unsqueeze(1).to_broadcast([P, 4, DH]), ALU.mult))
                        if tt < 2:
                            o = T_ROPE + tt * 128
                            cc = tables[:, o:o + 128]
                            ss = tables[:, o + 256:o + 384].rearrange("p (a w f) -> p a w f", a=2, w=2)
                            halves = dst.rearrange("p (h a w f) -> p h a w f", h=4, a=2, w=2)
                            tmp = side[:, 1024:1536]
                            tmph = tmp.rearrange("p (h a w f) -> p h a w f", h=4, a=2, w=2)
                            settle()
                            for w in range(2):
                                step(e.tensor_tensor(tmph[:, :, :, w, :], halves[:, :, :, 1 - w, :],
                                                     ss[:, :, w, :].unsqueeze(1).to_broadcast([P, 4, 2, 32]), ALU.mult))
                            settle()
                            step(e.tensor_tensor(heads, heads, cc.unsqueeze(1).to_broadcast([P, 4, DH]), ALU.mult))
                            settle()
                            step(e.tensor_tensor(dst, dst, tmp, ALU.add))
                        if b > 0 and tt == 0:
                            splits(u0 + 8 * b + 12, 2)
            assert steps == ROPE_STEPS, steps

            probs = gatedf[:, LO2:LO2 + 1024]

            def kv_turn(kv):
                def ahead(m):
                    if isinstance(kv, int):
                        split(u0 + 48 + 8 * kv + m)
                    else:
                        split(u0 + 48 + m, kv, 8)

                def top(j):
                    n = 3 * kv + j
                    e.wait_ge(S["scores_ready"], n + 1)
                    e.tensor_reduce(sm[:, 56:58], ps[:, 4:6, :], AX_X, ALU.max).then_inc(S["max_step"], 1)
                    e.wait_ge(S["max_step"], n + 1)
                    e.tensor_scalar(sm[:, 58:60], sm[:, 56:58], -ATT_SCALE, None, ALU.mult).then_inc(S["max_ready"], 1)

                def norm(j):
                    n = 3 * kv + j
                    e.wait_ge(S["exp_ready"], 2 * n + 2)
                    e.reciprocal(sm[:, 62:64], sm[:, 60:62]).then_inc(S["sum_inv"], 1)
                    e.wait_ge(S["sum_inv"], n + 1)
                    v = probs.rearrange("p (t s) -> p t s", t=2)
                    e.tensor_tensor(v, v, sm[:, 62:64].unsqueeze(2).to_broadcast([P, 2, 512]), ALU.mult).then_inc(S["probs_ready"], 1)

                def gate(j):
                    n = 3 * kv + j
                    e.wait_ge(S["o_ready"], n + 1)
                    e.tensor_tensor(t0[:, (j % 2) * 256:(j % 2) * 256 + 256], ps[:, 2, 256:512],
                                    gatedf[:, ds(768 * kv + LO + 256 * j, 256)], ALU.mult).then_inc(S["o_gated"], 1)

                def rest(j):
                    n = 3 * kv + j
                    e.wait_ge(S["o_hi"], n + 1)
                    v = t0[:, (j % 2) * 256:(j % 2) * 256 + 256]
                    e.tensor_tensor(gated[:, 1, ds(3 * kv + j, 1), :], v.unsqueeze(1),
                                    gated[:, 0, ds(3 * kv + j, 1), :].bitcast(F32), ALU.subtract).then_inc(S["o_lo"], 1)
                top(0)
                ahead(4)
                norm(0)
                ahead(5)
                top(1)
                gate(0)
                ahead(6)
                norm(1)
                rest(0)
                ahead(7)
                top(2)
                gate(1)
                ahead(8)
                norm(2)
                rest(1)
                ahead(9)
                ahead(10)
                ahead(11)
                gate(2)
                rest(2)
            each(e, HKV - 1, kv_turn)
            kv_turn(3)

            e.wait_ge(S["dft2"], 1)
            mixed = side[:, 2048:3072]
            e.tensor_tensor(mixed.rearrange("p (b c) -> p b c", b=2), ps[:, 0:2, :],
                            gatedf[:, LO + 3072:LO + 4096].rearrange("p (b c) -> p b c", b=2),
                            ALU.mult).then_inc(S["mix_ready"], 1)
            e.wait_ge(S["mix_hi"], 1)
            low(mixed, gated, 12, 4).then_inc(S["mix_lo"], 1)

            e.wait_ge(S["o_ready"], 12)
            e.memset(cols2.bitcast(F32), 0.0).then_inc(S["c_zero"], 1)
            c_rest(cols2, 2)
            segment("gate_a", 4, 4, lambda b, k: None)

            def gate_rows(b, k):
                e.wait_ge(units_used, ready("gate_b", b))
                e.tensor_scalar(side[0:4, ds(D + 512 * b, 512)], ps[0:4, 4 + k, :], 1.0, None,
                                ALU.mult).then_inc(S["rows_read"], 1)
            segment("gate_b", 8, 4, gate_rows)

            def proj(b, k):
                e.wait_ge(units_used, ready("proj", b))
                m = side[:, 1024:2048].rearrange("p (b c) -> p b c", b=2)
                t = side[:, 0:1024].rearrange("p (b c) -> p b c", b=2)
                e.tensor_tensor(m, ps[:, 4 * k:4 * k + 2, :], gatedf[:, ds(HI2 + 1024 * b, 1024)].rearrange(
                    "p (b c) -> p b c", b=2), ALU.mult).then_inc(S["proj_read"], 1)
                e.tensor_tensor(t, ps[:, 4 * k + 2:4 * k + 4, :], gatedf[:, ds(LO2 + 1024 * b, 1024)].rearrange(
                    "p (b c) -> p b c", b=2), ALU.mult).then_inc(dve_freed, 1)
                e.wait_ge(dve_freed, freed("proj", b))
                e.tensor_tensor(m, m, t, ALU.add).then_inc(S["proj_sum"], 1)
                e.wait_ge(S["proj_hi"], b + 1)
                v = side[:, 1024:2048].rearrange("p (c t) -> p c t", c=4)
                e.tensor_tensor(act[:, 1, ds(4 * b, 4), :], v, act[:, 0, ds(4 * b, 4), :].bitcast(F32),
                                ALU.subtract).then_inc(S["proj_lo"], 1)
            segment("proj", 4, 4, proj)

            e.wait_ge(S["bias_loaded"], 16)
            e.wait_ge(S["gate_turned"], 1)
            gate = side[:, 0:D]
            e.tensor_tensor(gate.rearrange("p (b c) -> p b c", b=4), ps[:, 4:8, :],
                            gate.rearrange("p (b c) -> p b c", b=4), ALU.add).then_inc(S["gate_ready"], 1)
            e.wait_ge(S["gate_ready"], 1)

            def out_add(b, k):
                e.wait_ge(units_used, ready("out", b))
                for tt in range(2):
                    e.wait_ge(S["out_step"], 2 * b + tt)
                    ins = e.tensor_tensor(t0[:, :], ps[:, 2 * k + tt, :], side[:, ds(512 * b, 512)], ALU.mult)
                    if tt == 0:
                        ins.then_inc(S["out_read"], 1)
                        e.wait_ge(S["out_read"], b + 1)
                    else:
                        ins.then_inc(dve_freed, 1)
                        e.wait_ge(dve_freed, freed("out", b))
                    v = x[:, tt, ds(512 * b, 512)]
                    e.tensor_tensor(v, v, t0[:, :], ALU.add).then_inc(S["out_step"], 1)
            segment("out", 4, 4, out_add)

            e.wait_ge(S["sq2"], 8)
            e.tensor_reduce(sm[:, 32:34], sm[:, 72:80].rearrange("p (t b) -> p t b", t=2), AX_X, ALU.add).then_inc(S["out_step"], 1)
            mean_root_rstd(2, S["out_step"], 9, D, S["mean2"], S["root2"], S["rstd2"])
            e.wait_ge(S["final_loaded"], 16)
            for q in range(4):
                for n in range(2):
                    e.wait_ge(S["scaled2"], 2 * q + n + 1)
                    v = x[:, n, q * 512:(q + 1) * 512]
                    e.tensor_tensor(v, v, side[:, D + q * 512:D + (q + 1) * 512], ALU.mult).then_inc(S["normed2"], 1)

            def low_x(hi, done):
                for q in range(4):
                    e.wait_ge(hi, q + 1)
                    b = 4 + 2 * (q % 2)
                    e.tensor_tensor(act[:, 1, 4 * q:4 * q + 4, :], ps[:, b:b + 2, :].rearrange("p b (c t) -> p (b c) t", c=2),
                                    act[:, 0, 4 * q:4 * q + 4, :].bitcast(F32), ALU.subtract).then_inc(done, 1)
            low_x(S["x2_hi"], S["x2_lo"])

            def conv(nb, ch0):
                def go(b, k):
                    e.wait_ge(units_used, ready("ssd_x") + nb + b)
                    e.wait_ge(S["conv_silu"], 2 * nb + 2 * b)
                    before = 14 * nb + 14 * b
                    for s in range(4):
                        for fc in range(4):
                            ch = 4 * b + ch0 + fc
                            o = (fc % 2) * 256
                            src = ps[:, 2 * k + fc // 2, o:o + 256]
                            acc = tx[:, fc * 256:(fc + 1) * 256]
                            if s == 0:
                                ins = e.tensor_scalar(acc, src, vec[:, ds(ch + V_CW + 144, 1)], vec[:, ds(ch + V_CB, 1)],
                                                      ALU.mult, ALU.add)
                            else:
                                e.wait_ge(S["conv_step"], before + 4 * s - 3 + fc)
                                ins = e.scalar_tensor_tensor(out=acc[:, s:], in0=src[:, :L - s],
                                                             scalar=vec[:, ds(ch + V_CW + 48 * (3 - s), 1)],
                                                             in1=acc[:, s:], op0=ALU.mult, op1=ALU.add)
                            if s == 3 and fc % 2 == 1:
                                ins.then_inc((S["conv_done"], dve_freed)[fc // 2], 1)
                            else:
                                ins.then_inc(S["conv_step"], 1)
                return go
            segment("ssd_x", 4, 8, conv(0, 0))
            segment("ssd_bc", 4, 4, conv(8, 32))

            y, mag, ee, u, ln, dd, dt = (tx[0:64, n * 256:(n + 1) * 256] for n in range(7))
            adt, acs, rec = u, mag, ee

            def dt_splits(u0):
                def step(ins):
                    ins.then_inc(S["dt_step"], 1)
                e.wait_ge(S["dt_act"], 1)
                step(e.scalar_tensor_tensor(out=mag, in0=y, scalar=-1.0, in1=y, op0=ALU.mult, op1=ALU.max))
                splits(u0, 1)
                e.wait_ge(S["dt_act"], 3)
                step(e.tensor_scalar(u, ee, 1.0, None, ALU.add))
                splits(u0 + 1, 1)
                e.wait_ge(S["dt_step"], 2)
                step(e.scalar_tensor_tensor(out=dd, in0=u, scalar=-1.0, in1=ee, op0=ALU.add, op1=ALU.subtract))
                e.wait_ge(S["dt_step"], 3)
                step(e.reciprocal(rec, u))
                splits(u0 + 2, 1)
                e.wait_ge(S["dt_step"], 4)
                step(e.tensor_tensor(dd, dd, rec, ALU.mult))
                e.wait_ge(S["dt_act"], 4)
                e.wait_ge(S["dt_step"], 5)
                step(e.tensor_tensor(ln, ln, dd, ALU.subtract))
                e.wait_ge(S["dt_step"], 6)
                step(e.scalar_tensor_tensor(out=dt, in0=y, scalar=0.0, in1=ln, op0=ALU.max, op1=ALU.add))
                step(e.memset(dd, 1.0))
                splits(u0 + 3, 1)
                e.wait_ge(S["dt_step"], 8)
                step(e.tensor_scalar(adt, dt, sm[0:64, 66:67], -1.0, ALU.mult, ALU.mult))
                e.wait_ge(S["dt_step"], 9)
                step(e.tensor_tensor_scan(acs, dd, adt, 0.0, ALU.mult, ALU.add))
                splits(u0 + 4, 4)
                e.wait_ge(S["dt_turned"], 1)
                e.tensor_copy(t1[:, :], ps[:, 5, 0:256]).then_inc(S["dt_ready"], 1)

            def z_two(i):
                for k in range(2):
                    ahead = 2 * FIRST["ssd_z"] + 8 * k + 4
                    if k == 0 and isinstance(i, int):
                        dt_splits(ahead)
                    else:
                        splits(ahead, 8, i, 16)
            each(e, 4, z_two)
            e.wait_ge(act_freed, freed("ssd_z", 7))
            e.wait_ge(units_used, ready("ssd_z", 7))
            e.wait_ge(S["xt_copied"], 8)
            e.wait_ge(S["x_scaled"], 1)
            e.wait_ge(S["acs_stored"], 16)

            ex = actf[:, 1024:4096]
            xdt = actf[:, 7168:8192]
            cbm = t0[:, 0:384]
            U0 = 2 * FIRST["ssd_out"]

            def add_out(t, g):
                n = 4 * g - 4 + t
                e.wait_ge(units_used, ready("ssd_out", n))
                e.wait_ge(dve_freed, freed("ssd_out", n - 4))
                v = x[:, :, t * 512:(t + 1) * 512]
                e.tensor_tensor(v, ps[:, 2 * (t % 2):2 * (t % 2) + 2, :], v, ALU.add).then_inc(dve_freed, 1)

            def scan_turn(g):
                def ahead(m):
                    if not isinstance(g, int):
                        split(U0 - 8 + m, g, 8)

                def add(t):
                    if not isinstance(g, int):
                        add_out(t, g)

                def masked(n):
                    e.wait_ge(S["decay_ready"], 2 * g + n + 1)
                    v = ex[:, n * 1536:(n + 1) * 1536].rearrange("p (h l) -> p h l", h=4)
                    e.tensor_tensor(v, v, cbm.unsqueeze(1).to_broadcast([P, 4, 384]), ALU.mult).then_inc(S["m_ready"], 1)

                v = gatedf[:, ds(1024 * g, 1024)].rearrange("p (t h d) -> p t h d", t=2, d=HD)
                yb = tx[:, 0:1024]
                dt = t1[:, 128:256].rearrange("p (t h) -> p t h", t=2)
                e.wait_ge(S["y_mm"], g)
                e.tensor_tensor(xdt.rearrange("p (t h d) -> p t h d", t=2, d=HD), v,
                                dt[:, :, ds(8 * g, 8)].unsqueeze(3).to_broadcast([P, 2, R, HD]),
                                ALU.mult).then_inc(S["xdt_step"], 1)
                e.wait_ge(S["cb_ready"], g + 1)
                e.wait_ge(S["m_ready"], 2 * g)
                e.tensor_tensor(cbm, ps[:, 4, 0:384], tables[:, T_TRI:T_TRI + 384], ALU.mult).then_inc(S["cb_masked"], 1)
                e.wait_ge(S["cb_masked"], g + 1)
                masked(0)
                masked(1)
                ahead(4)
                ahead(5)
                e.wait_ge(S["y_turned"], 2 * g)
                e.tensor_tensor(yb.rearrange("p (t h d) -> p t h d", t=2, d=HD), v,
                                t0[:, ds(8 * g + 384, 8)].unsqueeze(1).unsqueeze(3).to_broadcast([P, 2, R, HD]),
                                ALU.mult).then_inc(S["xdt_step"], 1)
                add(0)
                ahead(6)
                ahead(7)
                add(1)
                e.wait_ge(S["y_mm"], g + 1)
                e.wait_ge(S["xdt_step"], 2 * g + 2)
                e.tensor_tensor(yb.rearrange("p (b c) -> p b c", b=2), ps[:, 5:7, :], yb.rearrange("p (b c) -> p b c", b=2),
                                ALU.add).then_inc(S["y_step"], 1)
                e.wait_ge(S["y_step"], 4 * g + 1)
                e.tensor_tensor(yb, yb, gatedf[:, ds(1024 * g + LO, 1024)], ALU.mult).then_inc(S["y_step"], 1)
                ahead(8)
                e.wait_ge(S["y_act"], 3 * g + 2)
                e.tensor_scalar(sm[:, 36:38], sm[:, 32:34], 1.0 / 512, EPS, ALU.mult, ALU.add).then_inc(S["y_step"], 1)
                e.wait_ge(S["y_act"], 3 * g + 3)
                e.reciprocal(sm[:, 44:46], sm[:, 40:42]).then_inc(S["y_step"], 1)
                ahead(9)
                add(2)
                for c in range(4):
                    if c % 2 == 0:
                        e.wait_ge(S["y_hi"], 4 * g + 2 + c)
                    e.scalar_tensor_tensor(out=act[:, 1, c, :], in0=ps[:, 5 + c // 2, (c % 2) * 256:(c % 2) * 256 + 256],
                                           scalar=sm[:, 72 + c:73 + c], in1=act[:, 0, c, :].bitcast(F32),
                                           op0=ALU.mult, op1=ALU.subtract).then_inc(S["y_lo"], 1)
                ahead(10)
                ahead(11)
                add(3)
            each(e, G, scan_turn)

            def piece_stats(q, seg, b, dve):
                e.wait_ge(dve_freed, freed(seg, b))
                for n in range(2):
                    e.bn_stats(t0[:, n * 24 + q * 6:n * 24 + q * 6 + 6], x[:, n, q * 512:(q + 1) * 512]).then_inc(dve, 1)

            for t in range(4):
                splits(U0 + 60 + 2 * t, 2)
                add_out(t, G)
                piece_stats(t, "ssd_out", 28 + t, S["ln_dve"])

            def residual(seg, name):
                def go(b, k):
                    e.wait_ge(units_used, ready(seg, b))
                    for tt in range(2):
                        v = x[:, tt, ds(512 * b, 512)]
                        e.scalar_tensor_tensor(out=v, in0=v, scalar=ALPHA, in1=ps[:, 2 * k + tt, :], op0=ALU.mult,
                                               op1=ALU.add).then_inc(dve_freed if tt else S[name], 1)
                return go
            def layer_norm(dve, stats, act_sem, rstd, rows):
                e.wait_ge(dve, 8)
                for n in range(2):
                    e.bn_aggr(sm[:, 32 + 2 * n:34 + 2 * n], t0[:, n * 24:n * 24 + 24]).then_inc(dve, 1)
                e.wait_ge(dve, 10)
                e.tensor_scalar(sm[:, 38:40], sm[:, 33:37:2], LN_EPS, None, ALU.add).then_inc(stats, 1)
                e.wait_ge(act_sem, 1)
                e.reciprocal(sm[:, 44:46], sm[:, 40:42]).then_inc(dve, 1)
                e.wait_ge(dve, 11)
                e.scalar_tensor_tensor(out=sm[:, 46:48], in0=sm[:, 32:36:2], scalar=-1.0, in1=sm[:, 44:46],
                                       op0=ALU.mult, op1=ALU.mult).then_inc(rstd, 1)
                e.wait_ge(rows, 32)
                for q in range(4):
                    for n in range(2):
                        e.wait_ge(act_sem, 2 + 2 * q + n)
                        v = x[:, n, q * 512:(q + 1) * 512]
                        e.tensor_tensor(v, v, side[:, q * 512:(q + 1) * 512], ALU.mult).then_inc(dve, 1)
                    for n in range(2):
                        e.wait_ge(dve, 11 + 4 * q + n + 1)
                        v = x[:, n, q * 512:(q + 1) * 512]
                        e.tensor_tensor(v, v, side[:, D + q * 512:D + (q + 1) * 512], ALU.add).then_inc(dve, 1)
            layer_norm(S["ln_dve"], S["ln_stats"], S["ln_act"], S["ln_rstd"], S["ln_rows"])
            low_x(S["x3_hi"], S["x3_lo"])

            u0 = 2 * FIRST["lat_q"]
            splits(u0 + 4, 16)
            e.wait_ge(S["lat_sq"], 4)
            e.tensor_scalar(sm[:, 36:38], sm[:, 32:34], 1.0 / 512, EPS, ALU.mult, ALU.add).then_inc(S["lat_mean"], 1)
            e.tensor_scalar(sm[:, 38:40], sm[:, 34:36], 1.0 / 256, EPS, ALU.mult, ALU.add).then_inc(S["lat_mean"], 1)
            u0 = 2 * FIRST["lat_gate0"]
            splits(u0 + 4, 2)
            e.wait_ge(S["lat_root"], 1)
            e.reciprocal(sm[:, 44:48], sm[:, 40:44]).then_inc(S["lat_rstd"], 1)
            for tt in range(2):
                o = 1024 + tt * 336 + 256
                e.tensor_copy(t1[:, tt * 128:(tt + 1) * 128].rearrange("p (r d) -> p r d", r=2),
                              tx[:, o:o + 64].unsqueeze(1).to_broadcast([P, 2, 64])).then_inc(S["lat_act"], 1)
            splits(u0 + 6, 2)
            e.wait_ge(S["lat_turned"], 1)
            for c in range(6):
                bank, o = (4 + c // 2, (c % 2) * 256) if c < 4 else (6, (c - 4) * 256)
                gain = V_QN + c if c < 4 else V_KVN + c - 4
                dst = tx[:, c * 256:(c + 1) * 256] if c < 4 else t0[:, (c - 4) * 256:(c - 3) * 256]
                e.tensor_scalar(dst, ps[:, bank, o:o + 256],
                                vec[:, gain:gain + 1], None, ALU.mult).then_inc(S["lat_scaled"], 1)
            splits(u0 + 8, 2)
            e.wait_ge(S["lat_hi"], 2)
            low(tx[:, 0:1024], lat, 0, 4).then_inc(S["lat_lo"], 1)
            low(t0[:, 0:512], lat, 4, 2).then_inc(S["lat_lo"], 1)
            splits(u0 + 10, 10)
            splits(2 * FIRST["lat_gate"], 4)

            score = side[:, 3072:3456]
            bias = side[:, 3456:3840]
            parts = ((0, 128), (128, 384))
            for h in range(16):
                e.wait_ge(S["idx_relu"], h + 1)
                o = 2304 + (h % 2) * 384
                for tt, (lo, hi) in enumerate(parts):
                    w = tx[:, 1024 + tt * 336 + 320 + h:1025 + tt * 336 + 320 + h]
                    if h == 0:
                        ins = e.tensor_scalar(score[:, lo:hi], gatedf[:, o + lo:o + hi], w, None, ALU.mult)
                    else:
                        e.wait_ge(S["idx_step"], 2 * h - 1 + tt)
                        ins = e.scalar_tensor_tensor(out=score[:, lo:hi], in0=gatedf[:, o + lo:o + hi], scalar=w,
                                                     in1=score[:, lo:hi], op0=ALU.mult, op1=ALU.add)
                    ins.then_inc(S["idx_step"], 1)
            e.wait_ge(S["idx_step"], 32)
            for lo in (0, 256):
                v = score[:, lo:lo + 128]
                e.tensor_tensor(v, v, tables[:, T_UNSEEN:T_UNSEEN + 128], ALU.add).then_inc(S["idx_step"], 1)
            for r in range(TOPK // 8):
                for tt, (lo, hi) in enumerate(parts):
                    e.wait_ge(S["idx_step"], 34 + 4 * r if r == 0 else 33 + 4 * r + tt)
                    e.max(sm[:, 8 * tt:8 * tt + 8], score[:, lo:hi]).then_inc(S["idx_step"], 1)
                for tt, (lo, hi) in enumerate(parts):
                    e.wait_ge(S["idx_step"], 35 + 4 * r + tt)
                    e.match_replace(score[:, lo:hi], sm[:, 8 * tt:8 * tt + 8], score[:, lo:hi],
                                    TAKEN).then_inc(S["idx_step"], 1)
            e.wait_ge(S["idx_step"], 66)
            e.tensor_scalar(bias, score, -3.2e38, NEG, ALU.is_gt, ALU.mult).then_inc(S["idx_step"], 1)
            e.wait_ge(S["idx_step"], 67)
            for lo in (0, 256):
                v = bias[:, lo:lo + 128]
                e.tensor_tensor(v, v, tables[:, T_NEG:T_NEG + 128], ALU.add).then_inc(S["idx_done"], 1)
            segment("lat_gate", 4, 6, lambda b, k: None)

            e.wait_ge(S["idx_done"], 2)

            def heads_turn(t, k, ahead, i, softmax=True, project=True):
                def top(h, here=softmax, of=t - 1):
                    if here:
                        n = 4 * of + h
                        p = actf[:, 6144 + (h % 2) * 384:6528 + (h % 2) * 384]
                        c = 72 + 8 * (h % 2)
                        e.wait_ge(S["hs_mm"], n + 1)
                        if not isinstance(n, int) or n > 1:
                            e.wait_ge(S["hs_turned"], n - 1)
                        e.tensor_tensor(p, ps[:, 4 + h % 2, 0:384], bias, ALU.add).then_inc(S["hs_masked"], 1)
                        e.wait_ge(S["hs_masked"], n + 1)
                        for tt, (lo, hi) in enumerate(parts):
                            e.tensor_reduce(sm[:, c + tt:c + 1 + tt], p[:, lo:hi], AX_X, ALU.max).then_inc(S["hs_step"], 1)
                        e.wait_ge(S["hs_step"], 2 * n + 2)
                        e.tensor_scalar(sm[:, c + 2:c + 4], sm[:, c:c + 2], -ATT_SCALE, None, ALU.mult).then_inc(S["hs_max"], 1)

                def norm(h):
                    if softmax:
                        n = 4 * (t - 1) + h
                        p = actf[:, 6144 + (h % 2) * 384:6528 + (h % 2) * 384]
                        c = 72 + 8 * (h % 2)
                        e.wait_ge(S["hs_exp"], 2 * n + 2)
                        e.reciprocal(sm[:, c + 6:c + 8], sm[:, c + 4:c + 6]).then_inc(S["hs_inv"], 1)
                        e.wait_ge(S["hs_inv"], n + 1)
                        for tt, (lo, hi) in enumerate(parts):
                            ins = e.tensor_scalar(p[:, lo:hi], p[:, lo:hi], sm[:, c + 6 + tt:c + 7 + tt], None, ALU.mult)
                        ins.then_inc(S["hs_probs"], 1)

                def gate(h):
                    if softmax:
                        n = 4 * (t - 1) + h
                        e.wait_ge(S["ho_mm"], n + 1)
                        o = 7680 + (h % 2) * 256
                        if not isinstance(n, int) or n > 1:
                            e.wait_ge(S["ho_lo"], n - 1)
                        e.tensor_tensor(actf[:, o:o + 256], ps[:, 7, (h % 2) * 256:(h % 2) * 256 + 256],
                                        gatedf[:, ds(LO + 256 * n, 256)], ALU.mult).then_inc(S["ho_gated"], 1)

                def rest(h):
                    if softmax:
                        n = 4 * (t - 1) + h
                        e.wait_ge(S["ho_hi"], n + 1)
                        v = actf[:, 7680 + (h % 2) * 256:7936 + (h % 2) * 256]
                        e.tensor_tensor(gated[:, 1, ds(n, 1), :], v.unsqueeze(1), gated[:, 0, ds(n, 1), :].bitcast(F32),
                                        ALU.subtract).then_inc(S["ho_lo"], 1)
                norm(0)
                top(1)
                splits(ahead, 1, i, 8)
                norm(1)
                top(2)
                splits(ahead + 1, 1, i, 8)
                gate(0)
                norm(2)
                top(3)
                rest(0)
                gate(1)
                norm(3)
                splits(ahead + 2, 1, i, 8)
                rest(1)
                splits(ahead + 3, 1, i, 8)
                gate(2)
                rest(2)
                top(0, project, t)
                gate(3)
                rest(3)

            HEAD = 2 * FIRST["head_q"] + 4
            heads_turn(0, 0, HEAD, 0, softmax=False)
            heads_turn(1, 1, HEAD + 4, 0)
            with e.Fori(1, 3) as i:
                for k in range(2):
                    heads_turn(2 * i + k, k, HEAD + 4 * k, i)
            heads_turn(6, 0, HEAD + 24, 0)
            heads_turn(7, 1, HEAD + 28, 0)
            heads_turn(8, 0, HEAD + 32, 0, project=False)

            u0 = 2 * FIRST["lat_out"]
            add = residual("lat_out", "half_read")
            for b in range(4):
                splits(u0 + 16 * b + (4 if b else 8), 16 if b else 12)
                add(b, b % 2)
                piece_stats(b, "lat_out", b, S["fin_dve"])
            layer_norm(S["fin_dve"], S["fin_stats"], S["fin_act"], S["fin_rstd"], S["fin_rows"])

        @block.gpsimd
        def _(e):
            def fixed():
                e.wait_ge(S["small_loaded"], 16 * 13)

            def bc(dst, src, done):
                e.dma_start(dst, src.partition_broadcast(P)).then_inc(done, 16)

            def stage(kv):
                e.wait_ge(S["qt_turned"], kv)
                fixed()
                e.tensor_copy(side[:, 2048:2816].rearrange("p (t c) -> p t c", t=2),
                              gatedf[:, HI2:HI2 + 3072].rearrange("p (t c) -> p t c", t=2)[:, :, ds(384 * kv, 384)]
                              ).then_inc(S["q_staged"], 1)
                e.wait_ge(S["o_ready"], 3 * kv)
                fixed()
                e.tensor_copy(side[:, 2816:3328].rearrange("p (t c) -> p t c", t=4),
                              gatedf[:, LO2 + 2048:LO2 + 4096].rearrange("p (t c) -> p t c", t=4)[:, :, ds(128 * kv, 128)]
                              ).then_inc(S["v_staged"], 1)
            e.wait_ge(S["rope_step"], ROPE_STEPS)
            e.wait_ge(act_freed, freed("in", 1))
            each(e, HKV, stage)

            e.wait_ge(S["proj_lo"], 4)
            bc(side[:, 0:D], a["b_ada"][2 * D:3 * D], S["bias_loaded"])
            e.wait_ge(S["gate_turned"], 1)
            bc(side[:, D:2 * D], a["final_g"], S["final_loaded"])
            e.wait_ge(dve_freed, freed("out", 3))

            e.wait_ge(S["out_step"], 8)
            bc(t0[:, 384:448], a["ssd_d_skip_2"], S["rows_loaded"])
            e.dma_start(sm[0:64, 64:65], a["ssd_a_log_2"].rearrange("(h o) -> h o", o=1)).then_inc(S["rows_loaded"], 16)
            e.dma_start(sm[0:64, 65:66], a["ssd_dt_bias_2"].rearrange("(h o) -> h o", o=1)).then_inc(S["rows_loaded"], 16)
            for n in range(2):
                e.dma_start(gatedf[:, LO + 4096 + n * 512:LO + 4608 + n * 512].rearrange("p (c h) -> p c h", c=8),
                            a["ssd_w_in_2"][n * 1024:(n + 1) * 1024, 10240:10304].rearrange("(c p) h -> p c h", p=P)
                            ).then_inc(S["rows_loaded"], 16)
            e.wait_ge(S["dt_step"], 10)
            e.dma_start(acs_dram, tx[0:64, 256:512]).then_inc(S["acs_stored"], 16)
            e.wait_ge(S["acs_stored"], 16)

            e.wait_ge(units_used, ready("ssd_z", 7))
            e.wait_ge(S["conv_silu"], 24)

            def stage_scan(g):
                e.wait_ge(S["diff_ready"], 2 * g)
                e.dma_start(actf[:, 5120:7168], acs_dram[ds(8 * g, 8), :].rearrange("h l -> (h l)").partition_broadcast(P)
                            ).then_inc(S["r_loaded"], 16)
                fixed()
                e.tensor_copy(sm[:, 76:92].rearrange("p (t h) -> p t h", t=2),
                              t1[:, 0:128].rearrange("p (t h) -> p t h", t=2)[:, :, ds(8 * g, 8)]).then_inc(S["acs_staged"], 1)
                e.wait_ge(S["cb_ready"], g)
                fixed()
                e.tensor_copy(tx[:, 1024:1280], side[:, ds(256 * g, 256)]).then_inc(S["b_staged"], 1)
                e.wait_ge(S["y_lo"], 4 * g)
                fixed()
                e.tensor_copy(sm[:, 72:76], vec[:, ds(4 * g + V_SSDG, 4)]).then_inc(S["g_staged"], 1)
            each(e, G, stage_scan)
            e.wait_ge(S["cb_ready"], G)
            bc(side[:, 0:D], a["ln_g_2"][0, :], S["ln_rows"])
            bc(side[:, D:2 * D], a["ln_b_2"][0, :], S["ln_rows"])
            e.wait_ge(S["hs_masked"], 32)
            e.wait_ge(units_used, 2 * FIRST["lat_out"])
            bc(side[:, 0:D], a["ln_g_2"][1, :], S["fin_rows"])
            bc(side[:, D:2 * D], a["ln_b_2"][1, :], S["fin_rows"])
            o_v = out.rearrange("(t p) d -> p t d", p=P)
            for q in range(4):
                e.wait_ge(S["fin_dve"], 15 + 4 * q)
                e.dma_start(o_v[:, :, q * 512:(q + 1) * 512], x[:, :, q * 512:(q + 1) * 512]).then_inc(S["stored"], 16)
            e.wait_ge(S["stored"], 64)

        @block.tensor
        def _(e):
            def unit(u, i, step, body):
                e.wait_ge(lo_done, linear(lambda v: v + 1, u, step, i))
                for c in range(2):
                    last = body(c, u % SPLIT)
                last.then_inc(units_used, 1)

            def tokens_out(banks, left, kc, slot, c, first, last, w=CB):
                for bank, (hi, lo) in zip(banks, left):
                    e.matmul(ps[:, bank, :w], hi, w_hi[:, slot, c, :w], start=first, stop=False)
                    e.matmul(ps[:, bank, :w], hi, w_lo[:, slot, c, :w], start=False, stop=False)
                    ins = e.matmul(ps[:, bank, :w], lo, w_hi[:, slot, c, :w], start=False, stop=last)
                return ins

            def features_out(bank, hi, lo, slot, c, first, last):
                for f in range(4):
                    o = ps[:, bank + f // 2, (f % 2) * 256:(f % 2) * 256 + 256]
                    wh = w_hi[:, slot, c, f * P:(f + 1) * P]
                    wl = w_lo[:, slot, c, f * P:(f + 1) * P]
                    e.matmul(o, wh, hi, start=first and f % 2 == 0, stop=False, skip_group_check=True)
                    e.matmul(o, wh, lo, start=False, stop=False, skip_group_check=True)
                    ins = e.matmul(o, wl, hi, start=False, stop=last and f % 2 == 1, skip_group_check=True)
                return ins

            def tok(src, kc, tt):
                return src[:, 0, kc, tt * P:(tt + 1) * P], src[:, 1, kc, tt * P:(tt + 1) * P]

            def gemm(u0, n, src, bank, by_token, i=0, step=0, w=CB, kc0=0, starts=True, ends=True, after=None):
                for m in range(n):
                    def body(c, slot, m=m):
                        kc = kc0 + 2 * m + c
                        if after is not None and kc % 4 == 0:
                            e.wait_ge(after, kc // 4 + 1)
                        first, last = starts and m == 0 and c == 0, ends and m == n - 1 and c == 1
                        if by_token:
                            return tokens_out((bank, bank + 1), (tok(src, kc, 0), tok(src, kc, 1)), kc, slot, c, first, last, w)
                        return features_out(bank, src[:, 0, kc, :], src[:, 1, kc, :], slot, c, first, last)
                    unit(u0 + m, i, step, body)

            def pair_free(n, i=0):
                for sem_, who in ((act_freed, "act"), (dve_freed, "dve")):
                    if n >= 2 and isinstance(i, int) and freed_count(who, n + 2 * i - 2):
                        e.wait_ge(sem_, freed_count(who, n + 2 * i - 2))

            def segment(seg, per, nblocks, body):
                n0 = BI[seg]
                who = BLOCKS[n0][1]
                mine = act_freed if who == "act" else dve_freed
                other, its = (dve_freed, "dve") if who == "act" else (act_freed, "act")
                pair_free(n0)

                def two(i):
                    for k in range(2):
                        done = freed_count(who, n0 - 1) - 1 + k
                        if done >= 0:
                            e.wait_ge(mine, done + 2 * i)
                        if k == 1 and freed_count(its, n0 - 1):
                            e.wait_ge(other, freed_count(its, n0 - 1))
                        body(2 * i + k, k, i, 2 * FIRST[seg] + 2 * per * k, 4 * per)
                each(e, nblocks // 2, two)

            def turn4(src_at, q, b):
                for c in range(4):
                    for tt in range(2):
                        ins = e.transpose(ps[:, b + c // 2, (c % 2) * 256 + tt * P:(c % 2) * 256 + (tt + 1) * P],
                                          src_at(4 * q + c, tt), ident)
                return ins

            e.wait_ge(S["small_loaded"], 16 * 13)
            o = 0
            for n, rows in enumerate((102, 96, 96, 80)):
                ins = e.transpose(ps[:, 4, o:o + rows], t0[0:rows, n * P:(n + 1) * P], ident[0:rows, 0:rows])
                o += rows
            ins.then_inc(S["vec_turned"], 1)

            cols = gated[:, 1, 16:24, :].rearrange("p a b -> p (a b)").rearrange("p (k m) -> p k m", m=P)

            cols2 = lat.rearrange("p a b c -> p (a b c)")[:, 0:D].rearrange("p (k m) -> p k m", m=P)

            def modulation(b, k, i, u0, step, cols=cols, bank=0, m0=0, n=8):
                for m in range(m0, m0 + n):
                    def body(c, slot, m=m):
                        kc = 2 * m + c
                        e.matmul(ps[:, bank + 2 * k, :], cols[:, kc, :], w_hi[:, slot, c, :], start=kc == 0, stop=False)
                        return e.matmul(ps[:, bank + 2 * k, :], cols[:, kc, :], w_lo[:, slot, c, :], start=False, stop=kc == 15)
                    unit(u0 + m - m0, i, step, body)
            e.wait_ge(S["c_ready"], 1)
            ADA = BI["ada"]
            assert ADA == 0

            def first_two(i):
                for k in range(2):
                    if k == 1:
                        e.wait_ge(dve_freed, 2 * i)
                    modulation(2 * i + k, k, i, 8 * k, 16)
                    if k == 1:
                        e.wait_ge(dve_freed, 2 * i + 1)
            each(e, 2, first_two)

            def turn_rows(b0, b1):
                e.wait_ge(dve_freed, freed("ada", b1 - 1))
                for c in range(4 * b0, 4 * b1):
                    ins = e.matmul(ps[:, 1, 2 * c:2 * c + 2], actf[0:4, c * P:(c + 1) * P],
                                   tables[0:4, T_SEL:T_SEL + 2], start=True, stop=True)
                return ins
            for b in range(4, 8):
                e.wait_ge(dve_freed, b - 1)
                for half in range(2):
                    modulation(b, b % 2, 0, 8 * b + 4 * half, 0, m0=4 * half, n=4)
                    n = 2 * (b - 4) + half
                    src = gatedf if n < 4 else side
                    if n == 0:
                        e.wait_ge(S["xn_ready"], 4)
                        e.wait_ge(S["rows_in"], 16 * 5)
                    if n >= 2:
                        e.wait_ge(S["h_copied"], n - 1)
                    turn4(lambda c, tt: src[:, tt * D + c * P:tt * D + (c + 1) * P], n % 4,
                          4 + 2 * (n % 2)).then_inc(S["h_turned"], 1)
                turn_rows(0 if b == 4 else b - 1, b)

            e.wait_ge(S["h_copied"], 8)
            turn_rows(7, 8).then_inc(S["mod_turned"], 1)

            e.wait_ge(S["mod_ready"], 2)
            for b in range(6):
                u0 = 2 * FIRST["in"] + 8 * b
                if b < 2:
                    for m in range(8):
                        if b == 0 and m % 2 == 0:
                            e.wait_ge(S["h_lo"], m + 2)

                        def body(c, slot, m=m, b=b):
                            kc = 2 * m + c
                            return tokens_out([4 * b + t for t in range(4)],
                                              [tok(act, kc, 0), tok(act, kc, 1), tok(gated, kc, 0), tok(gated, kc, 1)],
                                              kc, slot, c, kc == 0, kc == 15)
                        unit(u0 + m, 0, 0, body)
                    continue
                if b < 4:
                    e.wait_ge(dve_freed, freed("in", 0))
                else:
                    pair_free(BI["in"] + b)
                gemm(u0, 8, act, 2 * (b % 2), b < 5)

            e.wait_ge(S["rope_step"], ROPE_STEPS)
            e.wait_ge(act_freed, freed("in", 1))
            for kv in range(HKV):
                for tt in range(4):
                    o = LO2 + tt * 512 + kv * P
                    ins = e.transpose(ps[:, 4 + kv, tt * P:(tt + 1) * P], gatedf[:, o:o + P], ident)
                ins.then_inc(S["k_turned"], 1)
            probs = gatedf[:, LO2:LO2 + 1024]
            pt = gatedf[:, LO2 + 1024:LO2 + 2048]
            qt = side[:, 3328:4096]
            u0 = 2 * FIRST["in"] + 48
            pair_free(BI["in"] + 6)

            def kv_turn(kv):
                token = isinstance(kv, int) and kv == 3

                def product(m):
                    if isinstance(kv, int):
                        gemm(u0 + 8 * kv + m, 1, act, 0, token, kc0=2 * m, starts=m == 0, ends=m == 7)
                    else:
                        gemm(u0 + m, 1, act, 0, token, kv, 8, kc0=2 * m, starts=m == 0, ends=m == 7)

                def scores(j):
                    e.wait_ge(S["qt_ready"], 2 * kv + (1, 1, 2)[j])
                    e.wait_ge(S["kt_ready"], 4)
                    e.wait_ge(S["exp_ready"], 6 * kv + 2 * j)
                    for tt in range(2):
                        ins = e.matmul(ps[:, 4 + tt, :], qt[:, j * 256 + tt * P:j * 256 + (tt + 1) * P],
                                       side[:, ds(512 * kv, 512)], start=True, stop=True)
                    ins.then_inc(S["scores_ready"], 1)

                def turn(j):
                    n = 3 * kv + j
                    e.wait_ge(S["probs_ready"], n + 1)
                    e.wait_ge(S["pt_ready"], n)
                    for tt in range(2):
                        for c in range(4):
                            o = tt * 512 + c * P
                            ins = e.transpose(ps[:, 6 + c // 2, (c % 2) * 256 + tt * P:(c % 2) * 256 + (tt + 1) * P],
                                              probs[:, o:o + P], ident)
                    ins.then_inc(S["probs_turned"], 1)

                def mix(j):
                    n = 3 * kv + j
                    e.wait_ge(S["pt_ready"], n + 1)
                    e.wait_ge(S["v_staged"], kv + 1)
                    e.wait_ge(S["qt_ready"], 2 * kv + 2)
                    e.wait_ge(S["o_gated"], n)
                    for c in range(4):
                        ins = e.matmul(ps[:, 2, 256:512], side[:, 2816 + c * P:2816 + (c + 1) * P],
                                       pt[:, c * 256:(c + 1) * 256], start=c == 0, stop=c == 3)
                    ins.then_inc(S["o_ready"], 1)

                e.wait_ge(S["q_staged"], kv + 1)
                e.wait_ge(act_freed, freed("in", 5) + kv)
                e.wait_ge(S["o_gated"], 3 * kv)
                for j in range(3):
                    for tt in range(2):
                        o = 2048 + tt * 384 + j * P
                        ins = e.transpose(ps[:, 3 - j // 2, (j % 2) * 256 + tt * P:(j % 2) * 256 + (tt + 1) * P],
                                          side[:, o:o + P], ident)
                ins.then_inc(S["qt_turned"], 1)
                product(0)
                scores(0)
                product(1)
                product(2)
                turn(0)
                scores(1)
                product(3)
                mix(0)
                product(4)
                turn(1)
                scores(2)
                product(5)
                mix(1)
                product(6)
                turn(2)
                product(7)
                mix(2)
            each(e, HKV - 1, kv_turn)
            kv_turn(3)

            e.wait_ge(act_freed, freed("in", 9))
            e.wait_ge(S["pt_ready"], 12)
            for g in range(4):
                for kt in range(2):
                    o = HI2 + 3072 + kt * 512 + g * P
                    ins = e.matmul(ps[:, 4 + g, :], gatedf[:, o:o + P], tables[:, T_DFT + kt * 512:T_DFT + (kt + 1) * 512],
                                   start=kt == 0, stop=kt == 1)
                ins.then_inc(S["dft1"], 1)
            e.wait_ge(S["dft1_out"], 4)
            for g in range(4):
                for w in range(2):
                    o = 2048 + g * 512 + w * 256
                    ins = e.matmul(ps[:, g // 2, (g % 2) * 256:(g % 2) * 256 + 256],
                                   tables[:, T_DFTC + w * P:T_DFTC + (w + 1) * P], side[:, o:o + 256],
                                   start=w == 0, stop=w == 1)
            ins.then_inc(S["dft2"], 1)
            e.wait_ge(S["mix_ready"], 1)
            e.wait_ge(S["o_gated"], 12)

            def from_act(by_token):
                def go(b, k, i, u0, step):
                    gemm(u0, 8, act, 2 * k, by_token, i, step)
                return go
            segment("gate_a", 4, 4, from_act(False))
            e.wait_ge(S["c_ready"], 2)

            def gate_b_block(b, k, i, u0, step):
                if not isinstance(b, int) or b > 1:
                    e.wait_ge(S["rows_read"], b - 1)
                for q in range(4):
                    gemm(u0 + 4 * q, 2, act, 2 * k, False, i, step, kc0=4 * q, starts=q == 0, ends=q == 3)
                    modulation(b, 0, i, u0 + 4 * q + 2, step, cols2, 4 + k, 2 * q, 2)
            segment("gate_b", 8, 4, gate_b_block)

            e.wait_ge(S["o_lo"], 12)
            e.wait_ge(S["mix_lo"], 1)
            e.wait_ge(act_freed, freed("gate_b", 3))
            e.wait_ge(S["rows_read"], 4)

            def project(b, k, i, u0, step):
                gemm(u0, 6, gated, 4 * k, False, i, step)
                gemm(u0 + 6, 2, gated, 4 * k + 2, False, i, step, kc0=12)
            segment("proj", 4, 4, project)

            e.wait_ge(dve_freed, freed("proj", 3))
            for q in range(4):
                ins = e.matmul(ps[:, 4 + q, :], tables[0:4, T_SELX:T_SELX + P],
                               side[0:4, D + q * 512:D + (q + 1) * 512], start=True, stop=True)
            ins.then_inc(S["gate_turned"], 1)
            e.wait_ge(S["proj_lo"], 4)
            segment("out", 4, 4, from_act(True))

            def turn_x(norm, value, gap, low_done, done):
                for q in range(4):
                    e.wait_ge(norm, value + gap * q)
                    if q >= 2:
                        e.wait_ge(low_done, q - 1)
                    turn4(lambda c, tt: x[:, tt, c * P:(c + 1) * P], q, 4 + 2 * (q % 2)).then_inc(done, 1)
            e.wait_ge(S["gate_ready"], 1)
            turn_x(S["normed2"], 2, 2, S["x2_lo"], S["x2_turned"])

            def dt_product():
                w = gatedf[:, LO + 4096:LO + 5120]
                for kc in range(KD):
                    for v in range(2):
                        ins = e.matmul(ps[0:64, 4, 0:256], w[:, kc * 64:(kc + 1) * 64], act[:, v, kc, :].bitcast(F32),
                                       start=kc == 0 and v == 0, stop=kc == KD - 1 and v == 1)
                ins.then_inc(S["dt_mm"], 1)

            def turn_dt():
                e.wait_ge(S["dt_step"], 10)
                for n in range(4):
                    o = (256, 384, 1536, 1664)[n]
                    ins = e.transpose(ps[:, 5, n * 64:(n + 1) * 64], tx[0:64, o:o + P], ident[0:64, 0:64])
                ins.then_inc(S["dt_turned"], 1)

            def turn_group(b, k):
                e.wait_ge(S["conv_silu"], 2 * b + 2)
                e.wait_ge(S["xt_copied"], b)
                for fc in range(4):
                    for tt in range(2):
                        o = LO + k * 1024 + fc * 256 + tt * P
                        ins = e.transpose(ps[:, 4 + 2 * k + tt, fc * P:(fc + 1) * P], gatedf[:, o:o + P], ident)
                ins.then_inc(S["xt_turned"], 1)

            def x_block(b, k, i, u0, step):
                first = k == 0 and isinstance(i, int)
                after = S["x2_lo"] if first else None
                gemm(u0, 4, act, 2 * k, False, i, step, ends=False, after=after)
                if not first:
                    turn_group(b - 1, (k + 1) % 2)
                gemm(u0 + 4, 4, act, 2 * k, False, i, step, kc0=8, starts=False, after=after)

            def bc_block(b, k, i, u0, step):
                gemm(u0, 4, act, 2 * k, False, i, step, ends=False)
                if k == 0 and isinstance(i, int) and i == 0:
                    turn_group(7, 1)
                gemm(u0 + 4, 4, act, 2 * k, False, i, step, kc0=8, starts=False)
            segment("ssd_x", 4, 8, x_block)
            segment("ssd_bc", 4, 4, bc_block)
            e.wait_ge(S["rows_loaded"], 16 * 5)
            e.wait_ge(S["xt_copied"], 8)
            dt_product()

            def z_block(b, k, i, u0, step):
                gemm(u0, 8, act, 2 * k, True, i, step)
                if k == 0 and isinstance(i, int):
                    turn_dt()
            segment("ssd_z", 4, 8, z_block)

            ex = actf[:, 1024:4096]
            bst = tx[:, 1024:1280]
            xdt = actf[:, 7168:8192]
            U0 = 2 * FIRST["ssd_out"]
            e.wait_ge(act_freed, freed("ssd_z", 7))

            def out_tile(t, g):
                n = 4 * g - 4 + t
                e.wait_ge(dve_freed, freed("ssd_out", n - 2))
                bank = 2 * (t % 2)
                for m in range(2):
                    def body(c, slot, m=m):
                        kc = 2 * m + c
                        return tokens_out((bank, bank + 1), (tok(act, kc, 0), tok(act, kc, 1)), kc, slot, c, kc == 0, kc == 3)
                    if t == 0:
                        e.wait_ge(S["y_lo"], 4 * g - 2 + 2 * m)
                    if isinstance(g, int):
                        unit(U0 - 8 + 8 * g + 2 * t + m, 0, 0, body)
                    else:
                        unit(U0 - 8 + 2 * t + m, g, 8, body)

            def scan_turn(g):
                later = not isinstance(g, int)
                e.wait_ge(S["b_staged"], g + 1)
                e.wait_ge(S["cb_masked"], g)
                e.matmul(ps[:, 4, 0:256], bst[:, 0:P], side[:, ds(256 * g + 2048, 256)], start=True, stop=True)
                e.matmul(ps[:, 4, 256:384], bst[:, P:2 * P], side[:, ds(256 * g + 2048 + P, P)],
                         start=True, stop=True).then_inc(S["cb_ready"], 1)
                if later:
                    out_tile(0, g)
                    out_tile(1, g)
                e.wait_ge(S["xdt_step"], 2 * g + 1)
                e.wait_ge(S["y_lo"], 4 * g)
                for n in range(2):
                    e.wait_ge(S["m_ready"], 2 * g + n + 1)
                    for h in range(4 * n, 4 * n + 4):
                        cs = slice(h * HD, (h + 1) * HD)
                        m = ex[:, h * 384:(h + 1) * 384]
                        e.matmul(ps[:, 5, cs], m[:, 0:128], xdt[:, h * HD:(h + 1) * HD], start=True, stop=True)
                        e.matmul(ps[:, 6, cs], m[:, 128:256], xdt[:, h * HD:(h + 1) * HD], start=True, stop=False)
                        ins = e.matmul(ps[:, 6, cs], m[:, 256:384], xdt[:, 512 + h * HD:512 + (h + 1) * HD],
                                       start=False, stop=True)
                ins.then_inc(S["y_mm"], 1)
                if later:
                    out_tile(2, g)
                    out_tile(3, g)
                e.wait_ge(S["y_ready"], 2 * g + 2)
                for c in range(4):
                    for tt in range(2):
                        o = tt * 512 + c * P
                        ins = e.transpose(ps[:, 5 + c // 2, (c % 2) * 256 + tt * P:(c % 2) * 256 + (tt + 1) * P],
                                          tx[:, o:o + P], ident)
                    if c % 2 == 1:
                        ins.then_inc(S["y_turned"], 1)
            each(e, G, scan_turn)
            for t in range(4):
                out_tile(t, G)
            turn_x(S["ln_dve"], 15, 4, S["x3_lo"], S["x3_turned"])

            u0 = 2 * FIRST["lat_q"]
            pair_free(BI["lat_q"])
            gemm(u0, 8, act, 0, True, after=S["x3_lo"])
            pair_free(BI["lat_kv"])
            gemm(u0 + 8, 8, act, 2, True, w=336)
            g0 = 2 * FIRST["lat_gate0"]
            pair_free(BI["lat_gate0"])
            gemm(g0, 4, act, 0, False, ends=False)
            e.wait_ge(S["lat_normed"], 4)
            turn4(lambda c, tt: tx[:, tt * 512 + c * P:tt * 512 + (c + 1) * P], 0, 4)
            for c in range(2):
                for tt in range(2):
                    o = 1024 + tt * 336 + c * P
                    e.transpose(ps[:, 6, c * 256 + tt * P:c * 256 + (tt + 1) * P], tx[:, o:o + P], ident)
            e.wait_ge(S["lat_act"], 2)
            for tt in range(2):
                ins = e.transpose(ps[:, 7, tt * P:(tt + 1) * P], t1[:, tt * P:(tt + 1) * P], ident)
            ins.then_inc(S["lat_turned"], 1)
            gemm(g0 + 4, 4, act, 0, False, kc0=8, starts=False)
            pair_free(BI["lat_gate0"] + 1)
            gemm(g0 + 8, 8, act, 2, False)
            e.wait_ge(S["lat_lo"], 2)
            for b in range(2):
                pair_free(BI["idx_q"] + b)
                gemm(2 * FIRST["idx_q"] + 2 * b, 2, lat, 2 * b, False)
            e.wait_ge(S["idxk_ready"], 1)
            e.wait_ge(act_freed, freed("idx_q", 1))
            for h in range(16):
                r = slice(64 * (h % 2), 64 * (h % 2) + 64)
                qa = gatedf[r, (h // 2) * 256:(h // 2) * 256 + 256]
                if h >= 4:
                    e.wait_ge(S["idx_relu"], h - 3)
                bank = 4 + h % 4
                e.matmul(ps[:, bank, 0:128], qa[:, 0:P], gatedf[r, 2048:2176], start=True, stop=True)
                e.matmul(ps[:, bank, 128:384], qa[:, P:2 * P], gatedf[r, 2048:2304],
                         start=True, stop=True).then_inc(S["idx_scores"], 1)
            segment("lat_gate", 4, 6, from_act(False))

            e.wait_ge(act_freed, freed("lat_gate", 5))
            e.wait_ge(S["idx_relu"], 16)

            def heads_turn(t, k, u0, i, attend=True, project=True):
                w = actf[:, (1 - k) * 3072:(2 - k) * 3072]
                w_next = actf[:, k * 3072:(k + 1) * 3072]

                def scores(h, here=attend, of=t - 1, w=w):
                    if here:
                        n = 4 * of + h
                        if h == 0:
                            e.wait_ge(S["hk_read"], of + 1)
                        if not isinstance(n, int) or n > 1:
                            e.wait_ge(S["hs_masked"], n - 1)
                        e.matmul(ps[:, 4 + h % 2, 0:128], w[:, h * 256:h * 256 + P], w[:, 1024 + h * 256:1152 + h * 256],
                                 start=True, stop=True)
                        e.matmul(ps[:, 4 + h % 2, 128:384], w[:, h * 256 + P:h * 256 + 2 * P],
                                 w[:, 1024 + h * 256:1280 + h * 256], start=True, stop=True).then_inc(S["hs_mm"], 1)

                def turn(h):
                    if attend:
                        n = 4 * (t - 1) + h
                        p = actf[:, 6144 + (h % 2) * 384:6528 + (h % 2) * 384]
                        e.wait_ge(S["hs_probs"], n + 1)
                        e.wait_ge(S["hs_pt"], n)
                        for c in range(3):
                            ins = e.transpose(ps[:, 6, c * P:(c + 1) * P], p[:, c * P:(c + 1) * P], ident)
                        ins.then_inc(S["hs_turned"], 1)

                def mix(h):
                    if attend:
                        n = 4 * (t - 1) + h
                        pt = actf[:, 6912 + (h % 2) * 384:7296 + (h % 2) * 384]
                        e.wait_ge(S["hs_pt"], n + 1)
                        if h == 0:
                            e.wait_ge(S["hv_read"], t)
                        e.wait_ge(S["ho_gated"], n)
                        o = (h % 2) * 256
                        e.matmul(ps[:, 7, o:o + 256], w[:, 2048 + h * P:2048 + (h + 1) * P], pt[:, 0:256],
                                 start=True, stop=False, skip_group_check=True)
                        e.matmul(ps[:, 7, o + P:o + 256], w[:, 2560 + h * P:2560 + (h + 1) * P], pt[:, 256:384],
                                 start=False, stop=True, skip_group_check=True).then_inc(S["ho_mm"], 1)

                def product(m):
                    if not project:
                        gemm(u0 + m, 1, gated, 0, True, kc0=2 * m, starts=m == 0, ends=False)
                    elif m < 2:
                        if m == 0:
                            e.wait_ge(S["hv_read"], t)
                        gemm(u0 + m, 1, lat, 0, False, i, 8, kc0=2 * m, starts=m == 0, ends=m == 1)
                    elif m == 2:
                        e.wait_ge(S["hk_read"], t)
                        gemm(u0 + 2, 1, lat, 2, False, i, 8, kc0=4)
                    else:
                        e.wait_ge(S["hq_read"], t + 1)
                        gemm(u0 + 3, 1, lat, 0, True, i, 8, kc0=4)
                product(0)
                turn(0)
                scores(2)
                product(1)
                mix(0)
                turn(1)
                scores(3)
                product(2)
                mix(1)
                turn(2)
                product(3)
                mix(2)
                turn(3)
                scores(0, project, t, w_next)
                scores(1, project, t, w_next)
                mix(3)

            HEAD = 2 * FIRST["head_q"]
            heads_turn(0, 0, HEAD, 0, attend=False)
            heads_turn(1, 1, HEAD + 4, 0)
            with e.Fori(1, 4) as i:
                for k in range(2):
                    heads_turn(2 * i + k, k, HEAD + 4 * k, i)
            e.wait_ge(S["hv_read"], 8)
            e.wait_ge(S["hk_read"], 8)
            e.wait_ge(S["ho_lo"], 16)
            heads_turn(8, 0, HEAD + 32, 0, project=False)

            e.wait_ge(S["ho_lo"], 32)
            u0 = 2 * FIRST["lat_out"]
            gemm(u0 + 4, 12, gated, 0, True, kc0=8, starts=False)
            for b in range(1, 4):
                pair_free(BI["lat_out"] + b)
                gemm(u0 + 16 * b, 16, gated, 2 * (b % 2), True)


_INS = ["x", "c", "ctx", "c_ctx", "w_ada", "b_ada", "norm_g", "w_in", "q_norm_g", "k_norm_g", "w_proj_a", "w_proj_b",
        "w_out", "final_g", "ssd_w_in_2", "ssd_conv_w_2", "ssd_conv_b_2", "ssd_dt_bias_2", "ssd_a_log_2",
        "ssd_d_skip_2", "ssd_norm_g_2", "ssd_w_out_2", "dsa_w_in_2", "dsa_q_norm_g_2", "dsa_kv_norm_g_2",
        "dsa_w_uq_2", "dsa_w_uk_2", "dsa_w_uv_2", "dsa_w_idx_q_2", "dsa_w_out_2", "ln_g_2", "ln_b_2"]


def kernel(**inputs):
    import concourse.bacc as bacc
    from concourse.bass_utils import run_bass_kernel_spmd

    nc = bacc.Bacc("TRN2", target_bir_lowering=False, num_devices=1)
    arrays, views = {}, {}
    for name in _INS:
        v = np.ascontiguousarray(inputs[name])
        if name not in ("c_ctx", "final_g", "ln_g_2", "ln_b_2"):
            v = v.reshape(v.shape[1:])
        arrays[f"in_{name}"] = v
    arrays["in_tables"] = make_tables()
    for name, v in arrays.items():
        views[name[3:]] = nc.dram_tensor(name, v.shape, F32, kind="ExternalInput").ap()
    out = nc.dram_tensor("out_dram", (L, D), F32, kind="ExternalOutput").ap()
    acs = nc.dram_tensor("acs_dram", (64, L), F32, kind="Internal").ap()
    build(nc, views, out, acs)
    r = run_bass_kernel_spmd(nc, [arrays], core_ids=[0])
    return r.results[0]["out_dram"].reshape(1, L, D)
```
